# Optimizing a Trainium2 kernel written in Bass

```python
import jax, jax.numpy as jnp
from jax import lax
import numpy as np

D_MODEL = 1024
BATCH = 1
SEQ = 256
DEPTH = 2

MIX_WIDTH = D_MODEL // 2
N_BRANCH = 3
A_HEAD_DIM = 64
A_HEADS = MIX_WIDTH // A_HEAD_DIM
A_WIDTH = A_HEADS * A_HEAD_DIM
A_RANK_W = 64
A_RANK_A = 64
A_RANK_G = 128
A_GN_EPS = 64e-5
B_KEY_DIM = 128
B_VAL_DIM = 128
B_HEADS = MIX_WIDTH // B_VAL_DIM
B_WIDTH = B_HEADS * B_VAL_DIM
B_CHUNK = 64
C_HEAD_DIM = 64
C_HEADS = MIX_WIDTH // C_HEAD_DIM
C_KV_HEADS = 2
C_WIDTH = C_HEADS * C_HEAD_DIM
IDX_HEADS = 4
IDX_DIM = C_HEAD_DIM
TOPK_MAX = 256
Q_BLOCK = 128
ROPE_THETA = 10000.0
D_FF = 2816
CONV_WIDTH = 3
NORM_EPS = 1e-6

A_COLS = 3 * A_WIDTH + A_RANK_W + A_RANK_A + A_RANK_G
B_COLS = 4 * B_WIDTH
C_COLS = C_WIDTH + 2 * C_KV_HEADS * C_HEAD_DIM + IDX_HEADS * IDX_DIM + IDX_DIM + IDX_HEADS
GATE_COLS = N_BRANCH * D_MODEL
IN_COLS = A_COLS + B_COLS + C_COLS + GATE_COLS


F32 = jnp.float32

def _split(t, sizes):
    out, start = [], 0
    for s in sizes:
        out.append(t[..., start:start + s])
        start += s
    return out

def rms_norm(x, g):
    xf = x.astype(F32)
    y = xf * lax.rsqrt(jnp.mean(xf * xf, axis=-1, keepdims=True) + NORM_EPS)
    return (y * g.astype(F32)).astype(x.dtype)

def token_shift(p):
    return jnp.pad(p, ((0, 0), (1, 0), (0, 0)))[:, :-1]

def rope_tables(seq, dim):
    half = dim // 2
    inv_freq = ROPE_THETA ** (-jnp.arange(half, dtype=F32) * (2.0 / dim))
    ang = jnp.arange(seq, dtype=F32)[:, None] * inv_freq[None, :]
    return jnp.cos(ang), jnp.sin(ang)

def apply_rope(t, cos, sin):
    half = t.shape[-1] // 2
    tf = t.astype(F32)
    t1, t2 = tf[..., :half], tf[..., half:]
    c, s = cos[None, :, None, :], sin[None, :, None, :]
    return jnp.concatenate([t1 * c - t2 * s, t2 * c + t1 * s], axis=-1).astype(t.dtype)

def rwkv7_scan(r, w, k, v, a, b):
    bsz, _, heads, n = r.shape

    def step(state, inp):
        r_t, w_t, k_t, v_t, a_t, b_t = inp
        sa = jnp.einsum('bhij,bhj->bhi', state, a_t)
        state = (state * w_t[:, :, None, :] + sa[..., None] * b_t[:, :, None, :]
                 + v_t[..., None] * k_t[:, :, None, :])
        return state, jnp.einsum('bhij,bhj->bhi', state, r_t)

    xs = tuple(jnp.moveaxis(t, 1, 0) for t in (r, w, k, v, a, b))
    _, ys = lax.scan(step, jnp.zeros((bsz, heads, n, n), F32), xs)
    return jnp.moveaxis(ys, 0, 1)

def rwkv7_branch(p, mu, w0, w_up, a0, a_up, g_up, k_k, k_a, r_k, gn_g, gn_b):
    bsz, seq, _ = p.shape
    p = p + (token_shift(p) - p) * mu
    r, k, v, wd, ad, gd = _split(p, (A_WIDTH, A_WIDTH, A_WIDTH, A_RANK_W, A_RANK_A, A_RANK_G))
    w_log = -jax.nn.softplus(-(w0 + jnp.tanh(wd) @ w_up).astype(F32)) - 0.5
    decay = jnp.exp(-jnp.exp(w_log))
    a = jax.nn.sigmoid((a0 + ad @ a_up).astype(F32))
    g = jax.nn.sigmoid(gd) @ g_up

    def hd(t):
        return t.astype(F32).reshape(bsz, seq, A_HEADS, A_HEAD_DIM)

    kk = hd(k * k_k)
    kk = kk * lax.rsqrt(jnp.maximum(jnp.sum(kk * kk, axis=-1, keepdims=True), 1e-24))
    k_mod = hd(k.astype(F32) * (1.0 + (a - 1.0) * k_a.astype(F32)))
    r_h, v_h, a_h = hd(r), hd(v), hd(a)
    y = rwkv7_scan(r_h, hd(decay), k_mod, v_h, -kk, kk * a_h)
    mean = jnp.mean(y, axis=-1, keepdims=True)
    var = jnp.mean(jnp.square(y - mean), axis=-1, keepdims=True)
    y = ((y - mean) * lax.rsqrt(var + A_GN_EPS)).reshape(bsz, seq, A_WIDTH)
    y = y * gn_g.astype(F32) + gn_b.astype(F32)
    bonus = jnp.sum(r_h * k_mod * r_k.astype(F32), axis=-1, keepdims=True) * v_h
    y = y + bonus.reshape(bsz, seq, A_WIDTH)
    return (y * g.astype(F32)).astype(p.dtype)

def hgrn2_chunk_step(state, inp):
    q, k, g, v = inp
    b = jnp.cumsum(g, axis=2)
    causal = jnp.tril(jnp.ones((B_CHUNK, B_CHUNK), dtype=bool))
    diff = b[:, :, :, None, :] - b[:, :, None, :, :]
    decay = jnp.exp(jnp.where(causal[:, :, None], diff, -jnp.inf))
    scores = jnp.einsum('bhtd,bhsd,bhtsd->bhts', q, k, decay)
    o = (jnp.einsum('bhts,bhsv->bhtv', scores, v)
         + jnp.einsum('bhtd,bhdv->bhtv', q * jnp.exp(b), state))
    b_end = b[:, :, -1:, :]
    state = (state * jnp.exp(b_end)[:, :, 0, :, None]
             + jnp.einsum('bhsd,bhsv->bhdv', k * jnp.exp(b_end - b), v))
    return state, o

def hgrn2_branch(p, lb, gn_g):
    bsz, seq, _ = p.shape
    q, f, i, g = _split(p, (B_WIDTH, B_WIDTH, B_WIDTH, B_WIDTH))
    f = f.astype(F32)
    lb = lb.astype(F32)
    log_f = jnp.logaddexp(jnp.log(lb), jnp.log1p(-lb) + jax.nn.log_sigmoid(f))
    k_in = (1.0 - lb) * jax.nn.sigmoid(-f)
    n_chunk = seq // B_CHUNK

    def chunks(t, d):
        return t.astype(F32).reshape(bsz, n_chunk, B_CHUNK, B_HEADS, d).transpose(1, 0, 3, 2, 4)

    s0 = jnp.zeros((bsz, B_HEADS, B_KEY_DIM, B_VAL_DIM), F32)
    _, o = lax.scan(hgrn2_chunk_step, s0,
                    (chunks(q, B_KEY_DIM), chunks(k_in, B_KEY_DIM),
                     chunks(log_f, B_KEY_DIM), chunks(i, B_VAL_DIM)))
    o = o.transpose(1, 0, 3, 2, 4).reshape(bsz, seq, B_HEADS, B_VAL_DIM)
    o = o * lax.rsqrt(jnp.mean(o * o, axis=-1, keepdims=True) + NORM_EPS)
    o = o.reshape(bsz, seq, B_WIDTH) * gn_g.astype(F32) * jax.nn.silu(g.astype(F32))
    return o.astype(p.dtype)

def dsa_branch(p, cos, sin):
    bsz, seq, _ = p.shape
    kv_w = C_KV_HEADS * C_HEAD_DIM
    q, k, v, qi, ki, wi = _split(p, (C_WIDTH, kv_w, kv_w, IDX_HEADS * IDX_DIM, IDX_DIM, IDX_HEADS))
    q = apply_rope(q.reshape(bsz, seq, C_HEADS, C_HEAD_DIM), cos, sin)
    k = apply_rope(k.reshape(bsz, seq, C_KV_HEADS, C_HEAD_DIM), cos, sin)
    v = v.reshape(bsz, seq, C_KV_HEADS, C_HEAD_DIM)
    qi = apply_rope(qi.reshape(bsz, seq, IDX_HEADS, IDX_DIM), cos, sin)
    ki = apply_rope(ki[:, :, None, :], cos, sin)[:, :, 0, :].astype(F32)
    wi = wi.astype(F32) * (IDX_HEADS ** -0.5) * (IDX_DIM ** -0.5)
    n_blk = seq // Q_BLOCK
    k_sel = min(TOPK_MAX, seq // 4)
    group = C_HEADS // C_KV_HEADS
    s_pos = jnp.arange(seq)

    def blockify(t):
        return jnp.moveaxis(t.reshape(bsz, n_blk, Q_BLOCK, *t.shape[2:]), 1, 0)

    def attend(args):
        qb, qib, wib, t0 = args
        t_pos = t0 + jnp.arange(Q_BLOCK)
        causal = s_pos[None, :] <= t_pos[:, None]
        dots = jnp.einsum('bqhd,bsd->bqhs', qib.astype(F32), ki)
        score = jnp.einsum('bqhs,bqh->bqs', jax.nn.relu(dots), wib)
        score = jnp.where(causal[None], score, -jnp.inf)
        _, idx = lax.top_k(score, k_sel)
        kg = jax.vmap(lambda kb, ib: kb[ib])(k, idx)
        vg = jax.vmap(lambda vb, ib: vb[ib])(v, idx)
        valid = idx <= t_pos[None, :, None]
        qg = qb.reshape(bsz, Q_BLOCK, C_KV_HEADS, group, C_HEAD_DIM)
        logits = jnp.einsum('bqcgd,bqkcd->bqcgk', qg, kg).astype(F32) * (C_HEAD_DIM ** -0.5)
        logits = jnp.where(valid[:, :, None, None, :], logits, -jnp.inf)
        prob = jax.nn.softmax(logits, axis=-1).astype(vg.dtype)
        out = jnp.einsum('bqcgk,bqkcd->bqcgd', prob, vg)
        return out.reshape(bsz, Q_BLOCK, C_WIDTH)

    outs = lax.map(attend, (blockify(q), blockify(qi), blockify(wi),
                            jnp.arange(n_blk, dtype=jnp.int32) * Q_BLOCK))
    return jnp.moveaxis(outs, 0, 1).reshape(bsz, seq, C_WIDTH).astype(p.dtype)

def conv_glu(h, w_up, conv_w, conv_b, w_down):
    seq = h.shape[1]
    up = h @ w_up
    up_pad = jnp.pad(up, ((0, 0), (CONV_WIDTH - 1, 0), (0, 0)))
    c = conv_b
    for j in range(CONV_WIDTH):
        c = c + conv_w[j] * up_pad[:, j:j + seq]
    gate, val = _split(c, (D_FF, D_FF))
    return (jax.nn.silu(gate) * val) @ w_down

def first_inputs(seed: int = 0) -> dict:
    key = jax.random.key(seed)
    ks = iter(jax.random.split(key, 32))

    def nrm(shape, scale):
        return jax.random.normal(next(ks), shape, F32) * scale

    def uni(shape, lo, hi):
        return jax.random.uniform(next(ks), shape, F32, lo, hi)

    f2 = 2 * D_FF
    return {
        'x': nrm((BATCH, SEQ, D_MODEL), 1.0),
        'norm_mix_g': 1.0 + nrm((DEPTH, D_MODEL), 0.02),
        'w_in': nrm((DEPTH, D_MODEL, IN_COLS), D_MODEL ** -0.5),
        'a_mu': uni((DEPTH, A_COLS), 0.0, 1.0),
        'a_w0': uni((DEPTH, A_WIDTH), -5.0, 0.0),
        'a_w_up': nrm((DEPTH, A_RANK_W, A_WIDTH), 0.5 * A_RANK_W ** -0.5),
        'a_a0': nrm((DEPTH, A_WIDTH), 0.5),
        'a_a_up': nrm((DEPTH, A_RANK_A, A_WIDTH), 0.5 * A_RANK_A ** -0.5),
        'a_g_up': nrm((DEPTH, A_RANK_G, A_WIDTH), A_RANK_G ** -0.5),
        'a_k_k': 0.85 + nrm((DEPTH, A_WIDTH), 0.05),
        'a_k_a': 1.0 + nrm((DEPTH, A_WIDTH), 0.05),
        'a_r_k': nrm((DEPTH, A_HEADS, A_HEAD_DIM), 0.1),
        'a_gn_g': 1.0 + nrm((DEPTH, A_WIDTH), 0.02),
        'a_gn_b': nrm((DEPTH, A_WIDTH), 0.02),
        'b_lb_logits': nrm((DEPTH, B_HEADS * B_KEY_DIM), 1.0),
        'b_gn_g': 1.0 + nrm((DEPTH, B_WIDTH), 0.02),
        'w_branch': nrm((DEPTH, N_BRANCH, MIX_WIDTH, D_MODEL), MIX_WIDTH ** -0.5),
        'w_o': nrm((DEPTH, D_MODEL, D_MODEL), D_MODEL ** -0.5),
        'norm_ffn_g': 1.0 + nrm((DEPTH, D_MODEL), 0.02),
        'w_up': nrm((DEPTH, D_MODEL, f2), D_MODEL ** -0.5),
        'conv_w': nrm((DEPTH, CONV_WIDTH, f2), CONV_WIDTH ** -0.5),
        'conv_b': nrm((DEPTH, f2), 0.02),
        'w_down': nrm((DEPTH, D_FF, D_MODEL), D_FF ** -0.5),
        'norm_final_g': 1.0 + nrm((D_MODEL,), 0.02),
    }

def first_block(x, norm_mix_g, w_in, a_mu, a_w0, a_w_up, a_a0, a_a_up, a_g_up, a_k_k, a_k_a,
              a_r_k, a_gn_g, a_gn_b, b_lb_logits, b_gn_g, w_branch, w_o, norm_ffn_g,
              w_up, conv_w, conv_b, w_down, norm_final_g):
    bsz, seq, _ = x.shape
    cos, sin = rope_tables(seq, C_HEAD_DIM)
    lb_cum = jnp.cumsum(jax.nn.softmax(b_lb_logits.astype(F32), axis=0), axis=0)
    lower_bounds = lb_cum - lb_cum[0]
    h = x
    for layer in range(DEPTH):
        u = rms_norm(h, norm_mix_g[layer])
        p = u @ w_in[layer]
        p_a, p_b, p_c, p_gate = _split(p, (A_COLS, B_COLS, C_COLS, GATE_COLS))
        y_a = rwkv7_branch(p_a, a_mu[layer], a_w0[layer], a_w_up[layer], a_a0[layer],
                           a_a_up[layer], a_g_up[layer], a_k_k[layer], a_k_a[layer],
                           a_r_k[layer], a_gn_g[layer], a_gn_b[layer])
        y_b = hgrn2_branch(p_b, lower_bounds[layer], b_gn_g[layer])
        y_c = dsa_branch(p_c, cos, sin)
        ys = jnp.stack([y_a, y_b, y_c], axis=2)
        branch = jnp.einsum('bsnc,ncd->bsnd', ys, w_branch[layer])
        gates = jax.nn.sigmoid(p_gate.reshape(bsz, seq, N_BRANCH, D_MODEL))
        merged = jnp.sum(gates * branch, axis=2)
        h = h + merged @ w_o[layer]
        u = rms_norm(h, norm_ffn_g[layer])
        h = h + conv_glu(u, w_up[layer], conv_w[layer], conv_b[layer], w_down[layer])
    return rms_norm(h, norm_final_g)


CHUNK = 64
GLA_HEADS = 4
GLA_DK = 64
GLA_DV = 128
GLA_RANK = 16
GLA_TAU = 16.0
RET_HEADS = 4
RET_DK = 128
RET_DV = 128
ROPE_BASE = 10000.0
N_EXPERTS = 8
TOP_K = 2
D_FF_EXPERT = 1408
EPS = 1e-6
GLA_QK = GLA_HEADS * GLA_DK
GLA_V = GLA_HEADS * GLA_DV
RET_QK = RET_HEADS * RET_DK
RET_V = RET_HEADS * RET_DV
MIX_WIDTH_2 = GLA_V + RET_V
IN_SPLITS = (GLA_QK, GLA_QK, GLA_V, GLA_V, GLA_RANK, RET_QK, RET_QK, RET_V, RET_V)
IN_WIDTH = sum(IN_SPLITS)
N_DENSE = (DEPTH + 1) // 2
N_MOE = DEPTH // 2


F32_2 = jnp.float32

def rms_norm_2(x, g):
    x32 = x.astype(F32_2)
    y = x32 * lax.rsqrt(jnp.mean(x32 * x32, axis=-1, keepdims=True) + EPS)
    return (y * g.astype(F32_2)).astype(x.dtype)

def to_chunks(t, n_heads):
    return t.reshape(t.shape[0], t.shape[1] // CHUNK, CHUNK, n_heads, -1)

def chunk_scan(decay, update):
    def step(state, inp):
        a, u = inp
        return a[..., None] * state + u, state
    init = jnp.zeros_like(update[:, 0])
    _, prev = lax.scan(step, init, (jnp.moveaxis(decay, 1, 0), jnp.moveaxis(update, 1, 0)))
    return jnp.moveaxis(prev, 0, 1)

def gla_core(q, k, v, log_a):
    b = jnp.cumsum(log_a, axis=2)
    b_last = b[:, :, -1:]
    eb, enb = jnp.exp(b), jnp.exp(-b)
    q_f, k_f = q * eb, k * enb
    q_b, k_b = q * enb, k * eb
    t_idx = jnp.arange(CHUNK)
    causal = t_idx[:, None] >= t_idx[None, :]
    s_fwd = jnp.einsum('bnthk,bnshk->bnhts', q_f, k_f)
    s_bwd = jnp.einsum('bnthk,bnshk->bnhts', q_b, k_b)
    scores = jnp.where(causal, s_fwd, s_bwd)
    o_intra = jnp.einsum('bnhts,bnshv->bnthv', scores, v)
    upd = jnp.einsum('bnshk,bnshv->bnhkv', k * jnp.exp(b_last - b), v)
    s_prev = chunk_scan(jnp.exp(b_last[:, :, 0]), upd)
    o_inter = jnp.einsum('bnthk,bnhkv->bnthv', q_f, s_prev)
    return o_intra + o_inter

def retention_core(q, k, v, log_gamma):
    t = jnp.arange(CHUNK, dtype=F32_2)
    dist = jnp.abs(t[:, None] - t[None, :])
    d_intra = jnp.exp(log_gamma[:, None, None] * dist)
    scores = jnp.einsum('bnthk,bnshk->bnhts', q, k) * d_intra
    o_intra = jnp.einsum('bnhts,bnshv->bnthv', scores, v)
    k_dec = k * jnp.exp(log_gamma[None, :] * (CHUNK - 1 - t)[:, None])[None, None, :, :, None]
    upd = jnp.einsum('bnshk,bnshv->bnhkv', k_dec, v)
    decay = jnp.broadcast_to(jnp.exp(log_gamma * CHUNK)[None, None, :, None], upd.shape[:-1])
    r_prev = chunk_scan(decay, upd)
    q_dec = q * jnp.exp(log_gamma[None, :] * (t + 1)[:, None])[None, None, :, :, None]
    o_inter = jnp.einsum('bnthk,bnhkv->bnthv', q_dec, r_prev)
    return o_intra + o_inter

def rotary(x, positions):
    half = x.shape[-1] // 2
    inv_freq = ROPE_BASE ** (-jnp.arange(half, dtype=F32_2) / half)
    ang = positions.astype(F32_2)[..., None] * inv_freq
    cos, sin = jnp.cos(ang)[:, :, None, :], jnp.sin(ang)[:, :, None, :]
    x1, x2 = x[..., :half], x[..., half:]
    return jnp.concatenate([x1 * cos - x2 * sin, x1 * sin + x2 * cos], axis=-1)

def hybrid_mixer(h, positions, w_in, w_alpha, b_alpha, gla_g, gn_g, gn_b, w_out):
    bsz, seq, _ = h.shape
    proj = (h @ w_in).astype(F32_2)
    gq, gk, gv, gr, ga, rq, rk, rv, rg = jnp.split(proj, np.cumsum(IN_SPLITS)[:-1], axis=-1)
    log_a = jax.nn.log_sigmoid(ga @ w_alpha.astype(F32_2) + b_alpha.astype(F32_2)) / GLA_TAU
    o_g = gla_core(to_chunks(gq * GLA_DK ** -0.5, GLA_HEADS), to_chunks(gk, GLA_HEADS),
                   to_chunks(gv, GLA_HEADS), to_chunks(log_a, GLA_HEADS))
    o_g = o_g.reshape(bsz, seq, GLA_HEADS, GLA_DV)
    o_g = o_g * lax.rsqrt(jnp.mean(o_g * o_g, axis=-1, keepdims=True) + EPS)
    o_g = o_g.reshape(bsz, seq, GLA_V) * gla_g.astype(F32_2) * jax.nn.silu(gr)
    log_gamma = jnp.log(1.0 - 2.0 ** (-5.0 - jnp.arange(RET_HEADS, dtype=F32_2)))
    rq = rotary(rq.reshape(bsz, seq, RET_HEADS, RET_DK), positions) * RET_DK ** -0.5
    rk = rotary(rk.reshape(bsz, seq, RET_HEADS, RET_DK), positions)
    o_r = retention_core(to_chunks(rq, RET_HEADS), to_chunks(rk, RET_HEADS),
                         to_chunks(rv, RET_HEADS), log_gamma)
    o_r = o_r.reshape(bsz, seq, RET_HEADS, RET_DV)
    mu = jnp.mean(o_r, axis=-1, keepdims=True)
    var = jnp.mean(jnp.square(o_r - mu), axis=-1, keepdims=True)
    o_r = ((o_r - mu) * lax.rsqrt(var + EPS)).reshape(bsz, seq, RET_V)
    o_r = (o_r * gn_g.astype(F32_2) + gn_b.astype(F32_2)) * jax.nn.silu(rg)
    o = jnp.concatenate([o_g, o_r], axis=-1).astype(h.dtype)
    return o @ w_out

def swiglu(h, w1, w3, w2):
    return (jax.nn.silu(h @ w1) * (h @ w3)) @ w2

def moe_swiglu(h, router_w, w1, w3, w2):
    logits = (h @ router_w).astype(F32_2)
    top_v, top_i = lax.top_k(logits, TOP_K)
    probs = jax.nn.softmax(top_v, axis=-1)
    gates = jnp.sum(jax.nn.one_hot(top_i, N_EXPERTS, dtype=F32_2) * probs[..., None], axis=-2)
    gates = gates.astype(h.dtype)
    out = jnp.zeros_like(h)
    for e in range(N_EXPERTS):
        out = out + gates[..., e:e + 1] * swiglu(h, w1[e], w3[e], w2[e])
    return out

def second_inputs(seed: int = 0) -> dict:
    key = jax.random.key(seed)
    ks = jax.random.split(key, 24)
    nrm = lambda k, shape, scale: jax.random.normal(k, shape, F32_2) * scale
    D = D_MODEL
    offsets = jax.random.randint(ks[2], (BATCH, 1), 0, 4096, dtype=jnp.int32)
    return {
        'x': nrm(ks[0], (BATCH, SEQ, D), 1.0),
        'c': nrm(ks[1], (BATCH, D), 1.0),
        'positions': offsets + jnp.arange(SEQ, dtype=jnp.int32)[None, :],
        'ada_w': nrm(ks[3], (DEPTH, D, 6 * D), 0.5 * D ** -0.5),
        'ada_b': nrm(ks[4], (DEPTH, 6 * D), 0.02),
        'norm_mix_g': 1.0 + nrm(ks[5], (DEPTH, D), 0.02),
        'norm_ffn_g': 1.0 + nrm(ks[6], (DEPTH, D), 0.02),
        'w_in': nrm(ks[7], (DEPTH, D, IN_WIDTH), D ** -0.5),
        'gla_w_alpha': nrm(ks[8], (DEPTH, GLA_RANK, GLA_QK), GLA_RANK ** -0.5),
        'gla_b_alpha': nrm(ks[9], (DEPTH, GLA_QK), 0.1),
        'gla_norm_g': 1.0 + nrm(ks[10], (DEPTH, GLA_V), 0.02),
        'ret_gn_g': 1.0 + nrm(ks[11], (DEPTH, RET_V), 0.02),
        'ret_gn_b': nrm(ks[12], (DEPTH, RET_V), 0.02),
        'w_out': nrm(ks[13], (DEPTH, MIX_WIDTH_2, D), MIX_WIDTH_2 ** -0.5),
        'ffn_w1': nrm(ks[14], (N_DENSE, D, D_FF), D ** -0.5),
        'ffn_w3': nrm(ks[15], (N_DENSE, D, D_FF), D ** -0.5),
        'ffn_w2': nrm(ks[16], (N_DENSE, D_FF, D), D_FF ** -0.5),
        'router_w': nrm(ks[17], (N_MOE, D, N_EXPERTS), D ** -0.5),
        'moe_w1': nrm(ks[18], (N_MOE, N_EXPERTS, D, D_FF_EXPERT), D ** -0.5),
        'moe_w3': nrm(ks[19], (N_MOE, N_EXPERTS, D, D_FF_EXPERT), D ** -0.5),
        'moe_w2': nrm(ks[20], (N_MOE, N_EXPERTS, D_FF_EXPERT, D), D_FF_EXPERT ** -0.5),
        'final_g': 1.0 + nrm(ks[21], (D,), 0.02),
    }

def second_block(x, c, positions, ada_w, ada_b, norm_mix_g, norm_ffn_g, w_in, gla_w_alpha,
              gla_b_alpha, gla_norm_g, ret_gn_g, ret_gn_b, w_out, ffn_w1, ffn_w3, ffn_w2,
              router_w, moe_w1, moe_w3, moe_w2, final_g):
    cond = jax.nn.silu(c)
    for layer in range(DEPTH):
        mod = (cond @ ada_w[layer] + ada_b[layer])[:, None, :]
        sh1, sc1, g1, sh2, sc2, g2 = jnp.split(mod, 6, axis=-1)
        h = rms_norm_2(x, norm_mix_g[layer]) * (1.0 + sc1) + sh1
        x = x + g1 * hybrid_mixer(h, positions, w_in[layer], gla_w_alpha[layer],
                                  gla_b_alpha[layer], gla_norm_g[layer], ret_gn_g[layer],
                                  ret_gn_b[layer], w_out[layer])
        h = rms_norm_2(x, norm_ffn_g[layer]) * (1.0 + sc2) + sh2
        i = layer // 2
        if layer % 2 == 0:
            y = swiglu(h, ffn_w1[i], ffn_w3[i], ffn_w2[i])
        else:
            y = moe_swiglu(h, router_w[i], moe_w1[i], moe_w3[i], moe_w2[i])
        x = x + g2 * y
    return rms_norm_2(x, final_g)


def setup_inputs(seed=0):
    out = dict(first_inputs(seed))
    for name, value in second_inputs(seed + 1).items():
        if name != "x":
            out[name + "_2"] = value
    return out


def reference(
    x, norm_mix_g, w_in, a_mu, a_w0, a_w_up, a_a0, a_a_up, a_g_up, a_k_k, a_k_a, a_r_k, a_gn_g,
    a_gn_b, b_lb_logits, b_gn_g, w_branch, w_o, norm_ffn_g, w_up, conv_w, conv_b, w_down,
    norm_final_g, c_2, positions_2, ada_w_2, ada_b_2, norm_mix_g_2, norm_ffn_g_2, w_in_2,
    gla_w_alpha_2, gla_b_alpha_2, gla_norm_g_2, ret_gn_g_2, ret_gn_b_2, w_out_2, ffn_w1_2,
    ffn_w3_2, ffn_w2_2, router_w_2, moe_w1_2, moe_w3_2, moe_w2_2, final_g_2,
):
    x = first_block(
        x, norm_mix_g, w_in, a_mu, a_w0, a_w_up, a_a0, a_a_up, a_g_up, a_k_k, a_k_a, a_r_k,
        a_gn_g, a_gn_b, b_lb_logits, b_gn_g, w_branch, w_o, norm_ffn_g, w_up, conv_w, conv_b,
        w_down, norm_final_g,
    )
    return second_block(
        x, c_2, positions_2, ada_w_2, ada_b_2, norm_mix_g_2, norm_ffn_g_2, w_in_2,
        gla_w_alpha_2, gla_b_alpha_2, gla_norm_g_2, ret_gn_g_2, ret_gn_b_2, w_out_2, ffn_w1_2,
        ffn_w3_2, ffn_w2_2, router_w_2, moe_w1_2, moe_w3_2, moe_w2_2, final_g_2,
    )


_drawn_inputs = setup_inputs


def setup_inputs(seed=0):
    import zlib

    import numpy as np

    out = dict(_drawn_inputs(seed))
    spreads = {}
    factors = {'a_gn_g': 3.555,
     'a_gn_b': 3.055,
     'b_gn_g': 2.796,
     'norm_mix_g_2': 3.1,
     'gla_b_alpha_2': 3.813,
     'gla_norm_g_2': 13.887,
     'ret_gn_g_2': 6.496,
     'ret_gn_b_2': 5.773,
     'final_g_2': 7.938,
     'norm_ffn_g_2': 8.0}
    for name, (base, spread) in spreads.items():
        noise = np.random.default_rng([zlib.crc32(name.encode()), seed]).standard_normal(out[name].shape)
        drawn = base * np.exp(spread * noise) if base else spread * noise
        out[name] = __import__('jax').numpy.asarray(drawn.astype(out[name].dtype))
    for name, factor in factors.items():
        out[name] = (out[name] * factor).astype(out[name].dtype)
    return out
```

```python
import numpy as np

P = 128
T = 256
D = 1024
KT = D // P
LAYERS = 2
CH = 64
NCH = T // CH
HALVES = T // P
FF, FFE, EXPERTS = 2816, 1408, 8
UNIT = KT * P
GROUP = 3
EXTRA = 8
SLOT = GROUP * UNIT + EXTRA
RING = 5
MIX1_GROUPS = 28
MIX2_GROUPS = 12
ADA_GROUPS = 16
FF_GROUPS = FF // P
MOE_GROUPS = EXPERTS * FFE // P
LAYER1_GROUPS = MIX1_GROUPS + FF_GROUPS
ALL_GROUPS = LAYERS * LAYER1_GROUPS + LAYERS * (ADA_GROUPS + MIX2_GROUPS) + FF_GROUPS + MOE_GROUPS
TOPK = 64

PAR1 = {}
PAR2 = {}
CONST = {}


def _columns(table, sizes):
    at = 0
    for name, n in sizes:
        table[name] = slice(at, at + n)
        at += n
    return at


PAR1_COLS = _columns(PAR1, [
    ("norm_mix", 8), ("mu", 14), ("w0", 4), ("a0", 4), ("k_k", 4), ("k_a", 4), ("r_k", 4),
    ("gn_g", 4), ("gn_b", 4), ("b_gn_g", 4), ("norm_ffn", 8), ("lb_logits", 8), ("lb_flag", 1),
    ("w_idx", 32)])
PAR2_COLS = _columns(PAR2, [
    ("norm_mix", 8), ("norm_ffn", 8), ("ada_b", 48), ("b_alpha", 2), ("gla_g", 4),
    ("ret_g", 4), ("ret_b", 4), ("w_ga", 128), ("w_alpha", 256)])
CONST_COLS = _columns(CONST, [
    ("ident", 128), ("strict_up_neg", 128), ("strict_up", 128), ("incl_up", 128),
    ("strict_low", 128), ("low16_neg", 128), ("up16_neg", 128), ("low32_neg", 128),
    ("low64_neg", 128), ("pair_blocks", 128), ("pair_mean", 128), ("mean128", 128),
    ("ones", 128), ("level0", 128), ("level1", 128), ("level2", 128), ("level3", 128),
    ("level4", 128), ("level5", 128), ("level6", 128), ("swap32", 128), ("swap64", 128),
    ("dup0", 128), ("dup1", 128), ("rope_cos", T), ("rope_sin", T), ("chunk_mask", T),
    ("noncausal", 2 * T), ("ret_intra", 4 * P), ("ret_q", 4 * CH), ("ret_k", 4 * CH),
    ("ret_chunk", 4), ("inv_freq", 1), ("sin_sign", 1)])


def constants():
    c = np.zeros((P, CONST_COLS), np.float32)
    r, q = np.arange(P)[:, None], np.arange(P)[None, :]
    same = (r // CH) == (q // CH)
    put = lambda name, a: c.__setitem__((slice(None), CONST[name]), a)
    put("ident", r == q)
    put("strict_up", same & (r < q))
    put("strict_up_neg", -1.0 * (same & (r < q)))
    put("incl_up", same & (r <= q))
    put("strict_low", same & (r > q))
    put("low16_neg", -1.0 * ((r // 16 == q // 16) & (r > q)))
    put("up16_neg", -1.0 * ((r // 16 == q // 16) & (r < q)))
    put("low32_neg", -1.0 * ((r // 32 == q // 32) & (r // 16 > q // 16)))
    put("low64_neg", -1.0 * ((r // 64 == q // 64) & (r // 32 > q // 32)))
    put("pair_blocks", same)
    put("pair_mean", same / float(CH))
    put("mean128", 1.0 / P)
    put("ones", 1.0)
    for n in range(6):
        h = 32 >> n
        put(f"level{n}", (r // (2 * h) == q // (2 * h)) & (r % (2 * h) < h) & (q % (2 * h) >= h))
    put("level6", r == q)
    put("swap32", (r // 64 == q // 64) & ((r % 64 + 32) % 64 == q % 64))
    put("swap64", (r + 64) % 128 == q)
    put("dup0", r == q % 64)
    put("dup1", r == 64 + q % 64)
    inv = np.float32(10000.0) ** (-np.arange(32, dtype=np.float32) * np.float32(2.0 / 64))
    ang = (np.arange(T, dtype=np.float32)[None, :] * inv.astype(np.float32)[:, None]).astype(np.float32)
    rows = np.arange(P) % 32
    put("rope_cos", np.cos(ang.astype(np.float64))[rows])
    put("rope_sin", np.sin(ang.astype(np.float64))[rows] * np.where(np.arange(P) % 64 < 32, -1, 1)[:, None])
    put("chunk_mask", (np.arange(T) % CH != 0)[None, :])
    s = np.arange(T)[None, :]
    put("noncausal", np.concatenate([np.where(s <= r + P * a, 0.0, -1e30) for a in range(2)], 1))
    lg = np.log(1.0 - 2.0 ** (-5.0 - np.arange(4)))
    put("ret_intra", np.concatenate([np.where(same, np.exp(g * np.abs(r - q)), 0.0) for g in lg], 1))
    t = np.arange(CH)
    put("ret_q", np.concatenate([np.exp(g * (t + 1)) for g in lg])[None, :] * 128 ** -0.5)
    put("ret_k", np.concatenate([np.exp(g * (CH - 1 - t)) for g in lg])[None, :])
    put("ret_chunk", np.exp(lg * CH)[None, :])
    inv = np.float32(10000.0) ** (-np.arange(64, dtype=np.float32) / np.float32(64))
    put("inv_freq", inv[np.arange(P) % 64][:, None])
    put("sin_sign", np.where(np.arange(P) < 64, -1.0, 1.0)[:, None])
    return c


def build(nc, a_x, a_pos, a_cond, a_const, a_par1, a_par2, a_router, a_norms, a_weights, a_out, probe=None):
    import concourse.bass as bass
    from concourse import mybir
    from contextlib import ExitStack

    f32, i32, u32 = mybir.dt.float32, mybir.dt.int32, mybir.dt.uint32
    ALU, ACTF, AX = mybir.AluOpType, mybir.ActivationFunctionType, mybir.AxisListType
    MUL, ADD, SUB, MAX = ALU.mult, ALU.add, ALU.subtract, ALU.max
    Exp, Ln, Sigmoid, Tanh, Sqrt, Sin, Copy, Ident, Square, Abs = (
        ACTF.Exp, ACTF.Ln, ACTF.Sigmoid, ACTF.Tanh, ACTF.Sqrt, ACTF.Sin, ACTF.Copy,
        ACTF.Identity, ACTF.Square, ACTF.Abs)
    es = ExitStack()

    class Queue:

        def __init__(self, engine, name, chained):
            self.engine, self.sem, self.count, self.chained = engine, sem(name), 0, chained
            self.passed = {}

        def wait(self, *tokens):
            for s, v in tokens:
                if isinstance(v, int):
                    if self.passed.get(id(s), 0) >= v:
                        continue
                    self.passed[id(s)] = v
                self.engine.wait_ge(s, v)

        def now(self):
            return (self.sem, self.count)

        def __call__(self, op, *args, after=(), signal=True, **kw):
            self.wait(*[x for x in after if x is not None])
            if self.chained and self.count:
                self.wait(self.now())
            ins = issue(self.engine, op)(*args, **kw)
            if signal:
                self.count += 1
                ins.then_inc(self.sem, 1)
            return self.now()

    def issue(engine, op):
        return {
            "tt": lambda *a, **k: engine.tensor_tensor(*a, **k),
            "ts": lambda *a, **k: engine.tensor_scalar(*a, **k),
            "stt": lambda *a, **k: engine.scalar_tensor_tensor(*a, **k),
            "scan": lambda *a, **k: engine.tensor_tensor_scan(*a, **k),
            "copy": lambda *a, **k: engine.tensor_copy(*a, **k),
            "recip": lambda *a, **k: engine.reciprocal(*a, **k),
            "memset": lambda *a, **k: engine.memset(*a, **k),
            "rmax": lambda *a, **k: engine.reduce_max(*a, **k),
            "max8": lambda *a, **k: engine.max(*a, **k),
            "maxidx": lambda *a, **k: engine.max_index(*a, **k),
            "replace": lambda *a, **k: engine.match_replace(*a, **k),
            "act": lambda *a, **k: engine.activation(*a, **k),
            "mm": lambda *a, **k: engine.matmul(*a, **k),
            "tr": lambda *a, **k: engine.transpose(*a, **k),
        }[op]

    def sem(name):
        return es.enter_context(nc.semaphore(name))

    def sb(name, cols, dt=f32):
        return es.enter_context(nc.sbuf_tensor(name, [P, cols], dt))

    ring = sb("ring", RING * SLOT)
    const = sb("const", CONST_COLS)
    par1 = sb("par1", PAR1_COLS)
    par2 = sb("par2", PAR2_COLS)
    norms = sb("norms", KT)
    final2 = sb("final2", KT)
    rope = sb("rope", 2 * T)[:, :]
    mod = sb("mod", 48)[:, :]
    cond = sb("cond", KT)[:, :]
    router = sb("router", KT * EXPERTS)
    x_sb = sb("x_res", KT * T)
    u_sb = sb("u_norm", KT * T)
    rstd = sb("rstd", T)
    small = sb("small", 512)
    y_sb = sb("y_mix", 12 * T)
    arena_cols = (nc.sbuf_bytes_remaining() if callable(nc.sbuf_bytes_remaining) else nc.sbuf_bytes_remaining) // 4 - 64
    arena = sb("arena", arena_cols)
    psum = [es.enter_context(nc.psum_tensor(f"bank{b}", [P, 512], f32)) for b in range(8)]

    X = x_sb[:, :].rearrange("p (k t) -> p k t", t=T)
    U = u_sb[:, :].rearrange("p (k t) -> p k t", t=T)
    Y = y_sb[:, :].rearrange("p (k t) -> p k t", t=T)

    def c_(name):
        return const[:, CONST[name]]

    def p1(name, j=None):
        s = PAR1[name]
        return par1[:, s] if j is None else par1[:, s.start + j:s.start + j + 1]

    def p2(name, j=None):
        s = PAR2[name]
        return par2[:, s] if j is None else par2[:, s.start + j:s.start + j + 1]

    class Space:

        def __init__(self, start=0):
            self.at = start

        def __call__(self, cols):
            self.at += cols
            assert self.at <= arena_cols, (self.at, arena_cols)
            return arena[:, self.at - cols:self.at]

    PE = Queue(nc.tensor, "s_pe", False)
    V = Queue(nc.vector, "s_dve", True)
    A = Queue(nc.scalar, "s_act", True)
    work = [PE, V, A]
    s_slot = [sem(f"s_slot{k}") for k in range(RING)]
    s_done = sem("s_group_done")
    s_in = sem("s_inputs")
    s_par = sem("s_params")
    s_out = sem("s_out")
    s_up = sem("s_ff_up")
    ff_sems = {True: (sem("s_ffc_act"), sem("s_ffc_dve")), False: (sem("s_ff_act"), sem("s_ff_dve"))}

    free = [()] * 8
    last_done = [None]

    def join():
        marks = [m for m in last_done if m] + [q.now() for q in work if q.count]
        for q in work:
            q.wait(*[m for m in marks])
        for b in range(8):
            free[b] = ()

    def restart():
        join()
        A("act", small[:, 0:1], small[:, 0:1], Copy)
        join_engines = [q.engine.engine for q in work]
        nc.multi_engine_barrier(join_engines)
        for q in work:
            q.engine.sem_clear(q.sem)
        nc.multi_engine_barrier(join_engines)
        for q in work:
            q.count, q.passed = 0, {}
        for b in range(8):
            free[b] = ()

    def weight_stream():
        def load(g, slot):
            nc.sync.dma_start(ring[:, slot * SLOT:(slot + 1) * SLOT],
                              a_weights[bass.ds(g, 1), :, :].rearrange("o p n -> p (o n)"))\
                .then_inc(s_slot[slot], 16)
        for g in range(RING):
            load(g, g)
        with nc.sync.Fori(0, (ALL_GROUPS - RING) // RING) as i:
            for j in range(RING):
                nc.sync.wait_ge(s_done, i * RING + (j + 1))
                load(i * RING + (RING + j), j)
        for g in range(ALL_GROUPS - (ALL_GROUPS - RING) % RING, ALL_GROUPS):
            nc.sync.wait_ge(s_done, g - RING + 1)
            load(g, g % RING)

    class Stream:

        def __init__(self, group0, layer=None):
            self.group0, self.layer, self.unit = group0, layer, 0

        def scaled(self, per_layer, n):
            return n if self.layer is None else self.layer * per_layer + n

        def arrived(self, g):
            n = (self.group0 + g) // RING + 1
            slot = (self.group0 + g) % RING
            return (s_slot[slot], self.scaled(16 * (LAYER1_GROUPS // RING), 16 * n))

        def weights(self, u):
            g = u // GROUP
            at = ((self.group0 + g) % RING) * SLOT + (u % GROUP) * UNIT
            return ring[:, at:at + UNIT]

        def extra(self, g):
            at = ((self.group0 + g) % RING) * SLOT + GROUP * UNIT
            return ring[:, at:at + EXTRA]

        def done(self, g):
            return (s_done, self.scaled(LAYER1_GROUPS, self.group0 + g + 1))

    ready = {}

    def need(st, u):
        g = u // GROUP
        if ready.get(id(st)) != g:
            PE.wait(st.arrived(g))
            ready[id(st)] = g

    def mm(out, lhsT, rhs, start, stop, after=(), signal=False, loose=False):
        return PE("mm", out, lhsT, rhs, start=start, stop=stop, after=after, signal=signal,
                  skip_group_check=loose)

    def last_mm(st, u, out, lhsT, rhs, start, stop, loose=False):
        if u % GROUP == GROUP - 1:
            nc.tensor.matmul(out, lhsT, rhs, start=start, stop=stop, skip_group_check=loose)\
                .then_inc(s_done, 1)
            last_done[0] = st.done(u // GROUP)
            return last_done[0]
        return mm(out, lhsT, rhs, start, stop, signal=True, loose=loose)

    def project(st, u, bank, half):
        need(st, u)
        w = st.weights(u).rearrange("p (k c) -> p k c", c=P)
        out = psum[bank][:, half * T:(half + 1) * T]
        for k in range(KT - 1):
            mm(out, w[:, k, :], U[:, k, :], k == 0, False)
        return last_mm(st, u, out, w[:, KT - 1, :], U[:, KT - 1, :], False, True)

    def project_tokens(st, u, bank, col):
        need(st, u)
        w = st.weights(u).rearrange("p (k c) -> p k c", c=P)
        for a in range(HALVES):
            out = psum[bank][:, col + a * P:col + (a + 1) * P]
            for k in range(KT):
                args = (out, U[:, k, a * P:(a + 1) * P], w[:, k, :], k == 0, k == KT - 1)
                if a == HALVES - 1 and k == KT - 1:
                    return last_mm(st, u, *args)
                mm(*args)

    turn = [0]

    def copy_out(out, src, after):
        turn[0] += 1
        if turn[0] % 2:
            return A("act", out, src, Copy, after=after)
        return V("copy", out, src, after=after)

    def rms(src, eps, g_of, add_of=None):
        sq = arena[:, 0:KT * T].rearrange("p (k t) -> p k t", t=T)
        t0 = A("act", sq[:, 0:4, :], src[:, 0:4, :], Square, after=(V.now(),))
        t1 = A("act", sq[:, 4:8, :], src[:, 4:8, :], Square)
        for k in range(KT):
            tok = mm(psum[0][:, 0:T], c_("ones"), sq[:, k, :], k == 0, k == KT - 1,
                     after=(t0 if k < 4 else t1,), signal=k == KT - 1)
        t = V("ts", rstd[:, :], psum[0][:, 0:T], 1.0 / D, eps, MUL, ADD, after=(tok,))
        t = A("act", rstd[:, :], rstd[:, :], Sqrt, after=(t,))
        V("recip", rstd[:, :], rstd[:, :], after=(t,))
        for k in range(KT):
            t = V("stt", U[:, k, :], src[:, k, :], g_of(k), rstd[:, :], MUL, MUL)
            if add_of is not None:
                t = A("act", U[:, k, :], U[:, k, :], Ident, bias=add_of(k), after=(t,))
        PE.wait(t, V.now(), A.now())

    def bc(ap, shape):
        return ap.to_broadcast(shape)

    def branch_a(PA, lora, lora_done):
        S = Space(14 * T)
        t4 = lambda ap: ap.rearrange("p (k t) -> p k t", t=T)
        Dif = t4(S(14 * T))
        V("tt", Dif[:, :, 1:T], PA[:, :, 0:T - 1], PA[:, :, 1:T], SUB)
        V("ts", Dif[:, :, 0:1], PA[:, :, 0:1], -1.0, None, MUL)
        for k in range(14):
            V("stt", PA[:, k, :], Dif[:, k, :], p1("mu", k), PA[:, k, :], MUL, ADD)
        mixed = V.now()
        S = Space(14 * T)
        R, K, VT, WA, GD = PA[:, 0:4, :], PA[:, 4:8, :], PA[:, 8:12, :], PA[:, 12, :], PA[:, 13, :]
        g_t, a_t, lw = t4(S(4 * T)), t4(S(4 * T)), t4(S(4 * T))
        kk, cw = t4(S(4 * T)), t4(S(4 * T))
        tmp = t4(Space(S.at)(4 * T))
        A("act", WA[0:64, :], WA[0:64, :], Tanh, after=(mixed,))
        low = A("act", GD[:, :], GD[:, :], Sigmoid)
        w_up = lora[0:64, 0:512]
        a_up = lora[64:128, 0:512]
        g_up = lora[:, 512:1024]
        for m in range(4):
            b = m // 2
            o = slice((m % 2) * T, (m % 2 + 1) * T)
            cs = slice(m * P, (m + 1) * P)
            mm(psum[b][:, o], w_up[:, cs], WA[0:64, :], True, True, after=(low,))
            mm(psum[2 + b][:, o], a_up[:, cs], WA[64:128, :], True, True)
            if m < 3:
                mm(psum[4 + b][:, o], g_up[:, cs], GD, True, True)
            else:
                nc.tensor.matmul(psum[4 + b][:, o], g_up[:, cs], GD, start=True, stop=True)\
                    .then_inc(s_done, 1)
                up = last_done[0] = lora_done
        for m in range(4):
            o = slice((m % 2) * T, (m % 2 + 1) * T)
            A("act", lw[:, m, :], psum[m // 2][:, o], Sigmoid, bias=p1("w0", m), after=(up,))
            A("act", a_t[:, m, :], psum[2 + m // 2][:, o], Sigmoid, bias=p1("a0", m))
            if m % 2:
                A("act", g_t[:, m - 1:m + 1, :].rearrange("p k t -> p (k t)"), psum[4 + m // 2][:, :], Copy)
        sig = A.now()
        V("ts", lw, lw, -float(np.exp(-0.5)), None, MUL, after=(sig,))
        for m in range(4):
            V("scan", cw[:, m, :], c_("chunk_mask"), lw[:, m, :], 0.0, MUL, ADD)
        for m in range(4):
            V("ts", kk[:, m, :], K[:, m, :], p1("k_k", m), None, MUL)
        t = V("tt", tmp, kk, kk, MUL)
        for m in range(4):
            tok = mm(psum[6 + m // 2][:, (m % 2) * T:(m % 2 + 1) * T], c_("pair_blocks"), tmp[:, m, :],
                     True, True, after=(t,), signal=True)
        for b in range(2):
            V("ts", tmp[:, 2 * b:2 * b + 2, :].rearrange("p k t -> p (k t)"), psum[6 + b][:, :],
              1e-24, None, MAX, after=(tok,))
        t = A("act", tmp, tmp, Sqrt, after=(V.now(),))
        V("recip", tmp, tmp, after=(t,))
        V("tt", kk, kk, tmp, MUL)
        omka = small[:, 0:4]
        V("ts", omka, p1("k_a"), -1.0, 1.0, MUL, ADD)
        for m in range(4):
            V("ts", tmp[:, m, :], a_t[:, m, :], p1("k_a", m), omka[:, m:m + 1], MUL, ADD)
        V("tt", K, K, tmp, MUL)
        for m in range(4):
            V("stt", tmp[:, m, :], R[:, m, :], p1("r_k", m), K[:, m, :], MUL, MUL)
        t = V.now()
        for m in range(4):
            tok = mm(psum[m // 2][:, (m % 2) * T:(m % 2 + 1) * T], c_("pair_blocks"), tmp[:, m, :],
                     True, True, after=(t, sig), signal=True)
        e = A("act", tmp, cw, Exp, scale=-1.0, after=(tok, V.now()))
        V("tt", a_t, a_t, kk, MUL)
        V("tt", a_t, a_t, tmp, MUL, after=(e,))
        V("tt", K, K, tmp, MUL)
        t = V("tt", lw, cw, lw, SUB)
        e = A("act", lw, lw, Exp, after=(t,))
        V("tt", kk, kk, lw, MUL, after=(e,))
        e = A("act", cw, cw, Exp, after=(V.now(),))
        V("tt", R, R, cw, MUL, after=(e,))
        bonus = lw
        for b in range(2):
            V("tt", bonus[:, 2 * b:2 * b + 2, :], psum[b][:, :].rearrange("p (k t) -> p k t", t=T),
              VT[:, 2 * b:2 * b + 2, :], MUL)
        at, bt, kt, rt, Dc = kk, a_t, K, R, cw
        join()
        S2 = S
        tokm = []
        for n, src in enumerate((bt, kt, VT)):
            dst = S2(2 * 512).rearrange("p (a c) -> p a c", a=2)
            for a in range(2):
                b = 2 * n + a
                for m in range(4):
                    tok = PE("tr", psum[b][:, m * P:(m + 1) * P], src[:, m, a * P:(a + 1) * P],
                             c_("ident"), signal=m == 3)
                free[b] = (copy_out(dst[:, a, :], psum[b][:, :], (tok,)),)
            tokm.append(dst)
        BT, KTk, VTk = tokm
        join()
        h8 = lambda ap: ap.rearrange("p (h c) -> p h c", c=P)
        TT = [h8(S2(1024)) for _ in range(2)]
        RB = [h8(S2(1024)) for _ in range(2)]
        keep = S2.at
        RK = h8(S2(1024))
        AK = h8(Y[:, 4:8, :].rearrange("p k t -> p (k t)"))
        AKV = [Y[:, 8 + 2 * a:10 + 2 * a, :].rearrange("p k t -> p (k t)") for a in range(2)]
        names = ("N16", "NT16", "M32", "M64", "N2", "N2T", "Pm")
        spare = {n: PA[:, 8 + 2 * j:10 + 2 * j, :].rearrange("p k t -> p (k t)")
                 for j, n in enumerate(("M32", "M64", "Pm"))}
        tmps = [{n: (spare[n] if par and n in spare else S2(512)).rearrange("p (h c) -> p h c", c=P)
                 for n in names} for par in range(2)]
        for w in tmps:
            w["N4"], w["N4T"], w["N8"] = w["N16"], w["NT16"], w["N2T"]
            w["Tm"], w["Z"] = w["N16"], w["NT16"]

        def gram(bank, lt, rt_, par, a, after=()):
            rows = slice(64 * par, 64 * par + 64)
            cs = slice(a * P, (a + 1) * P)
            for m in range(4):
                tok = mm(psum[bank][:, m * P:(m + 1) * P], lt[rows, m, cs], rt_[rows, m, cs], True, True,
                         after=tuple(after) + tuple(free[bank]), signal=m == 3)
            return tok

        def b4(name):
            return c_(name).rearrange("p (o c) -> p o c", o=1).to_broadcast([P, 4, P])

        def ps4(bank):
            return psum[bank][:, :].rearrange("p (h c) -> p h c", c=P)

        for a in range(2):
            bank = 0
            for par in range(2):
                for lt, r_, outs in (
                        (at, bt, (("N16", "low16_neg"), ("M32", "low32_neg"), ("M64", "low64_neg"))),
                        (bt, at, (("NT16", "up16_neg"),)),
                        (kt, at, ((AK, "strict_up"),)),
                        (bt, rt, ((RB[a], "incl_up"),)),
                        (kt, rt, ((RK, "incl_up"),))):
                    tok = gram(bank, lt, r_, par, a)
                    for dst, mask in outs:
                        o = tmps[par][dst] if isinstance(dst, str) else dst[:, par:8:2, :]
                        t = V("tt", o, ps4(bank), b4(mask), MUL, after=(tok,))
                    free[bank] = (t,)
                    bank = (bank + 1) % 8

            def four(bank, lt, r_, after):
                for m in range(4):
                    tok = mm(psum[bank][:, m * P:(m + 1) * P], lt[:, m, :], r_[:, m, :], True, True,
                             after=tuple(after) + tuple(free[bank]), signal=m == 3)
                return tok

            def product(par, slot, lt, r_, out, add=None, after=()):
                w = tmps[par]
                bank = 4 * par + slot
                tok = four(bank, w[lt], w[r_], tuple(after) or (V.now(), A.now()))
                o = w[out] if isinstance(out, str) else out
                if add is None:
                    t = A("act", o, ps4(bank), Copy, after=(tok,))
                else:
                    t = V("tt", o, ps4(bank), w[add], ADD, after=(tok,))
                free[bank] = (t,)
                return t

            def turned(par, slot, src, out):
                w = tmps[par]
                bank = 4 * par + slot
                for m in range(4):
                    tok = PE("tr", psum[bank][:, m * P:(m + 1) * P], w[src][:, m, :], c_("ident"),
                             after=(V.now(), A.now()) + tuple(free[bank]), signal=m == 3)
                free[bank] = (A("act", w[out], ps4(bank), Copy, after=(tok,)),)

            for par in range(2):
                V("tt", tmps[par]["Pm"], tmps[par]["NT16"], b4("ident"), ADD)
            for par in range(2):
                product(par, 0, "NT16", "N16", "N2")
                product(par, 1, "N16", "NT16", "N2T")
            for par in range(2):
                product(par, 0, "N2T", "N2", "N4")
                product(par, 1, "N2", "N2T", "N4T")
                product(par, 2, "N2", "Pm", "Pm", add="Pm")
            for par in range(2):
                product(par, 0, "N4T", "N4", "N8")
                product(par, 2, "N4", "Pm", "Pm", add="Pm")
            for par in range(2):
                product(par, 0, "N8", "Pm", "Pm", add="Pm")
            for m_, dst in (("M32", None), ("M64", TT[a])):
                for par in range(2):
                    turned(par, 0, "Pm", "Tm")
                    product(par, 1, m_, "Pm", "Z")
                for par in range(2):
                    product(par, 2, "Tm", "Z", "Pm" if dst is None else dst[:, par:8:2, :], add="Pm")
            for h in range(8):
                tok = mm(psum[3][:, h * 64:(h + 1) * 64], AK[:, h, :], VTk[:, a, h * 64:(h + 1) * 64],
                         True, True, after=(V.now(),) + tuple(free[3]), signal=h == 7)
            free[3] = (A("act", AKV[a], psum[3][:, :], Copy, after=(tok,)),)
            for h in range(8):
                tok = mm(psum[7][64 * (h % 2):64 * (h % 2) + 64, (h // 2) * P:(h // 2 + 1) * P],
                         VTk[:, a, h * 64:(h + 1) * 64], RK[:, h, :], True, True,
                         after=(V.now(),) + tuple(free[7]), signal=h == 7)
            free[7] = (A("act", Y[:, 0:4, a * P:(a + 1) * P], ps4(7), Copy, after=(tok,)),)
            V.wait(PE.now())
            A.wait(PE.now())
        join()
        S4 = Space(keep)
        state = S4(512).rearrange("p (m c) -> p m c", c=P)
        Wv = S4(512)
        Uv = S4(512)
        sd = S4(512).rearrange("p (m c) -> p m c", c=P)
        V("memset", state, 0.0)
        V("memset", Wv, 0.0)
        ycols = Y[:, 0:4, :]
        for c in range(NCH):
            a, par = c // 2, c % 2
            rows = slice(64 * par, 64 * par + 64)
            tcs = slice(c * CH, (c + 1) * CH)
            loc = slice(64 * par, 64 * par + 64)
            for m in range(4):
                tok = mm(psum[0][:, m * P:(m + 1) * P], at[:, m, a * P:(a + 1) * P], state[:, m, :],
                         True, True, after=(V.now(), A.now()), signal=m == 3)
            t = V("tt", Wv[rows, :], psum[0][rows, :], AKV[a][rows, :], ADD, after=(tok,))
            for h in range(8):
                tok = mm(psum[1][:, h * 64:(h + 1) * 64], TT[a][:, h, :], Wv[:, h * 64:(h + 1) * 64],
                         True, True, after=(t, A.now()), signal=h == 7)
            tu = A("act", Uv, psum[1][:, :], Copy, scale=-1.0, after=(tok,))
            for m in range(4):
                o = psum[2][:, m * CH:(m + 1) * CH]
                mm(o, state[:, m, :], rt[:, m, tcs], True, False, after=(tu,) if m == 0 else (), loose=True)
                for hp in range(2):
                    h = 2 * m + hp
                    oh = psum[2][64 * hp:64 * hp + 64, m * CH:(m + 1) * CH]
                    tok = mm(oh, Uv[:, h * 64:(h + 1) * 64], RB[a][:, h, loc], False, True, loose=True,
                             signal=m == 3 and hp == 1)
            V("tt", ycols[:, :, tcs], psum[2][:, 0:4 * CH].rearrange("p (m t) -> p m t", t=CH),
              ycols[:, :, tcs], ADD, after=(tok,))
            if c < NCH - 1:
                for m in range(4):
                    o = psum[3][:, m * P:(m + 1) * P]
                    cs = slice(m * P, (m + 1) * P)
                    mm(o, BT[rows, a, cs], Uv[rows, cs], True, False)
                    tok = mm(o, KTk[rows, a, cs], VTk[rows, a, cs], False, True, signal=m == 3)
                V("tt", sd, ps4(3), b4("pair_blocks"), MUL, after=(tok,))
                V("tt", sd, sd, state, ADD)
                end = (c + 1) * CH - 1
                V("tt", state, sd, Dc[:, :, end:end + 1].to_broadcast([P, 4, P]), MUL)
        S5 = Space(S4.at)
        q = t4(S5(4 * T))
        t = V.now()

        def head_mean(src, after):
            for m in range(4):
                tok = mm(psum[4 + m // 2][:, (m % 2) * T:(m % 2 + 1) * T], c_("pair_mean"), src[:, m, :],
                         True, True, after=after, signal=True)
            return tok
        tok = head_mean(ycols, (t,))
        for b in range(2):
            V("tt", ycols[:, 2 * b:2 * b + 2, :], ycols[:, 2 * b:2 * b + 2, :],
              psum[4 + b][:, :].rearrange("p (k t) -> p k t", t=T), SUB, after=(tok,))
        t = V("tt", q, ycols, ycols, MUL)
        tok = head_mean(q, (t,))
        for b in range(2):
            V("ts", q[:, 2 * b:2 * b + 2, :].rearrange("p k t -> p (k t)"), psum[4 + b][:, :], 64e-5, None,
              ADD, after=(tok,))
        t = A("act", q, q, Sqrt, after=(V.now(),))
        V("recip", q, q, after=(t,))
        V("tt", ycols, ycols, q, MUL)
        for m in range(4):
            V("ts", ycols[:, m, :], ycols[:, m, :], p1("gn_g", m), p1("gn_b", m), MUL, ADD)
        V("tt", ycols, ycols, bonus, ADD)
        V("tt", ycols, ycols, g_t, MUL)
        join()

    def branch_b(PB, VB, S):
        t4 = lambda ap: ap.rearrange("p (k t) -> p k t", t=T)
        Q, F, Gt = PB[:, 0:4, :], PB[:, 4:8, :], PB[:, 8:12, :]
        mx, e0, e1, lb, lnlb, omlb, flg = (small[:, 8 + 4 * n:12 + 4 * n] for n in range(7))
        lg = p1("lb_logits")
        V("tt", mx, lg[:, 0:4], lg[:, 4:8], MAX)
        V("tt", e0, lg[:, 0:4], mx, SUB)
        t = V("tt", e1, lg[:, 4:8], mx, SUB)
        A("act", e0, e0, Exp, after=(t,))
        t = A("act", e1, e1, Exp)
        V("tt", e0, e0, e1, ADD, after=(t,))
        V("recip", e0, e0)
        V("tt", lb, e1, e0, MUL)
        V("ts", lb, lb, p1("lb_flag"), None, MUL)
        V("ts", omlb, lb, -1.0, 1.0, MUL, ADD)
        V("ts", flg, lb, 2.0 ** -63, None, ALU.is_ge)
        V("ts", flg, flg, 1.0, 1e30, SUB, MUL)
        t = V("ts", lnlb, lb, 2.0 ** -63, None, MAX)
        t = A("act", lnlb, lnlb, Ln, after=(t,))
        V("tt", lnlb, lnlb, flg, ADD, after=(t,))
        s1, s2, s3, kin, bcum = (t4(S(4 * T)) for _ in range(5))
        A("act", s1, F, Abs, after=(V.now(),))
        t = A("act", s1, s1, Exp, scale=-1.0)
        t = A("act", s1, s1, Ln, bias=1.0)
        t = V("stt", kin, F, 0.0, s1, MAX, ADD, after=(t,))
        t = A("act", kin, kin, Exp, scale=-1.0, after=(t,))
        for m in range(4):
            V("ts", kin[:, m, :], kin[:, m, :], omlb[:, m:m + 1], None, MUL, after=(t,))
        t = V("ts", s2, F, -43.0, None, MAX)
        t = A("act", s2, s2, Exp, scale=-1.0, after=(t,))
        for m in range(4):
            t = A("act", s2[:, m, :], s2[:, m, :], Ln, bias=1.0, scale=lb[:, m:m + 1])
        V("stt", s3, F, 0.0, s1, ALU.min, SUB)
        V("tt", s3, s3, s2, ADD, after=(t,))
        for m in range(4):
            V("ts", s3[:, m, :], s3[:, m, :], lnlb[:, m:m + 1], None, MAX)
        for m in range(4):
            V("scan", bcum[:, m, :], c_("chunk_mask"), s3[:, m, :], 0.0, MUL, ADD)
        sc = S(1024).rearrange("p (g c) -> p g c", c=P)
        tmp8 = S(1024).rearrange("p (g c) -> p g c", c=P)
        Xl = s1, s2
        for n in range(7):
            x = Xl[n % 2]
            if n < 6:
                h = 32 >> n
                split = lambda ap: ap.rearrange("p k (b s) -> p (k b) s", s=2 * h)
                xs, bs, qs, ks = split(x), split(bcum), split(Q), split(kin)
                ref = bs[:, :, h - 1:h].to_broadcast([P, 4 * T // (2 * h), h])
                V("tt", xs[:, :, 0:h], ref, bs[:, :, 0:h], SUB, after=(PE.now(),))
                t = V("tt", xs[:, :, h:2 * h], bs[:, :, h:2 * h], ref, SUB)
                t = A("act", x, x, Exp, after=(t,))
                V("tt", xs[:, :, 0:h], xs[:, :, 0:h], ks[:, :, 0:h], MUL, after=(t,))
                t = V("tt", xs[:, :, h:2 * h], xs[:, :, h:2 * h], qs[:, :, h:2 * h], MUL)
            for bk in range(2):
                for j in range(4):
                    m, a = 2 * bk + j // 2, j % 2
                    cs = slice(a * P, (a + 1) * P)
                    lt, r_ = (x, x) if n < 6 else (kin, Q)
                    tok = mm(psum[2 * (n % 2) + bk][:, j * P:(j + 1) * P], lt[:, m, cs], r_[:, m, cs],
                             True, True, after=(t,) + tuple(free[2 * (n % 2) + bk]), signal=j == 3)
                src = psum[2 * (n % 2) + bk][:, :].rearrange("p (g c) -> p g c", c=P)
                msk = c_(f"level{n}").rearrange("p (o c) -> p o c", o=1).to_broadcast([P, 4, P])
                dst = (sc if n == 0 else tmp8)[:, 4 * bk:4 * bk + 4, :]
                free[2 * (n % 2) + bk] = (V("tt", dst, src, msk, MUL, after=(tok,)),)
            if n:
                V("tt", sc, sc, tmp8, ADD)
        b16 = bcum.rearrange("p k (c s) -> p (k c) s", s=CH)
        s16 = s3.rearrange("p k (c s) -> p (k c) s", s=CH)
        V("tt", s16, b16[:, :, CH - 1:CH].to_broadcast([P, 16, CH]), b16, SUB)
        t = A("act", s3, s3, Exp, after=(V.now(),))
        V("tt", s3, s3, kin, MUL, after=(t,))
        eb = kin
        t = A("act", eb, bcum, Exp, after=(V.now(), PE.now()))
        t = V("tt", Q, Q, eb, MUL, after=(t,))
        khat = tmp8.rearrange("p (a m) c -> p a m c", a=2)
        for a in range(2):
            for m in range(4):
                tok = PE("tr", psum[a][:, m * P:(m + 1) * P], s3[:, m, a * P:(a + 1) * P], c_("ident"),
                         after=(t,) + tuple(free[a]), signal=m == 3)
            free[a] = (V("copy", khat[:, a, :, :], psum[a][:, :].rearrange("p (m c) -> p m c", c=P),
                         after=(tok,)),)
        st = [None, s1.rearrange("p k t -> p (k t)")[:, 0:512], s1.rearrange("p k t -> p (k t)")[:, 512:1024],
              s2.rearrange("p k t -> p (k t)")[:, 0:512]]
        t = V.now()
        for c in range(NCH - 1):
            a, par = c // 2, c % 2
            rows = slice(64 * par, 64 * par + 64)
            for m in range(4):
                tok = mm(psum[2 + c][:, m * P:(m + 1) * P], khat[rows, a, m, :], VB[rows, a, m * P:(m + 1) * P],
                         True, True, after=(t,) + tuple(free[2 + c]), signal=m == 3)
            nxt = st[c + 1].rearrange("p (m c) -> p m c", c=P)
            if c == 0:
                V("copy", nxt, psum[2][:, :].rearrange("p (m c) -> p m c", c=P), after=(tok,))
            else:
                prev = st[c].rearrange("p (m c) -> p m c", c=P)
                end = (c + 1) * CH - 1
                V("tt", nxt, prev, eb[:, :, end:end + 1].to_broadcast([P, 4, P]), MUL)
                V("tt", nxt, nxt, psum[2 + c][:, :].rearrange("p (m c) -> p m c", c=P), ADD, after=(tok,))
        t = V.now()
        yb = Y[:, 4:8, :]
        for m in range(4):
            bank = psum[6 + m // 2]
            for a in range(2):
                at0 = (m % 2) * T + a * P
                mm(bank[:, at0:at0 + P], VB[:, a, m * P:(m + 1) * P], sc[:, 2 * m + a, :], True, False,
                   after=(t,), loose=True)
                for c in (2 * a, 2 * a + 1):
                    if c:
                        tok = mm(bank[:, at0 + (c % 2) * CH:at0 + (c % 2 + 1) * CH],
                                 st[c][:, m * P:(m + 1) * P], Q[:, m, c * CH:(c + 1) * CH], False, True,
                                 loose=True, signal=c == 3)
        for b in range(2):
            V("copy", yb[:, 2 * b:2 * b + 2, :], psum[6 + b][:, :].rearrange("p (k t) -> p k t", t=T),
              after=(tok,))
        head_rms_gate(yb, s3, s1, Gt, lambda m: p1("b_gn_g", m))
        join()

    def head_rms_gate(y, q, sg, Gt, gain):
        t = A("act", q, y, Square, after=(V.now(), PE.now()))
        sig = A("act", sg, Gt, Sigmoid)
        for m in range(4):
            tok = mm(psum[m // 2][:, (m % 2) * T:(m % 2 + 1) * T], c_("mean128"), q[:, m, :],
                     True, True, after=(t,) + tuple(free[m // 2]), signal=True)
        for b in range(2):
            V("ts", q[:, 2 * b:2 * b + 2, :].rearrange("p k t -> p (k t)"), psum[b][:, :], 1e-6, None,
              ADD, after=(tok,))
            free[b] = (V.now(),)
        t = A("act", q, q, Sqrt, after=(V.now(),))
        V("recip", q, q, after=(t, sig))
        V("tt", y, y, q, MUL)
        V("tt", sg, sg, Gt, MUL)
        for m in range(4):
            V("stt", y[:, m, :], y[:, m, :], gain(m), sg[:, m, :], MUL, MUL)

    def branch_c(PC, VC, WI, S):
        t4 = lambda ap: ap.rearrange("p (k t) -> p k t", t=T)
        rot = t4(S(8 * T))
        cosb = c_("rope_cos").rearrange("p (o t) -> p o t", o=1).to_broadcast([P, 8, T])
        for k in range(8):
            tok = mm(psum[k // 2][:, (k % 2) * T:(k % 2 + 1) * T], c_("swap32"), PC[:, k, :], True, True,
                     signal=True)
        V("tt", rot, PC, cosb, MUL)
        for b in range(4):
            sinb = c_("rope_sin").rearrange("p (o t) -> p o t", o=1).to_broadcast([P, 2, T])
            V("tt", PC[:, 2 * b:2 * b + 2, :], psum[b][:, :].rearrange("p (k t) -> p k t", t=T), sinb, MUL,
              after=(tok,))
        t = V("tt", rot, rot, PC, ADD)
        kd = t4(S(2 * T))
        for c in range(2):
            tok = mm(psum[4][:, c * T:(c + 1) * T], c_(f"dup{c}"), rot[:, 4, :], True, True, after=(t,),
                     signal=True)
        kd_t = A("act", kd.rearrange("p k t -> p (k t)"), psum[4][:, :], Copy, after=(tok,))
        wis = small[:, 64:72]
        V("ts", wis, WI, 0.5 * 0.125, None, MUL)
        score = S(2 * T).rearrange("p (a s) -> p a s", s=T)
        work_ = S(2 * T).rearrange("p (a s) -> p a s", s=T)
        dotw = S(T)
        top8 = small[:, 80:88]
        for a in range(2):
            n = P * (a + 1)
            for h in range(4):
                rows = slice(64 * (h % 2), 64 * (h % 2) + 64)
                b = (5, 6)[h % 2]
                tok = mm(psum[b][:, (h // 2) * T:(h // 2) * T + n], rot[rows, 5 + h // 2, a * P:(a + 1) * P],
                         rot[rows, 7, 0:n], True, True, after=(t,) + tuple(free[b]), signal=True)
            for h in range(4):
                b = (5, 6)[h % 2]
                dst = score[:, a, 0:n] if h == 0 else dotw[:, 0:n]
                V("ts", dst, psum[b][:, (h // 2) * T:(h // 2) * T + n], 0.0, wis[:, 4 * a + h:4 * a + h + 1],
                  MAX, MUL, after=(tok,))
                if h:
                    V("tt", score[:, a, 0:n], score[:, a, 0:n], dotw[:, 0:n], ADD)
            free[5] = free[6] = (V.now(),)
            nonc = c_("noncausal")[:, a * T:a * T + n]
            V("tt", work_[:, a, 0:n], score[:, a, 0:n], nonc, ADD)
            for _ in range(TOPK // 8):
                V("max8", top8, work_[:, a, 0:n])
                V("replace", work_[:, a, 0:n], top8, work_[:, a, 0:n], -3e30)
            V("ts", work_[:, a, 0:n], work_[:, a, 0:n], -2e30, -1e30, ALU.is_gt, MUL)
            V("tt", work_[:, a, 0:n], work_[:, a, 0:n], nonc, ADD)
        mark = S.at
        for a in range(2):
            S.at = mark
            n = P * (a + 1)
            L = S(8 * n).rearrange("p (h s) -> p h s", s=n)
            probT = S(8 * n).rearrange("p (h s) -> p h s", s=n)
            nm, sm = small[:, 96:104], small[:, 104:112]
            per = 512 // T
            for h in range(8):
                rows = slice(64 * (h % 2), 64 * (h % 2) + 64)
                b = 2 * (h % 2) + h // 4
                tok = mm(psum[b][:, (h // 2 % 2) * T:(h // 2 % 2) * T + n], rot[rows, h // 2, a * P:(a + 1) * P],
                         kd[rows, h // 4, 0:n], True, True, after=(kd_t,) + tuple(free[b]), signal=True)
            for h in range(8):
                b = 2 * (h % 2) + h // 4
                t = V("stt", L[:, h, :], psum[b][:, (h // 2 % 2) * T:(h // 2 % 2) * T + n], 0.125,
                      work_[:, a, 0:n], MUL, ADD, after=(tok, PE.now()))
            for b in range(4):
                free[b] = (t,)
            t = V("rmax", nm, L, axis=AX.X, negate=True)
            for h in range(8):
                t = A("act", L[:, h, :], L[:, h, :], Exp, bias=nm[:, h:h + 1], accum_out=sm[:, h:h + 1],
                      after=(t,) if h == 0 else ())
            V("recip", sm, sm, after=(A.now(),))
            t = V("tt", L, L, sm.rearrange("p (h o) -> p h o", o=1).to_broadcast([P, 8, n]), MUL)
            for j in range(2 * (a + 1)):
                b = 4 + j
                for i in range(4):
                    idx = 4 * j + i
                    h, s = idx // (a + 1), idx % (a + 1)
                    tok = PE("tr", psum[b][:, i * P:(i + 1) * P], L[:, h, s * P:(s + 1) * P], c_("ident"),
                             after=(t,) + tuple(free[b]), signal=i == 3)
                dst = probT.rearrange("p h s -> p (h s)")[:, j * 512:(j + 1) * 512]
                free[b] = (copy_out(dst, psum[b][:, :], (tok, PE.now())),)
            pts = (V.now(), A.now())
            pt = probT.rearrange("p h (s q) -> p (h s) q", q=P)
            for h in range(8):
                rows = slice(64 * (h % 2), 64 * (h % 2) + 64)
                out = psum[0][rows, (h // 2) * P:(h // 2 + 1) * P]
                for s in range(a + 1):
                    tok = mm(out, VC[:, s, 64 * (h // 4):64 * (h // 4) + 64], pt[:, h * (a + 1) + s, :],
                             s == 0, s == a, after=pts + tuple(free[0]), signal=h == 7 and s == a)
            t = V("copy", Y[:, 8:12, a * P:(a + 1) * P], psum[0][:, :].rearrange("p (m q) -> p m q", q=P),
                  after=(tok,))
            free[0] = (t,)
        join()

    PLACE = (0, 1, 2, 0, 1)

    def feed_forward(group0, groups, layer, conv, act0, dve0, up0, gates, scale_of):
        join()
        s_a, s_v = ff_sems[conv]
        NA = 3 if conv else 1
        NV = 6 if conv else (3 if gates is not None else 2)
        zeros = small[:, 128:256]
        V("memset", zeros, 0.0)
        zt = V("memset", rstd[:, :], 0.0)
        for b in range(4):
            for hf in range(2):
                mm(psum[b][:, hf * T:(hf + 1) * T], zeros, rstd[:, :], hf == 0, False, after=(zt,), loose=True)
        at = [0]

        def buffers():
            at[0] += 3
            return [arena[:, (GATE_COLS + at[0] - 3 + n) * T:(GATE_COLS + at[0] - 2 + n) * T] for n in range(3)]
        CG, CV, SG, HD = buffers(), buffers(), buffers(), buffers()

        def at_layer(per_layer, v):
            return v if layer is None else layer * per_layer + v

        def token(kind, i, j, n):
            s, per, base = {"a": (s_a, NA, act0), "v": (s_v, NV, dve0), "u": (s_up, 1, up0)}[kind]
            return (s, at_layer(FF_GROUPS * per, i * (RING * per) + (base + j * per + n)))

        def done(i, j):
            return (s_done, at_layer(LAYER1_GROUPS, i * RING + (group0 + j + 1)))

        def slot(j):
            return ((group0 + j) % RING) * SLOT

        def unit(j, n):
            return ring[:, slot(j) + n * UNIT:slot(j) + (n + 1) * UNIT]

        def up(i, j, first):
            b, pe = psum[4 + PLACE[j % RING]], nc.tensor
            pe.wait_ge(s_slot[(group0 + j) % RING],
                       at_layer(16 * (LAYER1_GROUPS // RING), i * 16 + 16 * ((group0 + j) // RING + 1)))
            if not first:
                pe.wait_ge(*token("v", i, j - 2, 4 if conv else 2))
            for half in range(2):
                w = unit(j, half).rearrange("p (k c) -> p k c", c=P)
                for k in range(KT):
                    ins = pe.matmul(b[:, half * T:(half + 1) * T], w[:, k, :], U[:, k, :],
                                    start=k == 0, stop=k == KT - 1)
            ins.then_inc(s_up, 1)

        def down(i, j, last):
            pe, n = nc.tensor, PLACE[j % RING]
            pe.wait_ge(*token("v", i, j, NV))
            w = unit(j, 2)
            for dt in range(KT):
                ins = pe.matmul(psum[dt // 2][:, (dt % 2) * T:(dt % 2 + 1) * T], w[:, dt * P:(dt + 1) * P],
                                HD[n], start=False, stop=last, skip_group_check=True)
            ins.then_inc(s_done, 1)

        def middle(i, j, first):
            n = PLACE[j % RING]
            pg, pv = (psum[4 + n][:, h * T:(h + 1) * T] for h in range(2))
            act, dve = nc.scalar, nc.vector
            chain = [0]

            def v(op, *args, after=()):
                if not (first and j == 0 and chain[0] == 0):
                    dve.wait_ge(*token("v", i, j, chain[0]))
                for tok in after:
                    dve.wait_ge(*tok)
                issue(dve, op)(*args).then_inc(s_v, 1)
                chain[0] += 1
            act.wait_ge(*token("u", i, j, 1))
            if not first:
                act.wait_ge(*token("v", i, j - 2, NV))
            if conv:
                ex = ring[:, slot(j) + GROUP * UNIT:slot(j) + SLOT]
                act.activation(CG[n], pg, Ident, bias=ex[:, 3:4], scale=ex[:, 2:3]).then_inc(s_a, 1)
                act.activation(CV[n], pv, Ident, bias=ex[:, 7:8], scale=ex[:, 6:7]).then_inc(s_a, 1)
                for h, (c_buf, p_) in enumerate(((CG[n], pg), (CV[n], pv))):
                    for tap in (1, 0):
                        d = 2 - tap
                        v("stt", c_buf[:, d:T], p_[:, 0:T - d], ex[:, 4 * h + tap:4 * h + tap + 1],
                          c_buf[:, d:T], MUL, ADD, after=(token("a", i, j, 2),) if h == 0 and tap else ())
                act.wait_ge(*token("v", i, j, 2))
                act.activation(SG[n], CG[n], Sigmoid).then_inc(s_a, 1)
                v("tt", SG[n], SG[n], CG[n], MUL, after=(token("a", i, j, 3),))
                v("tt", HD[n], SG[n], CV[n], MUL, after=() if first else (done(i, j - 2),))
            else:
                act.activation(SG[n], pg, Sigmoid).then_inc(s_a, 1)
                v("tt", SG[n], SG[n], pg, MUL, after=(token("a", i, j, 1),))
                v("tt", HD[n], SG[n], pv, MUL, after=() if first else (done(i, j - 2),))
                if gates is not None:
                    e = (i * RING + j) // (FFE // P)
                    g = gates[:, e * T:(e + 1) * T] if isinstance(e, int) else gates[:, bass.ds(e * T, T)]
                    v("tt", HD[n], HD[n], g, MUL)

        ET = mybir.EngineType
        up(0, 0, True)
        middle(0, 0, True)
        up(0, 1, True)
        middle(0, 1, True)
        down(0, 0, False)
        rounds = (groups - 2) // RING
        with nc.Fori(0, rounds, engines=(nc.tensor.engine, nc.vector.engine, nc.scalar.engine)) as i:
            for j in range(2, 2 + RING):
                up(i, j, False)
                down(i, j - 1, False)
                middle(i, j, False)
        rest = 2 + rounds * RING
        for g in range(rest, groups):
            up(rounds, g - rounds * RING, False)
            down(rounds, g - 1 - rounds * RING, False)
            middle(rounds, g - rounds * RING, False)
        last = groups - 1 - rounds * RING
        down(rounds, last, True)
        fin = done(rounds, last)
        last_done[0] = fin
        for dt in range(KT):
            src = psum[dt // 2][:, (dt % 2) * T:(dt % 2 + 1) * T]
            V("stt", X[:, dt, :], src, scale_of(dt), X[:, dt, :], MUL, ADD, after=(fin,) if dt == 0 else ())
        A.wait(fin)
        join()

    GATE_COLS = 8

    def modulation(st, cond, mod):
        for u in range(GROUP * ADA_GROUPS):
            need(st, u)
            w = st.weights(u).rearrange("p (k c) -> p k c", c=P)
            for k in range(KT - 1):
                mm(psum[0][:, u:u + 1], w[:, k, :], cond[:, k:k + 1], k == 0, False)
            tok = last_mm(st, u, psum[0][:, u:u + 1], w[:, KT - 1, :], cond[:, KT - 1:KT], False, True)
        V("tt", mod, psum[0][:, 0:48], p2("ada_b"), ADD, after=(tok,))
        for n, norm in ((1, "norm_mix"), (4, "norm_ffn")):
            V("stt", mod[:, 8 * n:8 * n + 8], mod[:, 8 * n:8 * n + 8], 1.0, p2(norm), ADD, MUL)
        join()

    def linear_attention(units, S, rope):
        t4 = lambda ap: ap.rearrange("p (k t) -> p k t", t=T)
        P2 = t4(S(20 * T))
        GV = S(2 * 512).rearrange("p (a c) -> p a c", a=2)
        RV = S(2 * 512).rearrange("p (a c) -> p a c", a=2)
        units(P2, GV, RV)
        gq, gk, gr, rq, rk, rg = (P2[:, s:e, :] for s, e in ((0, 2), (2, 4), (4, 8), (8, 12), (12, 16), (16, 20)))
        mark = S.at
        la, eb, enb, s4 = t4(S(2 * T)), t4(S(2 * T)), t4(S(2 * T)), t4(S(2 * T))
        ga = S(T)
        wga = p2("w_ga").rearrange("p (k r) -> p k r", r=16)
        for k in range(KT):
            tok = mm(psum[0][0:16, 0:T], wga[:, k, :], U[:, k, :], k == 0, k == KT - 1, signal=k == KT - 1)
        t = V("copy", ga[0:16, :], psum[0][0:16, 0:T], after=(tok,))
        for m in range(2):
            tok = mm(psum[1][:, m * T:(m + 1) * T], p2("w_alpha")[0:16, m * P:(m + 1) * P], ga[0:16, :],
                     True, True, after=(t,), signal=True)
        for m in range(2):
            V("ts", la[:, m, :], psum[1][:, m * T:(m + 1) * T], p2("b_alpha", m), None, ADD, after=(tok,))
        A("act", s4, la, Abs, after=(V.now(),))
        t = A("act", s4, s4, Exp, scale=-1.0)
        t = A("act", s4, s4, Ln, bias=1.0)
        V("stt", la, la, 0.0, s4, ALU.min, SUB, after=(t,))
        V("ts", la, la, 1.0 / 16.0, None, MUL)
        bc_ = s4
        for m in range(2):
            V("scan", bc_[:, m, :], c_("chunk_mask"), la[:, m, :], 0.0, MUL, ADD)
        t = A("act", eb, bc_, Exp, after=(V.now(),))
        t = A("act", enb, bc_, Exp, scale=-1.0)
        kend = la
        split = lambda ap: ap.rearrange("p k (c s) -> p (k c) s", s=CH)
        V("tt", split(kend), split(bc_)[:, :, CH - 1:CH].to_broadcast([P, 8, CH]), split(bc_), SUB)
        e = A("act", kend, kend, Exp, after=(V.now(),))
        V("tt", kend, kend, gk, MUL, after=(e,))
        V("ts", gq, gq, 0.125, None, MUL)
        kb, qf, kf, qb = t4(S(2 * T)), t4(S(2 * T)), t4(S(2 * T)), s4
        V("tt", qb, gq, enb, MUL)
        V("tt", qf, gq, eb, MUL)
        V("tt", kf, gk, enb, MUL)
        t = V("tt", kb, gk, eb, MUL)
        ps4 = lambda b: psum[b][:, :].rearrange("p (h c) -> p h c", c=P)
        sc = S(1024).rearrange("p (m r a c) -> p m r a c", m=2, r=2, a=2)
        tmp = S(512).rearrange("p (g c) -> p g c", c=P)
        for par in range(2):
            rows = slice(64 * par, 64 * par + 64)
            for d, (lt, r_, mask) in enumerate(((kf, qf, "incl_up"), (kb, qb, "strict_low"))):
                b = 2 + 2 * d + par
                for m in range(2):
                    for a in range(2):
                        cs = slice(a * P, (a + 1) * P)
                        tok = mm(psum[b][:, (2 * m + a) * P:(2 * m + a + 1) * P], lt[rows, m, cs],
                                 r_[rows, m, cs], True, True, after=(t,), signal=m == 1 and a == 1)
                msk = c_(mask).rearrange("p (o c) -> p o c", o=1).to_broadcast([P, 4, P])
                V("tt", tmp, ps4(b), msk, MUL, after=(tok,))
                for m in range(2):
                    dst = sc[:, m, par, :, :]
                    src = tmp[:, 2 * m:2 * m + 2, :]
                    V("copy", dst, src) if d == 0 else V("tt", dst, dst, src, ADD)
        kt_ = S(512).rearrange("p (a c) -> p a c", a=2)
        for a in range(2):
            for m in range(2):
                tok = PE("tr", psum[6][:, (2 * a + m) * P:(2 * a + m + 1) * P], kend[:, m, a * P:(a + 1) * P],
                         c_("ident"), after=(V.now(),), signal=True)
        t = V("copy", kt_, psum[6][:, :].rearrange("p (a c) -> p a c", a=2), after=(tok,))
        stt_ = [None] + [S(256).rearrange("p (m v) -> p m v", v=P) for _ in range(3)]
        for c in range(NCH - 1):
            a, par = c // 2, c % 2
            rows = slice(64 * par, 64 * par + 64)
            b = 2 + c
            for h in range(4):
                tok = mm(psum[b][64 * (h % 2):64 * (h % 2) + 64, (h // 2) * P:(h // 2 + 1) * P],
                         kt_[rows, a, 64 * h:64 * h + 64], GV[rows, a, h * P:(h + 1) * P], True, True,
                         after=(V.now(),), signal=h == 3)
            for m in range(2):
                src = psum[b][:, m * P:(m + 1) * P]
                if c == 0:
                    V("copy", stt_[1][:, m, :], src, after=(tok,))
                else:
                    end = (c + 1) * CH - 1
                    V("stt", stt_[c + 1][:, m, :], stt_[c][:, m, :], eb[:, m, end:end + 1], src, MUL, ADD,
                      after=(tok,))
        t = V.now()
        for par in range(2):
            rows = slice(64 * par, 64 * par + 64)
            for m in range(2):
                h = 2 * m + par
                for a in range(2):
                    at0 = m * T + a * P
                    mm(psum[6 + par][:, at0:at0 + P], GV[:, a, h * P:(h + 1) * P], sc[:, m, par, a, :],
                       True, False, after=(t,), loose=True)
                    for c in (2 * a, 2 * a + 1):
                        if c:
                            tok = mm(psum[6 + par][:, at0 + (c % 2) * CH:at0 + (c % 2 + 1) * CH],
                                     stt_[c][rows, m, :], qf[rows, m, c * CH:(c + 1) * CH], False, True,
                                     loose=True, signal=c == 3)
        yg = Y[:, 0:4, :]
        for par in range(2):
            V("copy", yg[:, par:4:2, :], psum[6 + par][:, :].rearrange("p (k t) -> p k t", t=T), after=(tok,))
        join()
        S.at = mark
        qn, sn = t4(S(4 * T)), t4(S(4 * T))
        head_rms_gate(yg, qn, sn, gr, lambda m: p2("gla_g", m))
        cos_b = rope[:, 0:T].rearrange("p (o t) -> p o t", o=1).to_broadcast([P, 4, T])
        sin_b = rope[:, T:2 * T].rearrange("p (o t) -> p o t", o=1).to_broadcast([P, 2, T])
        for n, src in enumerate((rq, rk)):
            for m in range(4):
                b = 4 + 2 * n + m // 2
                tok = mm(psum[b][:, (m % 2) * T:(m % 2 + 1) * T], c_("swap64"), src[:, m, :], True, True,
                         signal=True)
            V("tt", src, src, cos_b, MUL, after=(tok,))
            for bb in range(2):
                V("tt", sn[:, 2 * bb:2 * bb + 2, :],
                  psum[4 + 2 * n + bb][:, :].rearrange("p (k t) -> p k t", t=T), sin_b, MUL)
            V("tt", src, src, sn, ADD)
        join()
        S.at = mark
        sc2 = S(1024).rearrange("p (m a c) -> p m a c", m=4, a=2)
        kd, qd = t4(S(4 * T)), t4(S(4 * T))
        kdt = S(1024).rearrange("p (a m c) -> p a m c", a=2, m=4)
        st2 = [None] + [S(512).rearrange("p (m v) -> p m v", v=P) for _ in range(3)]
        for m in range(4):
            tab = lambda name: c_(name)[:, m * CH:(m + 1) * CH].rearrange("p (o s) -> p o s", o=1)\
                .to_broadcast([P, NCH, CH])
            V("tt", kd[:, m, :].rearrange("p (c s) -> p c s", s=CH),
              rk[:, m, :].rearrange("p (c s) -> p c s", s=CH), tab("ret_k"), MUL)
            V("tt", qd[:, m, :].rearrange("p (c s) -> p c s", s=CH),
              rq[:, m, :].rearrange("p (c s) -> p c s", s=CH), tab("ret_q"), MUL)
        for bk in range(2):
            for j in range(4):
                m, a = 2 * bk + j // 2, j % 2
                cs = slice(a * P, (a + 1) * P)
                tok = mm(psum[bk][:, j * P:(j + 1) * P], rk[:, m, cs], rq[:, m, cs], True, True, signal=j == 3)
            for mm_ in range(2):
                m = 2 * bk + mm_
                intra = c_("ret_intra")[:, m * P:(m + 1) * P].rearrange("p (o c) -> p o c", o=1)\
                    .to_broadcast([P, 2, P])
                V("tt", sc2[:, m, :, :], ps4(bk)[:, 2 * mm_:2 * mm_ + 2, :], intra, MUL, after=(tok,))
        V("ts", sc2.rearrange("p m a c -> p (m a c)"), sc2.rearrange("p m a c -> p (m a c)"), 128 ** -0.5, None, MUL)
        for a in range(2):
            for m in range(4):
                tok = PE("tr", psum[2 + a][:, m * P:(m + 1) * P], kd[:, m, a * P:(a + 1) * P], c_("ident"),
                         after=(V.now(),), signal=m == 3)
            copy_out(kdt[:, a, :, :], ps4(2 + a), (tok,))
        t = (V.now(), A.now())
        for c in range(NCH - 1):
            a, par = c // 2, c % 2
            rows = slice(64 * par, 64 * par + 64)
            b = 4 + c
            for m in range(4):
                tok = mm(psum[b][:, m * P:(m + 1) * P], kdt[rows, a, m, :], RV[rows, a, m * P:(m + 1) * P],
                         True, True, after=t, signal=m == 3)
            for m in range(4):
                src = psum[b][:, m * P:(m + 1) * P]
                if c == 0:
                    V("copy", st2[1][:, m, :], src, after=(tok,))
                else:
                    V("stt", st2[c + 1][:, m, :], st2[c][:, m, :], c_("ret_chunk")[:, m:m + 1], src, MUL, ADD,
                      after=(tok,))
        t = V.now()
        for m in range(4):
            bank = psum[m // 2]
            for a in range(2):
                at0 = (m % 2) * T + a * P
                mm(bank[:, at0:at0 + P], RV[:, a, m * P:(m + 1) * P], sc2[:, m, a, :], True, False,
                   after=(t,), loose=True)
                for c in (2 * a, 2 * a + 1):
                    if c:
                        tok = mm(bank[:, at0 + (c % 2) * CH:at0 + (c % 2 + 1) * CH], st2[c][:, m, :],
                                 qd[:, m, c * CH:(c + 1) * CH], False, True, loose=True, signal=c == 3)
        yr = Y[:, 4:8, :]
        for b in range(2):
            V("copy", yr[:, 2 * b:2 * b + 2, :], psum[b][:, :].rearrange("p (k t) -> p k t", t=T), after=(tok,))
        t = V.now()
        for m in range(4):
            tok = mm(psum[2 + m // 2][:, (m % 2) * T:(m % 2 + 1) * T], c_("mean128"), yr[:, m, :], True, True,
                     after=(t,), signal=True)
        for b in range(2):
            V("tt", yr[:, 2 * b:2 * b + 2, :], yr[:, 2 * b:2 * b + 2, :],
              psum[2 + b][:, :].rearrange("p (k t) -> p k t", t=T), SUB, after=(tok,))
        t = A("act", qd, yr, Square, after=(V.now(),))
        sig = A("act", kd, rg, Sigmoid)
        for m in range(4):
            tok = mm(psum[4 + m // 2][:, (m % 2) * T:(m % 2 + 1) * T], c_("mean128"), qd[:, m, :], True, True,
                     after=(t,), signal=True)
        for b in range(2):
            V("ts", qd[:, 2 * b:2 * b + 2, :].rearrange("p k t -> p (k t)"), psum[4 + b][:, :], 1e-6, None, ADD,
              after=(tok,))
        t = A("act", qd, qd, Sqrt, after=(V.now(),))
        V("recip", qd, qd, after=(t, sig))
        V("tt", yr, yr, qd, MUL)
        for m in range(4):
            V("ts", yr[:, m, :], yr[:, m, :], p2("ret_g", m), p2("ret_b", m), MUL, ADD)
        V("tt", kd, kd, rg, MUL)
        V("tt", yr, yr, kd, MUL)
        join()

    def route(gates):
        rw = router[:, :].rearrange("p (k e) -> p k e", e=EXPERTS)
        sm = small
        lg, m8, idx, oh0, oh1, gt = (sm[:, 256 + 8 * n:264 + 8 * n] for n in range(6))
        idf, p0, p1_ = sm[:, 304:312], sm[:, 312:313], sm[:, 313:314]
        lane = sm[:, 320:328]
        gT = sm[0:8, 0:T]
        for e in range(EXPERTS):
            V("memset", lane[:, e:e + 1], float(e))
        for a in range(2):
            for k in range(KT):
                tok = mm(psum[0][:, a * 8:a * 8 + 8], U[:, k, a * P:(a + 1) * P], rw[:, k, :], k == 0,
                         k == KT - 1, signal=k == KT - 1)
            V("copy", lg, psum[0][:, a * 8:a * 8 + 8], after=(tok,))
            V("max8", m8, lg)
            V("maxidx", idx.bitcast(u32), m8, lg)
            V("copy", idf, idx.bitcast(u32))
            V("ts", oh0, lane, idf[:, 0:1], None, ALU.is_equal)
            V("ts", oh1, lane, idf[:, 1:2], None, ALU.is_equal)
            t = V("tt", p1_, m8[:, 1:2], m8[:, 0:1], SUB)
            t = A("act", p1_, p1_, Exp, after=(t,))
            V("ts", p0, p1_, 1.0, None, ADD, after=(t,))
            V("recip", p0, p0)
            V("tt", p1_, p1_, p0, MUL)
            V("ts", gt, oh0, p0, None, MUL)
            t = V("stt", gt, oh1, p1_, gt, MUL, ADD)
            tok = PE("tr", psum[1][0:8, a * P:(a + 1) * P], gt, c_("ident"), after=(t,))
            V("copy", gT[:, a * P:(a + 1) * P], psum[1][0:8, a * P:(a + 1) * P], after=(tok,))
        t = V.now()
        for e in range(EXPERTS):
            sel = c_("ident")[0:8, e:e + 1].to_broadcast([8, P])
            tok = mm(psum[2 + e // 2][:, (e % 2) * T:(e % 2 + 1) * T], sel, gT, True, True, after=(t,), signal=True)
        for b in range(4):
            copy_out(gates[:, 2 * b * T:(2 * b + 2) * T], psum[2 + b][:, :], (tok,))
        join()

    layer_stream = [None]

    def run(u0, n, dst, stream=None, banks=(1, 2, 3, 4, 5, 6, 7)):
        for j in range(0, n, 2):
            b = banks[(j // 2) % len(banks)]
            PE.wait(*free[b])
            k = min(2, n - j)
            for h in range(k):
                tok = project(stream or layer_stream[0], u0 + j + h, b, h)
            free[b] = (copy_out(dst[:, j:j + k, :].rearrange("p k t -> p (k t)"), psum[b][:, 0:k * T],
                                (tok,)),)

    def run_tokens(u0, n, dst, stream=None):
        for j in range(n):
            b = 1 + j % 7
            PE.wait(*free[b])
            tok = project_tokens(stream or layer_stream[0], u0 + j, b, 0)
            free[b] = (copy_out(dst[:, :, j * P:(j + 1) * P],
                                psum[b][:, 0:T].rearrange("p (a c) -> p a c", a=2), (tok,)),)

    weight_stream()

    for dst, src in ((const, a_const), (norms, a_norms[:, 0:KT]), (final2, a_norms[:, KT:2 * KT]),
                     (router, a_router)):
        nc.scalar.dma_start(dst[:, :], src).then_inc(s_in, 16)
    nc.scalar.dma_start(X, a_x.rearrange("k p t -> p k t")).then_inc(s_in, 16)
    for q in work:
        q.engine.wait_ge(s_in, 80)

    with nc.Fori(0, LAYERS, engines=tuple(q.engine.engine for q in work)) as layer:
        st = Stream(0, layer)
        nc.scalar.dma_start(par1[:, :], a_par1[bass.ds(layer, 1), :, :].rearrange("o p n -> p (o n)"))\
            .then_inc(s_par, 16)
        for q in work:
            q.engine.wait_ge(s_par, layer * 16 + 16)
        t4 = lambda ap: ap.rearrange("p (k t) -> p k t", t=T)
        rms(X, 1e-6, lambda k: p1("norm_mix", k))

        layer_stream[0] = st
        PA = t4(arena[:, 0:14 * T])
        run(0, 14, PA)
        need(st, 14)
        join()
        branch_a(PA, st.weights(14), st.done(4))
        if probe:
            probe("ya", Y[:, 0:4, :], A)
        S = Space()
        PB = t4(S(12 * T))
        VB = S(1024).rearrange("p (a c) -> p a c", a=2)
        run(15, 8, PB[:, 0:8, :])
        run_tokens(23, 4, VB)
        run(27, 4, PB[:, 8:12, :])
        join()
        branch_b(PB, VB, S)
        S = Space()
        PC = t4(S(8 * T))
        VC = S(256).rearrange("p (a c) -> p a c", a=2)
        run(31, 8, PC)
        run_tokens(39, 1, VC)
        WI = small[:, 72:80]
        widx = p1("w_idx").rearrange("p (k h) -> p k h", h=4)
        for a in range(2):
            for k in range(KT):
                tok = mm(psum[0][:, 4 * a:4 * a + 4], U[:, k, a * P:(a + 1) * P], widx[:, k, :], k == 0,
                         k == KT - 1, signal=k == KT - 1)
        V("copy", WI, psum[0][:, 0:8], after=(tok,))
        join()
        branch_c(PC, VC, WI, S)
        gat = t4(arena[:, 0:24 * T])
        for j in range(0, 24, 2):
            b = (j // 2) % 8
            PE.wait(*free[b])
            for h in range(2):
                tok = project(st, 40 + j + h, b, h)
            free[b] = (A("act", gat[:, j:j + 2, :].rearrange("p k t -> p (k t)"), psum[b][:, :], Sigmoid,
                         after=(tok,)),)
        join()
        prod = t4(arena[:, 24 * T:28 * T])
        for n in range(3):
            for dt in range(KT):
                b = (n * KT + dt) % 8
                for m in range(4):
                    u = 64 + 4 * n + m
                    if dt == 0:
                        need(st, u)
                    args = (psum[b][:, 0:T], st.weights(u)[:, dt * P:(dt + 1) * P], Y[:, 4 * n + m, :],
                            m == 0, m == 3)
                    if m == 0:
                        PE.wait(*free[b])
                    if dt == KT - 1 and u % GROUP == GROUP - 1:
                        tok = last_mm(st, u, *args)
                    else:
                        tok = mm(*args, signal=m == 3)
                gk_ = gat[:, n * KT + dt, :]
                if n == 0:
                    t = V("tt", U[:, dt, :], psum[b][:, 0:T], gk_, MUL, after=(tok,))
                else:
                    t = V("tt", prod[:, dt % 4, :], psum[b][:, 0:T], gk_, MUL, after=(tok,))
                    V("tt", U[:, dt, :], U[:, dt, :], prod[:, dt % 4, :], ADD)
                free[b] = (t,)
        join()
        for dt in range(KT):
            tok = project(st, 76 + dt, dt, 0)
            V("tt", X[:, dt, :], X[:, dt, :], psum[dt][:, 0:T], ADD, after=(tok,))
        join()
        if probe:
            probe("hmix", X, A)
        rms(X, 1e-6, lambda k: p1("norm_ffn", k))
        feed_forward(MIX1_GROUPS, FF_GROUPS, layer, True, 0, 0, 0, None, lambda dt: 1.0)
        restart()

    rms(X, 1e-6, lambda k: norms[:, k:k + 1])
    for k in range(KT):
        V("copy", X[:, k, :], U[:, k, :])
    join()
    if probe:
        probe("x1", X, A)
        join()
    pos = arena[:, 0:T]
    ang, turns, red = (arena[:, (1 + n) * T:(2 + n) * T] for n in range(3))
    nc.scalar.dma_start(pos.bitcast(i32), a_pos).then_inc(s_in, 16)
    nc.scalar.dma_start(cond[:, :], a_cond).then_inc(s_in, 16)
    for q in work:
        q.engine.wait_ge(s_in, 112)
    t = A("act", small[:, 0:8], cond[:, :], Sigmoid)
    V("tt", cond[:, :], cond[:, :], small[:, 0:8], MUL, after=(t,))
    V("copy", ang, pos.bitcast(i32))
    V("ts", ang, ang, c_("inv_freq"), None, MUL)
    V("ts", turns, ang, float(1 / (2 * np.pi)), ROUND, MUL, ADD)
    V("ts", turns, turns, ROUND, None, SUB)
    for part in TWO_PI:
        V("stt", ang, turns, -part, ang, MUL, ADD)
    V("ts", ang, ang, -3.1415925, 3.1415925, MAX, ALU.min)
    t = V.now()
    A("act", rope[:, T:2 * T], ang, Sin, after=(t,))
    t = A("act", red, ang, Sin, scale=0.5)
    V("ts", rope[:, T:2 * T], rope[:, T:2 * T], c_("sin_sign"), None, MUL, after=(t,))
    V("tt", red, red, red, MUL)
    V("ts", rope[:, 0:T], red, -2.0, 1.0, MUL, ADD)
    join()

    at_group = LAYERS * LAYER1_GROUPS
    ff_base = 0
    for layer2 in range(LAYERS):
        nc.scalar.dma_start(par2[:, :], a_par2[layer2]).then_inc(s_par, 16)
        for q in work:
            q.engine.wait_ge(s_par, 16 * (LAYERS + layer2 + 1))
        modulation(Stream(at_group), cond, mod)
        at_group += ADA_GROUPS
        rms(X, 1e-6, lambda k: mod[:, 8 + k:9 + k], lambda k: mod[:, k:k + 1])
        st = Stream(at_group)

        def units(P2, GV, RV):
            run(0, 4, P2[:, 0:4, :], stream=st)
            run_tokens(4, 4, GV, stream=st)
            run(8, 4, P2[:, 4:8, :], stream=st)
            run(12, 8, P2[:, 8:16, :], stream=st)
            run_tokens(20, 4, RV, stream=st)
            run(24, 4, P2[:, 16:20, :], stream=st)
            join()
        linear_attention(units, Space(), rope)
        if probe:
            probe(f"mix{layer2}", Y[:, 0:8, :], A)
        for k in range(KT):
            V("copy", U[:, k, :], Y[:, k, :])
        join()
        for dt in range(KT):
            tok = project(st, 28 + dt, dt, 0)
            V("stt", X[:, dt, :], psum[dt][:, 0:T], mod[:, 16 + dt:17 + dt], X[:, dt, :], MUL, ADD, after=(tok,))
        join()
        at_group += MIX2_GROUPS
        rms(X, 1e-6, lambda k: mod[:, 32 + k:33 + k], lambda k: mod[:, 24 + k:25 + k])
        gates, n_groups = None, FF_GROUPS
        if layer2 == 1:
            join()
            gates, n_groups = arena[:, 0:EXPERTS * T], MOE_GROUPS
            route(gates)
        feed_forward(at_group, n_groups, None, False, FF_GROUPS * layer2, 2 * FF_GROUPS * layer2,
                     (LAYERS + layer2) * FF_GROUPS, gates, lambda dt: mod[:, 40 + dt:41 + dt])
        at_group += n_groups
        if probe:
            probe(f"x2{layer2}", X, A)
    assert at_group == ALL_GROUPS
    V("copy", norms[:, :], final2[:, :])
    rms(X, 1e-6, lambda k: norms[:, k:k + 1])
    nc.scalar.wait_ge(*V.now())
    nc.scalar.dma_start(a_out.rearrange("k p t -> p k t"), U).then_inc(s_out, 16)
    nc.scalar.wait_ge(s_out, 16)
    es.close()


TWO_PI = (6.28125, 0.0019340515136718750, float(2 * np.pi - 6.28125 - 0.0019340515136718750))
ROUND = float(1.5 * 2 ** 23)


def columns(a):
    k, n = a.shape
    return a.reshape(k // P, P, n // P, P).transpose(2, 1, 0, 3).reshape(n // P, P, k)


def per_channel(a):
    return np.asarray(a).reshape(-1, P).T


def weight_groups(inp):
    out = np.zeros((ALL_GROUPS, P, SLOT), np.float32)
    at = 0

    def put(units):
        nonlocal at
        n = len(units) // GROUP
        out[at:at + n, :, :GROUP * UNIT] = np.stack(units).reshape(n, GROUP, P, UNIT).transpose(0, 2, 1, 3)            .reshape(n, P, GROUP * UNIT)
        at += n
    A_END, B_END = 1792, 1792 + 2048
    for l in range(LAYERS):
        w = inp["w_in"][l]
        b, c = w[:, A_END:B_END], w[:, B_END:B_END + 1092]
        low = np.concatenate([np.concatenate([inp["a_w_up"][l], inp["a_a_up"][l]], 0), inp["a_g_up"][l]], 1)
        ki = c[:, 1024:1088]
        units = [*columns(w[:, :A_END]), low, *columns(b), *columns(c[:, 0:640]), *columns(c[:, 768:1024]),
                 *columns(np.concatenate([ki, ki], 1)), *columns(c[:, 640:768]), *columns(w[:, B_END + 1092:]),
                 *inp["w_branch"][l].reshape(12, P, D), *columns(inp["w_o"][l])]
        put(units)
        gate, val = columns(inp["w_up"][l][:, :FF]), columns(inp["w_up"][l][:, FF:])
        down = inp["w_down"][l].reshape(FF_GROUPS, P, D)
        taps = np.concatenate([inp["conv_w"][l], inp["conv_b"][l][None]], 0).reshape(4, 2, FF_GROUPS, P)
        out[at:at + FF_GROUPS, :, GROUP * UNIT:] = taps.transpose(2, 3, 1, 0).reshape(FF_GROUPS, P, EXTRA)
        put([u for g in range(FF_GROUPS) for u in (gate[g], val[g], down[g])])
    for l in range(LAYERS):
        put([*columns(inp["ada_w_2"][l])])
        w = inp["w_in_2"][l]
        cut = lambda s, n: [*columns(w[:, s:s + n])]
        put([*cut(0, 512), *cut(512, 512), *cut(1024, 512), *cut(1552, 1024), *cut(2576, 512), *cut(3088, 512),
             *columns(inp["w_out_2"][l])])
        if l == 0:
            w1, w3 = columns(inp["ffn_w1_2"][0]), columns(inp["ffn_w3_2"][0])
            w2 = inp["ffn_w2_2"][0].reshape(FF_GROUPS, P, D)
        else:
            w1, w3 = (np.concatenate([columns(inp[n][0, e]) for e in range(EXPERTS)]) for n in ("moe_w1_2", "moe_w3_2"))
            w2 = inp["moe_w2_2"][0].reshape(MOE_GROUPS, P, D)
        put([u for g in range(len(w1)) for u in (w1[g], w3[g], w2[g])])
    assert at == ALL_GROUPS
    return out


def laid_out(inp):
    par1 = np.zeros((LAYERS, P, PAR1_COLS), np.float32)
    par2 = np.zeros((LAYERS, P, PAR2_COLS), np.float32)
    for l in range(LAYERS):
        put = lambda name, a: par1[l].__setitem__((slice(None), PAR1[name]), a)
        for name, key in (("norm_mix", "norm_mix_g"), ("mu", "a_mu"), ("w0", "a_w0"), ("a0", "a_a0"),
                          ("k_k", "a_k_k"), ("k_a", "a_k_a"), ("gn_g", "a_gn_g"), ("gn_b", "a_gn_b"),
                          ("b_gn_g", "b_gn_g"), ("norm_ffn", "norm_ffn_g")):
            put(name, per_channel(inp[key][l]))
        put("r_k", per_channel(inp["a_r_k"][l].reshape(-1)))
        put("lb_logits", np.concatenate([per_channel(inp["b_lb_logits"][j]) for j in range(LAYERS)], 1))
        put("lb_flag", float(l))
        put("w_idx", inp["w_in"][l][:, 4928:4932].reshape(KT, P, 4).transpose(1, 0, 2).reshape(P, 32))
        put = lambda name, a: par2[l].__setitem__((slice(None), PAR2[name]), a)
        for name, key in (("norm_mix", "norm_mix_g_2"), ("norm_ffn", "norm_ffn_g_2"), ("ada_b", "ada_b_2"),
                          ("b_alpha", "gla_b_alpha_2"), ("gla_g", "gla_norm_g_2"), ("ret_g", "ret_gn_g_2"),
                          ("ret_b", "ret_gn_b_2")):
            put(name, per_channel(inp[key][l]))
        put("w_ga", inp["w_in_2"][l][:, 1536:1552].reshape(KT, P, 16).transpose(1, 0, 2).reshape(P, 128))
        par2[l, 0:16, PAR2["w_alpha"]] = inp["gla_w_alpha_2"][l]
    return {
        "x": np.ascontiguousarray(inp["x"][0].T.reshape(KT, P, T)),
        "pos": np.ascontiguousarray(np.broadcast_to(inp["positions_2"], (P, T))),
        "cond": np.ascontiguousarray(per_channel(inp["c_2"][0])),
        "const": constants(),
        "par1": par1, "par2": par2,
        "router": np.ascontiguousarray(
            inp["router_w_2"][0].reshape(KT, P, EXPERTS).transpose(1, 0, 2).reshape(P, KT * EXPERTS)),
        "norms": np.ascontiguousarray(
            np.concatenate([per_channel(inp["norm_final_g"]), per_channel(inp["final_g_2"])], 1)),
        "weights": weight_groups(inp),
    }


def kernel(**inputs):
    import concourse.bacc as bacc
    from concourse import mybir
    from concourse.bass_utils import run_bass_kernel_spmd

    arrays = laid_out({k: np.asarray(v) for k, v in inputs.items()})
    nc = bacc.Bacc("TRN2", target_bir_lowering=False, num_devices=1)
    aps = {n: nc.dram_tensor(f"in_{n}", a.shape, mybir.dt.from_np(a.dtype), kind="ExternalInput").ap()
           for n, a in arrays.items()}
    out = nc.dram_tensor("out", (KT, P, T), mybir.dt.float32, kind="ExternalOutput").ap()
    build(nc, aps["x"], aps["pos"], aps["cond"], aps["const"], aps["par1"], aps["par2"], aps["router"],
          aps["norms"], aps["weights"], out)
    r = run_bass_kernel_spmd(nc, [{f"in_{n}": a for n, a in arrays.items()}], core_ids=[0])
    got = r.results[0]["out"]
    return np.ascontiguousarray(got.reshape(D, T).T[None])
```

```python
import numpy as np

P = 128
T = 256
D = 1024
KT = D // P
LAYERS = 2
CH = 64
NCH = T // CH
HALVES = T // P
FF, FFE, EXPERTS = 2816, 1408, 8
UNIT = KT * P
GROUP = 3
EXTRA = 8
SLOT = GROUP * UNIT + EXTRA
RING = 2
MIX1_GROUPS = 28
MIX2_GROUPS = 12
ADA_GROUPS = 16
MOD_UNITS = GROUP * ADA_GROUPS
MOD_FIRST = 12
LOW_UNIT = 14 + MOD_FIRST
GATES_B = 18
FF_GROUPS = FF // P
MOE_GROUPS = EXPERTS * FFE // P
LAYER1_GROUPS = MIX1_GROUPS + ADA_GROUPS + FF_GROUPS
ALL_GROUPS = LAYERS * (LAYER1_GROUPS + MIX2_GROUPS) + FF_GROUPS + MOE_GROUPS
TOPK = 64

PAR1 = {}
PAR2 = {}
CONST = {}


def _columns(table, sizes):
    at = 0
    for name, n in sizes:
        table[name] = slice(at, at + n)
        at += n
    return at


PAR1_COLS = _columns(PAR1, [
    ("norm_mix", 8), ("mu", 14), ("w0", 4), ("a0", 4), ("k_k", 4), ("k_a", 4), ("r_k", 4),
    ("gn_g", 4), ("gn_b", 4), ("b_gn_g", 4), ("norm_ffn", 8), ("lb_logits", 8), ("lb_flag", 1),
    ("w_idx", 32)])
PAR2_COLS = _columns(PAR2, [
    ("norm_mix", 8), ("norm_ffn", 8), ("ada_b", 48), ("b_alpha", 2), ("gla_g", 4),
    ("ret_g", 4), ("ret_b", 4), ("w_ga", 128), ("w_alpha", 256)])
CONST_COLS = _columns(CONST, [
    ("ident", 128), ("strict_up_neg", 128), ("strict_up", 128), ("incl_up", 128),
    ("strict_low", 128), ("low16_neg", 128), ("up16_neg", 128), ("low32_neg", 128),
    ("low64_neg", 128), ("pair_blocks", 128), ("pair_mean", 128), ("mean128", 128),
    ("ones", 128), ("level0", 128), ("level1", 128), ("level2", 128), ("level3", 128),
    ("level4", 128), ("level5", 128), ("level6", 128), ("swap32", 128), ("swap64", 128),
    ("dup0", 128), ("dup1", 128), ("rope_cos", T), ("rope_sin", T), ("chunk_mask", T),
    ("noncausal", 2 * T), ("ret_intra", 4 * P), ("ret_q", 4 * CH), ("ret_k", 4 * CH),
    ("ret_chunk", 4), ("inv_freq", 1), ("sin_sign", 1)])


def constants():
    c = np.zeros((P, CONST_COLS), np.float32)
    r, q = np.arange(P)[:, None], np.arange(P)[None, :]
    same = (r // CH) == (q // CH)
    put = lambda name, a: c.__setitem__((slice(None), CONST[name]), a)
    put("ident", r == q)
    put("strict_up", same & (r < q))
    put("strict_up_neg", -1.0 * (same & (r < q)))
    put("incl_up", same & (r <= q))
    put("strict_low", same & (r > q))
    put("low16_neg", -1.0 * ((r // 16 == q // 16) & (r > q)))
    put("up16_neg", -1.0 * ((r // 16 == q // 16) & (r < q)))
    put("low32_neg", -1.0 * ((r // 32 == q // 32) & (r // 16 > q // 16)))
    put("low64_neg", -1.0 * ((r // 64 == q // 64) & (r // 32 > q // 32)))
    put("pair_blocks", same)
    put("pair_mean", same / float(CH))
    put("mean128", 1.0 / P)
    put("ones", 1.0)
    for n in range(6):
        h = 32 >> n
        put(f"level{n}", (r // (2 * h) == q // (2 * h)) & (r % (2 * h) < h) & (q % (2 * h) >= h))
    put("level6", r == q)
    put("swap32", (r // 64 == q // 64) & ((r % 64 + 32) % 64 == q % 64))
    put("swap64", (r + 64) % 128 == q)
    put("dup0", r == q % 64)
    put("dup1", r == 64 + q % 64)
    inv = np.float32(10000.0) ** (-np.arange(32, dtype=np.float32) * np.float32(2.0 / 64))
    ang = (np.arange(T, dtype=np.float32)[None, :] * inv.astype(np.float32)[:, None]).astype(np.float32)
    rows = np.arange(P) % 32
    put("rope_cos", np.cos(ang.astype(np.float64))[rows])
    put("rope_sin", np.sin(ang.astype(np.float64))[rows] * np.where(np.arange(P) % 64 < 32, -1, 1)[:, None])
    put("chunk_mask", (np.arange(T) % CH != 0)[None, :])
    s = np.arange(T)[None, :]
    put("noncausal", np.concatenate([np.where(s <= r + P * a, 0.0, -1e30) for a in range(2)], 1))
    lg = np.log(1.0 - 2.0 ** (-5.0 - np.arange(4)))
    put("ret_intra", np.concatenate([np.where(same, np.exp(g * np.abs(r - q)), 0.0) for g in lg], 1))
    t = np.arange(CH)
    put("ret_q", np.concatenate([np.exp(g * (t + 1)) for g in lg])[None, :] * 128 ** -0.5)
    put("ret_k", np.concatenate([np.exp(g * (CH - 1 - t)) for g in lg])[None, :])
    put("ret_chunk", np.exp(lg * CH)[None, :])
    inv = np.float32(10000.0) ** (-np.arange(64, dtype=np.float32) / np.float32(64))
    put("inv_freq", inv[np.arange(P) % 64][:, None])
    put("sin_sign", np.where(np.arange(P) < 64, -1.0, 1.0)[:, None])
    return c


def build(nc, a_x, a_pos, a_cond, a_const, a_par1, a_par2, a_router, a_norms, a_weights, a_out, probe=None):
    import concourse.bass as bass
    from concourse import mybir
    from contextlib import ExitStack

    f32, i32, u32 = mybir.dt.float32, mybir.dt.int32, mybir.dt.uint32
    ALU, ACTF, AX = mybir.AluOpType, mybir.ActivationFunctionType, mybir.AxisListType
    MUL, ADD, SUB, MAX = ALU.mult, ALU.add, ALU.subtract, ALU.max
    Exp, Ln, Sigmoid, Tanh, Sqrt, Sin, Copy, Ident, Square, Abs = (
        ACTF.Exp, ACTF.Ln, ACTF.Sigmoid, ACTF.Tanh, ACTF.Sqrt, ACTF.Sin, ACTF.Copy,
        ACTF.Identity, ACTF.Square, ACTF.Abs)
    es = ExitStack()

    class Queue:

        def __init__(self, engine, name, chained):
            self.engine, self.sem, self.count, self.chained = engine, sem(name), 0, chained
            self.passed, self.tail = {}, None

        def wait(self, *tokens):
            for s, v in tokens:
                if isinstance(v, int):
                    if self.passed.get(id(s), 0) >= v:
                        continue
                    self.passed[id(s)] = v
                self.engine.wait_ge(s, v)

        def now(self):
            return self.tail or (self.sem, self.count)

        def __call__(self, op, *args, after=(), signal=True, raises=None, **kw):
            self.wait(*[x for x in after if x is not None])
            if self.chained and (self.count or self.tail):
                self.wait(self.now())
            ins = issue(self.engine, op)(*args, **kw)
            if raises is not None:
                self.tail = raises
                ins.then_inc(raises[0], 1)
            elif signal:
                self.tail = None
                self.count += 1
                ins.then_inc(self.sem, 1)
            return self.now()

    def issue(engine, op):
        return {
            "tt": lambda *a, **k: engine.tensor_tensor(*a, **k),
            "ts": lambda *a, **k: engine.tensor_scalar(*a, **k),
            "stt": lambda *a, **k: engine.scalar_tensor_tensor(*a, **k),
            "scan": lambda *a, **k: engine.tensor_tensor_scan(*a, **k),
            "copy": lambda *a, **k: engine.tensor_copy(*a, **k),
            "recip": lambda *a, **k: engine.reciprocal(*a, **k),
            "memset": lambda *a, **k: engine.memset(*a, **k),
            "rmax": lambda *a, **k: engine.reduce_max(*a, **k),
            "max8": lambda *a, **k: engine.max(*a, **k),
            "maxidx": lambda *a, **k: engine.max_index(*a, **k),
            "replace": lambda *a, **k: engine.match_replace(*a, **k),
            "act": lambda *a, **k: engine.activation(*a, **k),
            "mm": lambda *a, **k: engine.matmul(*a, **k),
            "tr": lambda *a, **k: engine.transpose(*a, **k),
        }[op]

    def sem(name):
        return es.enter_context(nc.semaphore(name))

    def sb(name, cols, dt=f32):
        return es.enter_context(nc.sbuf_tensor(name, [P, cols], dt))

    ring = sb("ring", RING * SLOT)
    f32r = mybir.dt.float32r
    UH = sb("u_high", KT * T, f32r)[:, :].rearrange("p (k t) -> p k t", t=T)
    UL = sb("u_low", KT * T, f32r)[:, :].rearrange("p (k t) -> p k t", t=T)
    const = sb("const", CONST_COLS)
    par1 = sb("par1", PAR1_COLS)
    par2 = sb("par2", PAR2_COLS)
    norms = sb("norms", KT)
    final2 = sb("final2", KT)
    rope = sb("rope", 2 * T)[:, :]
    extra = sb("taps", 2 * EXTRA)
    mod = sb("mod", MOD_UNITS)[:, :]
    raw_mod = sb("raw_mod", LAYERS * MOD_UNITS)[:, :]
    cond = sb("cond", KT)[:, :]
    router = sb("router", KT * EXPERTS)
    x_sb = sb("x_res", KT * T)
    rstd = sb("rstd", T)
    small = sb("small", 512)
    y_sb = sb("y_mix", 12 * T)
    arena_base = nc.sbuf_base
    arena_cols = nc.sbuf_bytes_remaining // 4 - 64
    arena = sb("arena", arena_cols)

    def over_arena(name, col, cols):
        assert col + cols <= arena_cols
        t = nc.alloc_sbuf_tensor_at(name, [P, cols], f32r, offset=arena_base + 4 * col)
        return t[:, :]

    SPLIT = 2 * GROUP
    split_at = arena_cols - 2 * SPLIT * UNIT
    WH = over_arena("w_high", split_at, SPLIT * UNIT).rearrange("p (b n) -> p b n", n=UNIT)
    WL = over_arena("w_low", split_at + SPLIT * UNIT, SPLIT * UNIT).rearrange("p (b n) -> p b n", n=UNIT)
    y_at = 0
    YH = over_arena("y_high", y_at, 12 * T).rearrange("p (k t) -> p k t", t=T)
    YL = over_arena("y_low", y_at + 12 * T, 12 * T).rearrange("p (k t) -> p k t", t=T)
    hid_at = 24 * T
    HH = over_arena("hid_high", hid_at, 3 * T)
    HL = over_arena("hid_low", hid_at + 3 * T, 3 * T)
    psum = [es.enter_context(nc.psum_tensor(f"bank{b}", [P, 512], f32)) for b in range(8)]

    X = x_sb[:, :].rearrange("p (k t) -> p k t", t=T)
    Y = y_sb[:, :].rearrange("p (k t) -> p k t", t=T)

    def c_(name):
        return const[:, CONST[name]]

    def p1(name, j=None):
        s = PAR1[name]
        return par1[:, s] if j is None else par1[:, s.start + j:s.start + j + 1]

    def p2(name, j=None):
        s = PAR2[name]
        return par2[:, s] if j is None else par2[:, s.start + j:s.start + j + 1]

    class Space:

        def __init__(self, start=0):
            self.at = start

        def __call__(self, cols):
            self.at += cols
            assert self.at <= arena_cols, (self.at, arena_cols)
            return arena[:, self.at - cols:self.at]

    PE = Queue(nc.tensor, "s_pe", False)
    V = Queue(nc.vector, "s_dve", True)
    A = Queue(nc.scalar, "s_act", True)
    work = [PE, V, A]
    s_slot = [sem(f"s_slot{k}") for k in range(RING)]
    s_done = sem("s_group_done")
    s_in = sem("s_inputs")
    s_par = sem("s_params")
    s_out = sem("s_out")
    s_up = sem("s_ff_up")
    s_down = sem("s_ff_down")
    ff_sems = {conv: tuple(sem(f"s_ff_{who}_{kind}") for who in ("act", "dve", "cut_act", "cut_dve"))
               for conv, kind in ((True, "conv"), (False, "plain"))}

    free = [()] * 8
    last_done = [None]

    def join():
        marks = [m for m in last_done if m] + [q.now() for q in work if q.count]
        for q in work:
            q.wait(*[m for m in marks])
        for b in range(8):
            free[b] = ()
        for b in range(SPLIT):
            read_by[b] = None

    def restart():
        join()
        A("act", small[:, 0:1], small[:, 0:1], Copy)
        join_engines = [q.engine.engine for q in work]
        nc.multi_engine_barrier(join_engines)
        for q in work:
            q.engine.sem_clear(q.sem)
        nc.multi_engine_barrier(join_engines)
        for q in work:
            q.count, q.passed, q.tail = 0, {}, None
        for b in range(8):
            free[b] = ()

    def weight_stream():
        def load(g, slot):
            nc.sync.dma_start(ring[:, slot * SLOT:(slot + 1) * SLOT],
                              a_weights[bass.ds(g, 1), :, :].rearrange("o p n -> p (o n)"))\
                .then_inc(s_slot[slot], 16)
        for g in range(RING):
            load(g, g)
        with nc.sync.Fori(0, (ALL_GROUPS - RING) // RING) as i:
            for j in range(RING):
                nc.sync.wait_ge(s_done, i * RING + (j + 1))
                load(i * RING + (RING + j), j)
        for g in range(ALL_GROUPS - (ALL_GROUPS - RING) % RING, ALL_GROUPS):
            nc.sync.wait_ge(s_done, g - RING + 1)
            load(g, g % RING)

    class Stream:

        def __init__(self, group0, layer=None):
            self.group0, self.layer, self.split_to = group0, layer, 0

        def scaled(self, per_layer, n):
            return n if self.layer is None else self.layer * per_layer + n

        def arrived(self, g):
            n = (self.group0 + g) // RING + 1
            slot = (self.group0 + g) % RING
            return (s_slot[slot], self.scaled(16 * (LAYER1_GROUPS // RING), 16 * n))

        def weights(self, u):
            g = u // GROUP
            at = ((self.group0 + g) % RING) * SLOT + (u % GROUP) * UNIT
            return ring[:, at:at + UNIT]

        def extra(self, g):
            at = ((self.group0 + g) % RING) * SLOT + GROUP * UNIT
            return ring[:, at:at + EXTRA]

        def done(self, g):
            return (s_done, self.scaled(LAYER1_GROUPS, self.group0 + g + 1))

    ready = {}

    def need(queue, st, u):
        g = u // GROUP
        if ready.get((id(queue), id(st))) != g:
            queue.wait(st.arrived(g))
            ready[id(queue), id(st)] = g

    read_by = [None] * SPLIT
    parts_ready = {}

    def split(st, u, end):
        for v in range(st.split_to, min(u + 1, end)):
            b = v % SPLIT
            w = st.weights(v)
            need(A, st, v)
            t = A("act", WH[:, b, :], w, Copy, after=(read_by[b],))
            need(V, st, v)
            closes = v % GROUP == GROUP - 1
            t = V("tt", WL[:, b, :], w, WH[:, b, :].bitcast(f32), SUB, after=(t, read_by[b]),
                  raises=st.done(v // GROUP) if closes else None)
            if closes:
                last_done[0] = t
            parts_ready[id(st), v] = t
            st.split_to = v + 1

    AHEAD = 4

    def mm(out, lhsT, rhs, start, stop, after=(), signal=False, loose=False):
        return PE("mm", out, lhsT, rhs, start=start, stop=stop, after=after, signal=signal,
                  skip_group_check=loose)

    def mm3(out, a, b, start, stop, signal=False, loose=False):
        (ah, al), (bh, bl) = a, b
        mm(out, ah, bh, start, False, loose=loose)
        mm(out, ah, bl, False, False, loose=loose)
        return mm(out, al, bh, False, stop, signal=signal, loose=loose)

    def last_mm(st, u, out, lhsT, rhs, start, stop, loose=False):
        if u % GROUP == GROUP - 1:
            nc.tensor.matmul(out, lhsT, rhs, start=start, stop=stop, skip_group_check=loose)\
                .then_inc(s_done, 1)
            last_done[0] = st.done(u // GROUP)
            return last_done[0]
        return mm(out, lhsT, rhs, start, stop, signal=True, loose=loose)

    def parts(st, u, cols):
        b = u % SPLIT
        return (WH[:, b, cols], WL[:, b, cols])

    def project(st, u, end, bank, half):
        split(st, u + AHEAD, end)
        PE.wait(parts_ready[id(st), u])
        out = psum[bank][:, half * T:(half + 1) * T]
        for k in range(KT):
            tok = mm3(out, parts(st, u, slice(k * P, (k + 1) * P)), (UH[:, k, :], UL[:, k, :]),
                      k == 0, k == KT - 1, signal=k == KT - 1)
        read_by[u % SPLIT] = tok
        return tok

    def project_tokens(st, u, end, bank, col):
        split(st, u + AHEAD, end)
        PE.wait(parts_ready[id(st), u])
        for a in range(HALVES):
            out = psum[bank][:, col + a * P:col + (a + 1) * P]
            ts_ = slice(a * P, (a + 1) * P)
            for k in range(KT):
                tok = mm3(out, (UH[:, k, ts_], UL[:, k, ts_]), parts(st, u, slice(k * P, (k + 1) * P)),
                          k == 0, k == KT - 1, signal=k == KT - 1 and a == HALVES - 1)
        read_by[u % SPLIT] = tok
        return tok

    def mm_u(out, k, other, cols, start, stop, signal, u_first):
        for n, part in enumerate((UH, UL)):
            x = part[:, k, cols].bitcast(f32)
            lt, r_ = (x, other) if u_first else (other, x)
            tok = mm(out, lt, r_, start and n == 0, stop and n == 1, signal=signal and n == 1)
        return tok

    turn = [0]

    def copy_out(out, src, after):
        turn[0] += 1
        if turn[0] % 2:
            return A("act", out, src, Copy, after=after)
        return V("copy", out, src, after=after)

    class Beside:

        def __init__(self, st, end, banks):
            self.st, self.end, self.banks, self.jobs, self.made, self.held = st, end, banks, [], 0, []

        def add(self, u0, n, dst, act=None):
            for j in range(0, n, 2):
                self.jobs.append((u0 + j, dst[:, j:j + 2, :].rearrange("p k t -> p (k t)"), act))

        def add_tokens(self, u0, n, dst):
            for j in range(0, n, 2):
                self.jobs.append((u0 + j, dst[:, :, j * P:(j + 2) * P].rearrange("p a (j c) -> p j a c", c=P), None))

        def clear(self):
            for bank, dst, act, tok in self.held:
                src = psum[bank][:, :]
                if len(dst.shape) == 4:
                    src = src.rearrange("p (j a c) -> p j a c", j=2, a=2)
                free[bank] = (copy_out(dst, src, (tok,)) if act is None else A("act", dst, src, act, after=(tok,)),)
            self.held = []

        def __call__(self, n):
            self.clear()
            for _ in range(min(n, len(self.jobs))):
                u, dst, act = self.jobs.pop(0)
                bank = self.banks[self.made % len(self.banks)]
                if bank in [h[0] for h in self.held]:
                    self.clear()
                PE.wait(*free[bank])
                for h in range(2):
                    if len(dst.shape) == 4:
                        tok = project_tokens(self.st, u + h, self.end, bank, h * T)
                    else:
                        tok = project(self.st, u + h, self.end, bank, h)
                self.held.append((bank, dst, act, tok))
                self.made += 1

        def finish(self):
            self(len(self.jobs))
            self.clear()

    def split_u(src, after):
        for h in range(2):
            ks = slice(4 * h, 4 * h + 4)
            t = A("act", UH[:, ks, :], src[:, ks, :], Copy, after=after)
            V("tt", UL[:, ks, :], src[:, ks, :], UH[:, ks, :].bitcast(f32), SUB, after=(t,))

    def rms(src, eps, g_of, add_of=None, out=None):
        sq = arena[:, 0:KT * T].rearrange("p (k t) -> p k t", t=T)
        un = out if out is not None else arena[:, KT * T:2 * KT * T].rearrange("p (k t) -> p k t", t=T)
        t0 = A("act", sq[:, 0:4, :], src[:, 0:4, :], Square, after=(V.now(),))
        t1 = A("act", sq[:, 4:8, :], src[:, 4:8, :], Square)
        for k in range(KT):
            tok = mm(psum[0][:, 0:T], c_("ones"), sq[:, k, :], k == 0, k == KT - 1,
                     after=(t0 if k < 4 else t1,), signal=k == KT - 1)
        t = V("ts", rstd[:, :], psum[0][:, 0:T], 1.0 / D, eps, MUL, ADD, after=(tok,))
        t = A("act", rstd[:, :], rstd[:, :], Sqrt, after=(t,))
        V("recip", rstd[:, :], rstd[:, :], after=(t,))
        for k in range(KT):
            t = V("stt", un[:, k, :], src[:, k, :], g_of(k), rstd[:, :], MUL, MUL)
            if add_of is not None:
                t = A("act", un[:, k, :], un[:, k, :], Ident, bias=add_of(k), after=(t,))
        if out is None:
            split_u(un, (t,))
        PE.wait(V.now(), A.now())

    FILL = (8, 3, 8, 2, 2, 3, 3)
    FILL_B = (2, 2, 1, 1, 1, 1, 1, 0, 0)
    FILL_C = (1, 1, 1)
    FILL_G = (2, 3, 1, 1, 1)

    def branch_a(PA, st, beside):
        S = Space(14 * T)
        t4 = lambda ap: ap.rearrange("p (k t) -> p k t", t=T)
        Dif = t4(S(14 * T))
        V("tt", Dif[:, :, 1:T], PA[:, :, 0:T - 1], PA[:, :, 1:T], SUB)
        V("ts", Dif[:, :, 0:1], PA[:, :, 0:1], -1.0, None, MUL)
        for k in range(14):
            V("stt", PA[:, k, :], Dif[:, k, :], p1("mu", k), PA[:, k, :], MUL, ADD)
        beside(MOD_FIRST)
        mixed = V.now()
        S = Space(14 * T)
        R, K, VT, WA, GD = PA[:, 0:4, :], PA[:, 4:8, :], PA[:, 8:12, :], PA[:, 12, :], PA[:, 13, :]
        g_t, a_t, lw = t4(S(4 * T)), t4(S(4 * T)), t4(S(4 * T))
        kk, cw = t4(S(4 * T)), t4(S(4 * T))
        tmp = t4(Space(S.at)(4 * T))
        A("act", WA[0:64, :], WA[0:64, :], Tanh, after=(mixed,))
        low = A("act", GD[:, :], GD[:, :], Sigmoid)
        lora = st.weights(LOW_UNIT)
        need(PE, st, LOW_UNIT)
        w_up = lora[0:64, 0:512]
        a_up = lora[64:128, 0:512]
        g_up = lora[:, 512:1024]
        for m in range(4):
            b = m // 2
            o = slice((m % 2) * T, (m % 2 + 1) * T)
            cs = slice(m * P, (m + 1) * P)
            mm(psum[b][:, o], w_up[:, cs], WA[0:64, :], True, True, after=(low,))
            mm(psum[2 + b][:, o], a_up[:, cs], WA[64:128, :], True, True)
            if m < 3:
                mm(psum[4 + b][:, o], g_up[:, cs], GD, True, True)
            else:
                nc.tensor.matmul(psum[4 + b][:, o], g_up[:, cs], GD, start=True, stop=True)\
                    .then_inc(s_done, 1)
                up = last_done[0] = st.done(LOW_UNIT // GROUP)
        beside(FILL[0])
        for m in range(4):
            o = slice((m % 2) * T, (m % 2 + 1) * T)
            A("act", lw[:, m, :], psum[m // 2][:, o], Sigmoid, bias=p1("w0", m), after=(up,))
            A("act", a_t[:, m, :], psum[2 + m // 2][:, o], Sigmoid, bias=p1("a0", m))
            if m % 2:
                A("act", g_t[:, m - 1:m + 1, :].rearrange("p k t -> p (k t)"), psum[4 + m // 2][:, :], Copy)
        sig = A.now()
        V("ts", lw, lw, -float(np.exp(-0.5)), None, MUL, after=(sig,))
        for m in range(4):
            V("scan", cw[:, m, :], c_("chunk_mask"), lw[:, m, :], 0.0, MUL, ADD)
        for m in range(4):
            V("ts", kk[:, m, :], K[:, m, :], p1("k_k", m), None, MUL)
        t = V("tt", tmp, kk, kk, MUL)
        for m in range(4):
            tok = mm(psum[(6, 0)[m // 2]][:, (m % 2) * T:(m % 2 + 1) * T], c_("pair_blocks"), tmp[:, m, :],
                     True, True, after=(t,), signal=True)
        beside(FILL[1])
        for b in range(2):
            V("ts", tmp[:, 2 * b:2 * b + 2, :].rearrange("p k t -> p (k t)"), psum[(6, 0)[b]][:, :],
              1e-24, None, MAX, after=(tok,))
        t = A("act", tmp, tmp, Sqrt, after=(V.now(),))
        V("recip", tmp, tmp, after=(t,))
        V("tt", kk, kk, tmp, MUL)
        omka = small[:, 0:4]
        V("ts", omka, p1("k_a"), -1.0, 1.0, MUL, ADD)
        for m in range(4):
            V("ts", tmp[:, m, :], a_t[:, m, :], p1("k_a", m), omka[:, m:m + 1], MUL, ADD)
        V("tt", K, K, tmp, MUL)
        for m in range(4):
            V("stt", tmp[:, m, :], R[:, m, :], p1("r_k", m), K[:, m, :], MUL, MUL)
        t = V.now()
        for m in range(4):
            tok = mm(psum[m // 2][:, (m % 2) * T:(m % 2 + 1) * T], c_("pair_blocks"), tmp[:, m, :],
                     True, True, after=(t, sig), signal=True)
        beside(FILL[2])
        e = A("act", tmp, cw, Exp, scale=-1.0, after=(tok, V.now()))
        V("tt", a_t, a_t, kk, MUL)
        V("tt", a_t, a_t, tmp, MUL, after=(e,))
        V("tt", K, K, tmp, MUL)
        t = V("tt", lw, cw, lw, SUB)
        e = A("act", lw, lw, Exp, after=(t,))
        V("tt", kk, kk, lw, MUL, after=(e,))
        e = A("act", cw, cw, Exp, after=(V.now(),))
        V("tt", R, R, cw, MUL, after=(e,))
        bonus = lw
        for b in range(2):
            V("tt", bonus[:, 2 * b:2 * b + 2, :], psum[b][:, :].rearrange("p (k t) -> p k t", t=T),
              VT[:, 2 * b:2 * b + 2, :], MUL)
        at, bt, kt, rt, Dc = kk, a_t, K, R, cw
        join()
        S2 = S
        beside.out()
        tokm = []
        for n, src in enumerate((bt, kt, VT)):
            dst = S2(2 * 512).rearrange("p (a c) -> p a c", a=2)
            for a in range(2):
                b = 2 * n + a
                for m in range(4):
                    tok = PE("tr", psum[b][:, m * P:(m + 1) * P], src[:, m, a * P:(a + 1) * P],
                             c_("ident"), signal=m == 3)
                free[b] = (copy_out(dst[:, a, :], psum[b][:, :], (tok,)),)
            tokm.append(dst)
        BT, KTk, VTk = tokm
        join()
        h8 = lambda ap: ap.rearrange("p (h c) -> p h c", c=P)
        TT = [h8(S2(1024)) for _ in range(2)]
        RB = [h8(S2(1024)) for _ in range(2)]
        keep = S2.at
        RK = h8(S2(1024))
        AK = h8(Y[:, 4:8, :].rearrange("p k t -> p (k t)"))
        AKV = [Y[:, 8 + 2 * a:10 + 2 * a, :].rearrange("p k t -> p (k t)") for a in range(2)]
        names = ("N16", "NT16", "M32", "M64", "N2", "N2T", "Pm")
        spare = {n: PA[:, 8 + 2 * j:10 + 2 * j, :].rearrange("p k t -> p (k t)")
                 for j, n in enumerate(("M32", "M64", "Pm"))}
        tmps = [{n: (spare[n] if par and n in spare else S2(512)).rearrange("p (h c) -> p h c", c=P)
                 for n in names} for par in range(2)]
        for w in tmps:
            w["N4"], w["N4T"], w["N8"] = w["N16"], w["NT16"], w["N2T"]
            w["Tm"], w["Z"] = w["N16"], w["NT16"]

        def gram(bank, lt, rt_, par, a, after=()):
            rows = slice(64 * par, 64 * par + 64)
            cs = slice(a * P, (a + 1) * P)
            for m in range(4):
                tok = mm(psum[bank][:, m * P:(m + 1) * P], lt[rows, m, cs], rt_[rows, m, cs], True, True,
                         after=tuple(after) + tuple(free[bank]), signal=m == 3)
            return tok

        def b4(name):
            return c_(name).rearrange("p (o c) -> p o c", o=1).to_broadcast([P, 4, P])

        def ps4(bank):
            return psum[bank][:, :].rearrange("p (h c) -> p h c", c=P)

        beside(8)
        for a in range(2):
            made = {}
            used = {}
            bank = 0
            for lt, r_, outs in (
                    (bt, at, (("NT16", "up16_neg"),)),
                    (at, bt, (("N16", "low16_neg"), ("M32", "low32_neg"), ("M64", "low64_neg"))),
                    (kt, at, (("AK", "strict_up"),)),
                    (bt, rt, (("RB", "incl_up"),)),
                    (kt, rt, (("RK", "incl_up"),))):
                for par in range(2):
                    tok = gram(bank, lt, r_, par, a)
                    for dst, mask in outs:
                        whole = {"AK": AK, "RB": RB[a], "RK": RK}.get(dst)
                        o = tmps[par][dst] if whole is None else whole[:, par:8:2, :]
                        t = made[par, dst] = V("tt", o, ps4(bank), b4(mask), MUL, after=(tok,))
                    free[bank] = (t,)
                    bank = (bank + 1) % 7
                    if dst == "NT16":
                        made[par, "Pm"] = V("tt", tmps[par]["Pm"], tmps[par]["NT16"], b4("ident"), ADD)

            def product(par, slot, lt, r_, out, add=None, over=()):
                w = tmps[par]
                bank = 4 * par + slot
                need_ = (made[par, lt], made[par, r_]) + tuple(free[bank])
                for m in range(4):
                    tok = mm(psum[bank][:, m * P:(m + 1) * P], w[lt][:, m, :], w[r_][:, m, :], True, True,
                             after=need_, signal=m == 3)
                used[par, lt] = used[par, r_] = tok
                o = w[out] if isinstance(out, str) else out
                after = (tok,) + tuple(used[par, n] for n in over if (par, n) in used)
                if add is None:
                    t = A("act", o, ps4(bank), Copy, after=after)
                else:
                    t = V("tt", o, ps4(bank), w[add], ADD, after=after)
                free[bank] = (t,)
                made[par, out if isinstance(out, str) else "TT"] = t

            def turned(par, slot, src, out, over=()):
                w = tmps[par]
                bank = 4 * par + slot
                for m in range(4):
                    tok = PE("tr", psum[bank][:, m * P:(m + 1) * P], w[src][:, m, :], c_("ident"),
                             after=(made[par, src],) + tuple(free[bank]), signal=m == 3)
                used[par, src] = tok
                after = (tok,) + tuple(used[par, n] for n in over if (par, n) in used)
                made[par, out] = A("act", w[out], ps4(bank), Copy, after=after)
                free[bank] = (made[par, out],)

            both = range(2)
            for par in both:
                product(par, 0, "NT16", "N16", "N2")
                product(par, 1, "N16", "NT16", "N2T")
            for par in both:
                product(par, 0, "N2T", "N2", "N4", over=("N16",))
                product(par, 1, "N2", "N2T", "N4T", over=("NT16", "N16"))
            for par in both:
                product(par, 2, "N2", "Pm", "Pm", add="Pm", over=("Pm",))
                product(par, 0, "N4T", "N4", "N8", over=("N2T", "N2"))
            for par in both:
                product(par, 2, "N4", "Pm", "Pm", add="Pm", over=("Pm",))
            for par in both:
                product(par, 2, "N8", "Pm", "Pm", add="Pm", over=("Pm",))
            for m_, dst in (("M32", "Pm"), ("M64", TT[a][:, :, :])):
                for par in both:
                    turned(par, 0, "Pm", "Tm", over=("N4", "Tm"))
                    product(par, 1, m_, "Pm", "Z", over=("N4T", "Z"))
                for par in both:
                    product(par, 2, "Tm", "Z", dst if isinstance(dst, str) else dst[:, par:8:2, :], add="Pm",
                            over=("Pm",))
            for h in range(8):
                tok = mm(psum[3][:, h * 64:(h + 1) * 64], AK[:, h, :], VTk[:, a, h * 64:(h + 1) * 64],
                         True, True, after=(V.now(),) + tuple(free[3]), signal=h == 7)
            free[3] = (A("act", AKV[a], psum[3][:, :], Copy, after=(tok,)),)
            for h in range(8):
                tok = mm(psum[3][64 * (h % 2):64 * (h % 2) + 64, (h // 2) * P:(h // 2 + 1) * P],
                         VTk[:, a, h * 64:(h + 1) * 64], RK[:, h, :], True, True,
                         after=(V.now(),) + tuple(free[3]), signal=h == 7)
            free[3] = (A("act", Y[:, 0:4, a * P:(a + 1) * P], ps4(3), Copy, after=(tok,)),)
            beside.out()
            beside(0)
            V.wait(PE.now())
            A.wait(PE.now())
        join()
        S4 = Space(keep)
        state = S4(512).rearrange("p (m c) -> p m c", c=P)
        Wv = S4(512)
        Uv = S4(512)
        sd = S4(512).rearrange("p (m c) -> p m c", c=P)
        V("memset", state, 0.0)
        V("memset", Wv, 0.0)
        ycols = Y[:, 0:4, :]
        for c in range(NCH):
            a, par = c // 2, c % 2
            rows = slice(64 * par, 64 * par + 64)
            tcs = slice(c * CH, (c + 1) * CH)
            loc = slice(64 * par, 64 * par + 64)
            for m in range(4):
                tok = mm(psum[0][:, m * P:(m + 1) * P], at[:, m, a * P:(a + 1) * P], state[:, m, :],
                         True, True, after=(V.now(), A.now()), signal=m == 3)
            t = V("tt", Wv[rows, :], psum[0][rows, :], AKV[a][rows, :], ADD, after=(tok,))
            for h in range(8):
                tok = mm(psum[1][:, h * 64:(h + 1) * 64], TT[a][:, h, :], Wv[:, h * 64:(h + 1) * 64],
                         True, True, after=(t, A.now()), signal=h == 7)
            beside(FILL[3])
            tu = A("act", Uv, psum[1][:, :], Copy, scale=-1.0, after=(tok,))
            for m in range(4):
                o = psum[2][:, m * CH:(m + 1) * CH]
                mm(o, state[:, m, :], rt[:, m, tcs], True, False, after=(tu,) if m == 0 else (), loose=True)
                for hp in range(2):
                    h = 2 * m + hp
                    oh = psum[2][64 * hp:64 * hp + 64, m * CH:(m + 1) * CH]
                    tok = mm(oh, Uv[:, h * 64:(h + 1) * 64], RB[a][:, h, loc], False, True, loose=True,
                             signal=m == 3 and hp == 1)
            beside.out()
            V("tt", ycols[:, :, tcs], psum[2][:, 0:4 * CH].rearrange("p (m t) -> p m t", t=CH),
              ycols[:, :, tcs], ADD, after=(tok,))
            if c < NCH - 1:
                for m in range(4):
                    o = psum[3][:, m * P:(m + 1) * P]
                    cs = slice(m * P, (m + 1) * P)
                    mm(o, BT[rows, a, cs], Uv[rows, cs], True, False)
                    tok = mm(o, KTk[rows, a, cs], VTk[rows, a, cs], False, True, signal=m == 3)
                beside(FILL[4])
                V("tt", sd, ps4(3), b4("pair_blocks"), MUL, after=(tok,))
                V("tt", sd, sd, state, ADD)
                end = (c + 1) * CH - 1
                V("tt", state, sd, Dc[:, :, end:end + 1].to_broadcast([P, 4, P]), MUL)
        S5 = Space(S4.at)
        q = t4(S5(4 * T))
        t = V.now()

        def head_mean(src, after):
            for m in range(4):
                tok = mm(psum[4 + m // 2][:, (m % 2) * T:(m % 2 + 1) * T], c_("pair_mean"), src[:, m, :],
                         True, True, after=after, signal=True)
            return tok
        tok = head_mean(ycols, (t,))
        beside(FILL[5])
        for b in range(2):
            V("tt", ycols[:, 2 * b:2 * b + 2, :], ycols[:, 2 * b:2 * b + 2, :],
              psum[4 + b][:, :].rearrange("p (k t) -> p k t", t=T), SUB, after=(tok,))
        t = V("tt", q, ycols, ycols, MUL)
        tok = head_mean(q, (t,))
        beside(FILL[6])
        for b in range(2):
            V("ts", q[:, 2 * b:2 * b + 2, :].rearrange("p k t -> p (k t)"), psum[4 + b][:, :], 64e-5, None,
              ADD, after=(tok,))
        t = A("act", q, q, Sqrt, after=(V.now(),))
        V("recip", q, q, after=(t,))
        V("tt", ycols, ycols, q, MUL)
        for m in range(4):
            V("ts", ycols[:, m, :], ycols[:, m, :], p1("gn_g", m), p1("gn_b", m), MUL, ADD)
        V("tt", ycols, ycols, bonus, ADD)
        V("tt", ycols, ycols, g_t, MUL)
        join()

    def branch_b(PB, VB, S, beside):
        t4 = lambda ap: ap.rearrange("p (k t) -> p k t", t=T)
        Q, F, Gt = PB[:, 0:4, :], PB[:, 4:8, :], PB[:, 8:12, :]
        mx, e0, e1, lb, lnlb, omlb, flg = (small[:, 8 + 4 * n:12 + 4 * n] for n in range(7))
        lg = p1("lb_logits")
        beside(FILL_B[0])
        V("tt", mx, lg[:, 0:4], lg[:, 4:8], MAX)
        V("tt", e0, lg[:, 0:4], mx, SUB)
        t = V("tt", e1, lg[:, 4:8], mx, SUB)
        A("act", e0, e0, Exp, after=(t,))
        t = A("act", e1, e1, Exp)
        V("tt", e0, e0, e1, ADD, after=(t,))
        V("recip", e0, e0)
        V("tt", lb, e1, e0, MUL)
        V("ts", lb, lb, p1("lb_flag"), None, MUL)
        V("ts", omlb, lb, -1.0, 1.0, MUL, ADD)
        V("ts", flg, lb, 2.0 ** -63, None, ALU.is_ge)
        V("ts", flg, flg, 1.0, 1e30, SUB, MUL)
        t = V("ts", lnlb, lb, 2.0 ** -63, None, MAX)
        t = A("act", lnlb, lnlb, Ln, after=(t,))
        V("tt", lnlb, lnlb, flg, ADD, after=(t,))
        s1, s2, s3, kin, bcum = (t4(S(4 * T)) for _ in range(5))
        A("act", s1, F, Abs, after=(V.now(),))
        t = A("act", s1, s1, Exp, scale=-1.0)
        t = A("act", s1, s1, Ln, bias=1.0)
        t = V("stt", kin, F, 0.0, s1, MAX, ADD, after=(t,))
        t = A("act", kin, kin, Exp, scale=-1.0, after=(t,))
        for m in range(4):
            V("ts", kin[:, m, :], kin[:, m, :], omlb[:, m:m + 1], None, MUL, after=(t,))
        t = V("ts", s2, F, -43.0, None, MAX)
        t = A("act", s2, s2, Exp, scale=-1.0, after=(t,))
        for m in range(4):
            t = A("act", s2[:, m, :], s2[:, m, :], Ln, bias=1.0, scale=lb[:, m:m + 1])
        V("stt", s3, F, 0.0, s1, ALU.min, SUB)
        V("tt", s3, s3, s2, ADD, after=(t,))
        for m in range(4):
            V("ts", s3[:, m, :], s3[:, m, :], lnlb[:, m:m + 1], None, MAX)
        beside(FILL_B[1])
        for m in range(4):
            V("scan", bcum[:, m, :], c_("chunk_mask"), s3[:, m, :], 0.0, MUL, ADD)
        sc = S(1024).rearrange("p (g c) -> p g c", c=P)
        tmp8 = S(1024).rearrange("p (g c) -> p g c", c=P)
        Xl = s1, s2
        for n in range(7):
            x = Xl[n % 2]
            if n < 6:
                h = 32 >> n
                split = lambda ap: ap.rearrange("p k (b s) -> p (k b) s", s=2 * h)
                xs, bs, qs, ks = split(x), split(bcum), split(Q), split(kin)
                ref = bs[:, :, h - 1:h].to_broadcast([P, 4 * T // (2 * h), h])
                V("tt", xs[:, :, 0:h], ref, bs[:, :, 0:h], SUB, after=(PE.now(),))
                t = V("tt", xs[:, :, h:2 * h], bs[:, :, h:2 * h], ref, SUB)
                t = A("act", x, x, Exp, after=(t,))
                V("tt", xs[:, :, 0:h], xs[:, :, 0:h], ks[:, :, 0:h], MUL, after=(t,))
                t = V("tt", xs[:, :, h:2 * h], xs[:, :, h:2 * h], qs[:, :, h:2 * h], MUL)
            for bk in range(2):
                for j in range(4):
                    m, a = 2 * bk + j // 2, j % 2
                    cs = slice(a * P, (a + 1) * P)
                    lt, r_ = (x, x) if n < 6 else (kin, Q)
                    tok = mm(psum[2 * (n % 2) + bk][:, j * P:(j + 1) * P], lt[:, m, cs], r_[:, m, cs],
                             True, True, after=(t,) + tuple(free[2 * (n % 2) + bk]), signal=j == 3)
                src = psum[2 * (n % 2) + bk][:, :].rearrange("p (g c) -> p g c", c=P)
                msk = c_(f"level{n}").rearrange("p (o c) -> p o c", o=1).to_broadcast([P, 4, P])
                dst = (sc if n == 0 else tmp8)[:, 4 * bk:4 * bk + 4, :]
                free[2 * (n % 2) + bk] = (V("tt", dst, src, msk, MUL, after=(tok,)),)
            beside(FILL_B[2 + n])
            if n:
                V("tt", sc, sc, tmp8, ADD)
        b16 = bcum.rearrange("p k (c s) -> p (k c) s", s=CH)
        s16 = s3.rearrange("p k (c s) -> p (k c) s", s=CH)
        V("tt", s16, b16[:, :, CH - 1:CH].to_broadcast([P, 16, CH]), b16, SUB)
        t = A("act", s3, s3, Exp, after=(V.now(),))
        V("tt", s3, s3, kin, MUL, after=(t,))
        eb = kin
        t = A("act", eb, bcum, Exp, after=(V.now(), PE.now()))
        t = V("tt", Q, Q, eb, MUL, after=(t,))
        khat = tmp8.rearrange("p (a m) c -> p a m c", a=2)
        for a in range(2):
            for m in range(4):
                tok = PE("tr", psum[a][:, m * P:(m + 1) * P], s3[:, m, a * P:(a + 1) * P], c_("ident"),
                         after=(t,) + tuple(free[a]), signal=m == 3)
            free[a] = (V("copy", khat[:, a, :, :], psum[a][:, :].rearrange("p (m c) -> p m c", c=P),
                         after=(tok,)),)
        st = [None, s1.rearrange("p k t -> p (k t)")[:, 0:512], s1.rearrange("p k t -> p (k t)")[:, 512:1024],
              s2.rearrange("p k t -> p (k t)")[:, 0:512]]
        t = V.now()
        for c in range(NCH - 1):
            a, par = c // 2, c % 2
            rows = slice(64 * par, 64 * par + 64)
            for m in range(4):
                tok = mm(psum[2 + c][:, m * P:(m + 1) * P], khat[rows, a, m, :], VB[rows, a, m * P:(m + 1) * P],
                         True, True, after=(t,) + tuple(free[2 + c]), signal=m == 3)
            nxt = st[c + 1].rearrange("p (m c) -> p m c", c=P)
            if c == 0:
                V("copy", nxt, psum[2][:, :].rearrange("p (m c) -> p m c", c=P), after=(tok,))
            else:
                prev = st[c].rearrange("p (m c) -> p m c", c=P)
                end = (c + 1) * CH - 1
                V("tt", nxt, prev, eb[:, :, end:end + 1].to_broadcast([P, 4, P]), MUL)
                V("tt", nxt, nxt, psum[2 + c][:, :].rearrange("p (m c) -> p m c", c=P), ADD, after=(tok,))
        beside.clear()
        t = V.now()
        yb = Y[:, 4:8, :]
        for m in range(4):
            bank = psum[6 + m // 2]
            for a in range(2):
                at0 = (m % 2) * T + a * P
                mm(bank[:, at0:at0 + P], VB[:, a, m * P:(m + 1) * P], sc[:, 2 * m + a, :], True, False,
                   after=(t,) + tuple(free[6 + m // 2]), loose=True)
                for c in (2 * a, 2 * a + 1):
                    if c:
                        tok = mm(bank[:, at0 + (c % 2) * CH:at0 + (c % 2 + 1) * CH],
                                 st[c][:, m * P:(m + 1) * P], Q[:, m, c * CH:(c + 1) * CH], False, True,
                                 loose=True, signal=c == 3)
        for b in range(2):
            V("copy", yb[:, 2 * b:2 * b + 2, :], psum[6 + b][:, :].rearrange("p (k t) -> p k t", t=T),
              after=(tok,))
        head_rms_gate(yb, s3, s1, Gt, lambda m: p1("b_gn_g", m))
        join()

    def head_rms_gate(y, q, sg, Gt, gain):
        t = A("act", q, y, Square, after=(V.now(), PE.now()))
        sig = A("act", sg, Gt, Sigmoid)
        for m in range(4):
            tok = mm(psum[m // 2][:, (m % 2) * T:(m % 2 + 1) * T], c_("mean128"), q[:, m, :],
                     True, True, after=(t,) + tuple(free[m // 2]), signal=True)
        for b in range(2):
            V("ts", q[:, 2 * b:2 * b + 2, :].rearrange("p k t -> p (k t)"), psum[b][:, :], 1e-6, None,
              ADD, after=(tok,))
            free[b] = (V.now(),)
        t = A("act", q, q, Sqrt, after=(V.now(),))
        V("recip", q, q, after=(t, sig))
        V("tt", y, y, q, MUL)
        V("tt", sg, sg, Gt, MUL)
        for m in range(4):
            V("stt", y[:, m, :], y[:, m, :], gain(m), sg[:, m, :], MUL, MUL)

    def branch_c(PC, VC, WI, S, beside):
        t4 = lambda ap: ap.rearrange("p (k t) -> p k t", t=T)
        rot = t4(S(8 * T))
        cosb = c_("rope_cos").rearrange("p (o t) -> p o t", o=1).to_broadcast([P, 8, T])
        for k in range(8):
            tok = mm(psum[k // 2][:, (k % 2) * T:(k % 2 + 1) * T], c_("swap32"), PC[:, k, :], True, True,
                     signal=True)
        V("tt", rot, PC, cosb, MUL)
        for b in range(4):
            sinb = c_("rope_sin").rearrange("p (o t) -> p o t", o=1).to_broadcast([P, 2, T])
            V("tt", PC[:, 2 * b:2 * b + 2, :], psum[b][:, :].rearrange("p (k t) -> p k t", t=T), sinb, MUL,
              after=(tok,))
        t = V("tt", rot, rot, PC, ADD)
        kd = t4(S(2 * T))
        for c in range(2):
            tok = mm(psum[4][:, c * T:(c + 1) * T], c_(f"dup{c}"), rot[:, 4, :], True, True, after=(t,),
                     signal=True)
        kd_t = A("act", kd.rearrange("p k t -> p (k t)"), psum[4][:, :], Copy, after=(tok,))
        beside(FILL_C[0])
        wis = small[:, 64:72]
        V("ts", wis, WI, 0.5 * 0.125, None, MUL)
        score = S(2 * T).rearrange("p (a s) -> p a s", s=T)
        work_ = S(2 * T).rearrange("p (a s) -> p a s", s=T)
        dotw = S(T)
        top8 = small[:, 80:88]
        for a in range(2):
            n = P * (a + 1)
            for h in range(4):
                rows = slice(64 * (h % 2), 64 * (h % 2) + 64)
                b = (5, 6)[h % 2]
                tok = mm(psum[b][:, (h // 2) * T:(h // 2) * T + n], rot[rows, 5 + h // 2, a * P:(a + 1) * P],
                         rot[rows, 7, 0:n], True, True, after=(t,) + tuple(free[b]), signal=True)
            for h in range(4):
                b = (5, 6)[h % 2]
                dst = score[:, a, 0:n] if h == 0 else dotw[:, 0:n]
                V("ts", dst, psum[b][:, (h // 2) * T:(h // 2) * T + n], 0.0, wis[:, 4 * a + h:4 * a + h + 1],
                  MAX, MUL, after=(tok,))
                if h:
                    V("tt", score[:, a, 0:n], score[:, a, 0:n], dotw[:, 0:n], ADD)
            free[5] = free[6] = (V.now(),)
            if a:
                beside(FILL_C[1])
            nonc = c_("noncausal")[:, a * T:a * T + n]
            V("tt", work_[:, a, 0:n], score[:, a, 0:n], nonc, ADD)
            for _ in range(TOPK // 8):
                V("max8", top8, work_[:, a, 0:n])
                V("replace", work_[:, a, 0:n], top8, work_[:, a, 0:n], -3e30)
            V("ts", work_[:, a, 0:n], work_[:, a, 0:n], -2e30, -1e30, ALU.is_gt, MUL)
            V("tt", work_[:, a, 0:n], work_[:, a, 0:n], nonc, ADD)
        beside(FILL_C[2])
        beside.finish()
        mark = S.at
        for a in range(2):
            S.at = mark
            n = P * (a + 1)
            L = S(8 * n).rearrange("p (h s) -> p h s", s=n)
            probT = S(8 * n).rearrange("p (h s) -> p h s", s=n)
            nm, sm = small[:, 96:104], small[:, 104:112]
            per = 512 // T
            for h in range(8):
                rows = slice(64 * (h % 2), 64 * (h % 2) + 64)
                b = 2 * (h % 2) + h // 4
                tok = mm(psum[b][:, (h // 2 % 2) * T:(h // 2 % 2) * T + n], rot[rows, h // 2, a * P:(a + 1) * P],
                         kd[rows, h // 4, 0:n], True, True, after=(kd_t,) + tuple(free[b]), signal=True)
            for h in range(8):
                b = 2 * (h % 2) + h // 4
                t = V("stt", L[:, h, :], psum[b][:, (h // 2 % 2) * T:(h // 2 % 2) * T + n], 0.125,
                      work_[:, a, 0:n], MUL, ADD, after=(tok, PE.now()))
            for b in range(4):
                free[b] = (t,)
            t = V("rmax", nm, L, axis=AX.X, negate=True)
            for h in range(8):
                t = A("act", L[:, h, :], L[:, h, :], Exp, bias=nm[:, h:h + 1], accum_out=sm[:, h:h + 1],
                      after=(t,) if h == 0 else ())
            V("recip", sm, sm, after=(A.now(),))
            t = V("tt", L, L, sm.rearrange("p (h o) -> p h o", o=1).to_broadcast([P, 8, n]), MUL)
            for j in range(2 * (a + 1)):
                b = 4 + j
                for i in range(4):
                    idx = 4 * j + i
                    h, s = idx // (a + 1), idx % (a + 1)
                    tok = PE("tr", psum[b][:, i * P:(i + 1) * P], L[:, h, s * P:(s + 1) * P], c_("ident"),
                             after=(t,) + tuple(free[b]), signal=i == 3)
                dst = probT.rearrange("p h s -> p (h s)")[:, j * 512:(j + 1) * 512]
                free[b] = (copy_out(dst, psum[b][:, :], (tok, PE.now())),)
            pts = (V.now(), A.now())
            pt = probT.rearrange("p h (s q) -> p (h s) q", q=P)
            for h in range(8):
                rows = slice(64 * (h % 2), 64 * (h % 2) + 64)
                out = psum[0][rows, (h // 2) * P:(h // 2 + 1) * P]
                for s in range(a + 1):
                    tok = mm(out, VC[:, s, 64 * (h // 4):64 * (h // 4) + 64], pt[:, h * (a + 1) + s, :],
                             s == 0, s == a, after=pts + tuple(free[0]), signal=h == 7 and s == a)
            t = V("copy", Y[:, 8:12, a * P:(a + 1) * P], psum[0][:, :].rearrange("p (m q) -> p m q", q=P),
                  after=(tok,))
            free[0] = (t,)
        join()

    def feed_forward(group0, groups, layer, conv, before, dve0, up0, gates, scale_of):
        join()
        s_a, s_v, s_ca, s_cv = ff_sems[conv]
        NA = 4 if conv else 2
        NV = 7 if conv else (4 if gates is not None else 3)
        NCA, NCV = (4 if conv else 3), 2
        zeros = small[:, 128:256]
        V("memset", zeros, 0.0)
        zt = V("memset", rstd[:, :], 0.0)
        for b in range(4):
            for hf in range(2):
                mm(psum[b][:, hf * T:(hf + 1) * T], zeros, rstd[:, :], hf == 0, False, after=(zt,), loose=True)
        at = [GATE_COLS]

        def buffers():
            at[0] += 2
            return [arena[:, (at[0] - 2 + n) * T:(at[0] - 1 + n) * T] for n in range(2)]
        CG, CV, SG, HD = buffers(), buffers(), buffers(), buffers()

        def at_layer(per_layer, v):
            return v if layer is None else layer * per_layer + v

        def token(kind, i, j, n):
            s, per, base = {"a": (s_a, NA, NA * before), "v": (s_v, NV, dve0), "ca": (s_ca, NCA, NCA * before),
                            "cv": (s_cv, NCV, NCV * before), "u": (s_up, 1, up0), "d": (s_down, 1, up0)}[kind]
            return (s, at_layer(FF_GROUPS * per, i * (RING * per) + (base + j * per + n)))

        def done(i, j):
            return (s_done, at_layer(LAYER1_GROUPS, i * RING + (group0 + j + 1)))

        def slot(j):
            return ((group0 + j) % RING) * SLOT

        def unit(j, n):
            return ring[:, slot(j) + n * UNIT:slot(j) + (n + 1) * UNIT]

        def halves(j, n, cols):
            b = GROUP * (j % 2) + n
            return (WH[:, b, cols], WL[:, b, cols])

        def passes(out, w, x, start, stop, loose=False):
            nc.tensor.matmul(out, w[0], x[0], start=start, stop=False, skip_group_check=loose)
            nc.tensor.matmul(out, w[0], x[1], start=False, stop=False, skip_group_check=loose)
            return nc.tensor.matmul(out, w[1], x[0], start=False, stop=stop, skip_group_check=loose)

        def cut(i, j, n, first):
            act, dve, b = nc.scalar, nc.vector, GROUP * (j % 2) + n
            arrived = (s_slot[(group0 + j) % RING],
                       at_layer(16 * (LAYER1_GROUPS // RING), i * 16 + 16 * ((group0 + j) // RING + 1)))
            if n == 0:
                act.wait_ge(*arrived)
                dve.wait_ge(*arrived)
            if not first:
                act.wait_ge(*(token("u", i, j - 2, 1) if n < 2 else token("d", i, j - 2, 1)))
            act.activation(WH[:, b, :], unit(j, n), Copy).then_inc(s_ca, 1)
            if n == 2 and conv:
                if not first:
                    act.wait_ge(*token("v", i, j - 2, NV))
                act.activation(extra[:, (j % 2) * EXTRA:(j % 2 + 1) * EXTRA],
                               ring[:, slot(j) + GROUP * UNIT:slot(j) + SLOT], Copy).then_inc(s_ca, 1)
            dve.wait_ge(*token("ca", i, j, NCA if n == 2 else n + 1))
            if not first:
                dve.wait_ge(*(token("u", i, j - 2, 1) if n < 2 else token("d", i, j - 2, 1)))
            ins = dve.tensor_tensor(WL[:, b, :], unit(j, n), WH[:, b, :].bitcast(f32), SUB)
            if n < 2:
                ins.then_inc(s_cv, 1)
            else:
                ins.then_inc(s_done, 1)

        def up(i, j, first):
            b, pe = psum[4 + j % 2], nc.tensor
            if not first:
                pe.wait_ge(*token("v", i, j - 2, 4 if conv else 2))
            for half in range(2):
                pe.wait_ge(*token("cv", i, j, half + 1))
                for k in range(KT):
                    ins = passes(b[:, half * T:(half + 1) * T], halves(j, half, slice(k * P, (k + 1) * P)),
                                 (UH[:, k, :], UL[:, k, :]), k == 0, k == KT - 1)
            ins.then_inc(s_up, 1)

        def down(i, j, last):
            pe, n = nc.tensor, j % 2
            pe.wait_ge(*done(i, j))
            pe.wait_ge(*token("a", i, j, NA))
            pe.wait_ge(*token("v", i, j, NV))
            ts_ = slice(n * T, (n + 1) * T)
            for dt in range(KT):
                ins = passes(psum[dt // 2][:, (dt % 2) * T:(dt % 2 + 1) * T],
                             halves(j, 2, slice(dt * P, (dt + 1) * P)), (HH[:, ts_], HL[:, ts_]),
                             False, last, loose=True)
            ins.then_inc(s_down, 1)

        def middle(i, j, first):
            n = j % 2
            pg, pv = (psum[4 + n][:, h * T:(h + 1) * T] for h in range(2))
            act, dve = nc.scalar, nc.vector
            chain = [0]
            ts_ = slice(n * T, (n + 1) * T)

            def v(op, *args, after=()):
                if chain[0]:
                    dve.wait_ge(*token("v", i, j, chain[0]))
                for tok in after:
                    dve.wait_ge(*tok)
                issue(dve, op)(*args).then_inc(s_v, 1)
                chain[0] += 1
            act.wait_ge(*token("u", i, j, 1))
            if not first:
                act.wait_ge(*token("v", i, j - 2, NV))
            free_hid = () if first else (token("d", i, j - 2, 1),)
            if conv:
                ex = extra[:, n * EXTRA:(n + 1) * EXTRA]
                act.wait_ge(*token("ca", i, j, NCA))
                act.activation(CG[n], pg, Ident, bias=ex[:, 3:4], scale=ex[:, 2:3]).then_inc(s_a, 1)
                act.activation(CV[n], pv, Ident, bias=ex[:, 7:8], scale=ex[:, 6:7]).then_inc(s_a, 1)
                for h, (c_buf, p_) in enumerate(((CG[n], pg), (CV[n], pv))):
                    for tap in (1, 0):
                        d = 2 - tap
                        v("stt", c_buf[:, d:T], p_[:, 0:T - d], ex[:, 4 * h + tap:4 * h + tap + 1],
                          c_buf[:, d:T], MUL, ADD, after=(token("a", i, j, 2),) if h == 0 and tap else ())
                act.wait_ge(*token("v", i, j, 4))
                act.activation(SG[n], CG[n], Sigmoid).then_inc(s_a, 1)
                v("tt", SG[n], SG[n], CG[n], MUL, after=(token("a", i, j, 3),))
                v("tt", HD[n], SG[n], CV[n], MUL)
            else:
                act.activation(SG[n], pg, Sigmoid).then_inc(s_a, 1)
                v("tt", SG[n], SG[n], pg, MUL, after=(token("a", i, j, 1),))
                v("tt", HD[n], SG[n], pv, MUL)
                if gates is not None:
                    e = (i * RING + j) // (FFE // P)
                    g = gates[:, e * T:(e + 1) * T] if isinstance(e, int) else gates[:, bass.ds(e * T, T)]
                    v("tt", HD[n], HD[n], g, MUL)
            act.wait_ge(*token("v", i, j, chain[0]))
            for tok in free_hid:
                act.wait_ge(*tok)
            act.activation(HH[:, ts_], HD[n], Copy).then_inc(s_a, 1)
            v("tt", HL[:, ts_], HD[n], HH[:, ts_].bitcast(f32), SUB, after=(token("a", i, j, NA),) + free_hid)

        def steps(i, j, first, more=True):
            up(i, j, first)
            if not (first and j == 0):
                down(i, j - 1, False)
            if more:
                for n in range(2):
                    cut(i, j + 1, n, first and j == 0)
            middle(i, j, first)
            if more:
                cut(i, j + 1, 2, first and j == 0)

        for n in range(GROUP):
            cut(0, 0, n, True)
        steps(0, 0, True)
        steps(0, 1, True)
        rounds = (groups - 3) // RING
        with nc.Fori(0, rounds, engines=(nc.tensor.engine, nc.vector.engine, nc.scalar.engine)) as i:
            for j in range(2, 2 + RING):
                steps(i, j, False)
        for g in range(2 + rounds * RING, groups):
            steps(rounds, g - rounds * RING, False, more=g < groups - 1)
        last = groups - 1 - rounds * RING
        down(rounds, last, True)
        last_done[0] = done(rounds, last)
        fin = token("d", rounds, last, 1)
        for dt in range(KT):
            src = psum[dt // 2][:, (dt % 2) * T:(dt % 2 + 1) * T]
            V("stt", X[:, dt, :], src, scale_of(dt), X[:, dt, :], MUL, ADD, after=(fin,) if dt == 0 else ())
        A.wait(fin)
        join()

    GATE_COLS = 8

    class Modulation:
        ROUND_UNITS = 2 * KT

        def __init__(self, st, u0):
            self.st, self.u0, self.taken, self.stage, self.turned = st, u0, 0, 0, 0

        def unit(self, j):
            return self.u0 + j + (1 if j >= MOD_FIRST else 0)

        def __call__(self, n):
            r = self.stage // 3
            if self.stage % 3 == 1:
                for i in range(4):
                    self.last = PE("tr", psum[7][:, i * P:(i + 1) * P], rope[:, i * P:(i + 1) * P], c_("ident"),
                                   after=(self.fetched,), signal=i == 3)
                self.stage += 1
            if self.stage % 3:
                return
            end = min(self.taken + n, (r + 1) * self.ROUND_UNITS, MOD_UNITS)
            for j in range(self.taken, end):
                u, k = self.unit(j), j % KT
                if j == r * self.ROUND_UNITS and r:
                    PE.wait(self.fetched)
                need(PE, self.st, u)
                w = self.st.weights(u)
                for h in range(2):
                    q = (2 * (j // KT) + h) % 4
                    args = (psum[7][32 * q:32 * q + 32, :], cond[:, k:k + 1].to_broadcast([P, 32]),
                            w[:, h * 512:(h + 1) * 512], k == 0, k == KT - 1)
                    if h == 0:
                        mm(*args)
                    else:
                        self.last = last_mm(self.st, u, *args)
                self.taken = j + 1

        def out(self):
            r = self.stage // 3
            if self.stage % 3 == 0 and self.taken == (r + 1) * self.ROUND_UNITS:
                self.fetched = A("act", rope, psum[7][:, :], Copy, after=(self.last,))
                self.stage += 1
            elif self.stage % 3 == 2:
                src = psum[7][:, :].rearrange("p (i q s) -> p q i s", i=4, q=4)[:, :, :, 0:1]
                dst = mod[:, 16 * r:16 * r + 16].rearrange("p (q i o) -> p q i o", q=4, o=1)
                self.fetched = A("act", dst, src, Copy, after=(self.last,))
                self.stage += 1

        def finish(self):
            while self.stage < 3 * MOD_UNITS // self.ROUND_UNITS:
                self(MOD_UNITS)
                self.out()

    def modulation(raw):
        V("tt", mod, raw, p2("ada_b"), ADD)
        for n, norm in ((1, "norm_mix"), (4, "norm_ffn")):
            V("stt", mod[:, 8 * n:8 * n + 8], mod[:, 8 * n:8 * n + 8], 1.0, p2(norm), ADD, MUL)
        join()

    def linear_attention(units, S, rope):
        t4 = lambda ap: ap.rearrange("p (k t) -> p k t", t=T)
        P2 = t4(S(20 * T))
        GV = S(2 * 512).rearrange("p (a c) -> p a c", a=2)
        RV = S(2 * 512).rearrange("p (a c) -> p a c", a=2)
        beside = units(P2, GV, RV)
        gq, gk, gr, rq, rk, rg = (P2[:, s:e, :] for s, e in ((0, 2), (2, 4), (4, 8), (8, 12), (12, 16), (16, 20)))
        mark = S.at
        la, eb, enb, s4 = t4(S(2 * T)), t4(S(2 * T)), t4(S(2 * T)), t4(S(2 * T))
        ga = S(T)
        wga = p2("w_ga").rearrange("p (k r) -> p k r", r=16)
        for k in range(KT):
            tok = mm_u(psum[0][0:16, 0:T], k, wga[:, k, :], slice(0, T), k == 0, k == KT - 1, k == KT - 1, False)
        t = V("copy", ga[0:16, :], psum[0][0:16, 0:T], after=(tok,))
        for m in range(2):
            tok = mm(psum[1][:, m * T:(m + 1) * T], p2("w_alpha")[0:16, m * P:(m + 1) * P], ga[0:16, :],
                     True, True, after=(t,), signal=True)
        beside(FILL_G[0])
        for m in range(2):
            V("ts", la[:, m, :], psum[1][:, m * T:(m + 1) * T], p2("b_alpha", m), None, ADD, after=(tok,))
        A("act", s4, la, Abs, after=(V.now(),))
        t = A("act", s4, s4, Exp, scale=-1.0)
        t = A("act", s4, s4, Ln, bias=1.0)
        V("stt", la, la, 0.0, s4, ALU.min, SUB, after=(t,))
        V("ts", la, la, 1.0 / 16.0, None, MUL)
        bc_ = s4
        for m in range(2):
            V("scan", bc_[:, m, :], c_("chunk_mask"), la[:, m, :], 0.0, MUL, ADD)
        t = A("act", eb, bc_, Exp, after=(V.now(),))
        t = A("act", enb, bc_, Exp, scale=-1.0)
        beside(FILL_G[1])
        kend = la
        split = lambda ap: ap.rearrange("p k (c s) -> p (k c) s", s=CH)
        V("tt", split(kend), split(bc_)[:, :, CH - 1:CH].to_broadcast([P, 8, CH]), split(bc_), SUB)
        e = A("act", kend, kend, Exp, after=(V.now(),))
        V("tt", kend, kend, gk, MUL, after=(e,))
        V("ts", gq, gq, 0.125, None, MUL)
        kb, qf, kf, qb = t4(S(2 * T)), t4(S(2 * T)), t4(S(2 * T)), s4
        V("tt", qb, gq, enb, MUL)
        V("tt", qf, gq, eb, MUL)
        V("tt", kf, gk, enb, MUL)
        t = V("tt", kb, gk, eb, MUL)
        ps4 = lambda b: psum[b][:, :].rearrange("p (h c) -> p h c", c=P)
        sc = S(1024).rearrange("p (m r a c) -> p m r a c", m=2, r=2, a=2)
        tmp = S(512).rearrange("p (g c) -> p g c", c=P)
        for par in range(2):
            rows = slice(64 * par, 64 * par + 64)
            for d, (lt, r_, mask) in enumerate(((kf, qf, "incl_up"), (kb, qb, "strict_low"))):
                b = 2 + 2 * d + par
                for m in range(2):
                    for a in range(2):
                        cs = slice(a * P, (a + 1) * P)
                        tok = mm(psum[b][:, (2 * m + a) * P:(2 * m + a + 1) * P], lt[rows, m, cs],
                                 r_[rows, m, cs], True, True, after=(t,), signal=m == 1 and a == 1)
                msk = c_(mask).rearrange("p (o c) -> p o c", o=1).to_broadcast([P, 4, P])
                V("tt", tmp, ps4(b), msk, MUL, after=(tok,))
                for m in range(2):
                    dst = sc[:, m, par, :, :]
                    src = tmp[:, 2 * m:2 * m + 2, :]
                    V("copy", dst, src) if d == 0 else V("tt", dst, dst, src, ADD)
        beside(FILL_G[2])
        kt_ = S(512).rearrange("p (a c) -> p a c", a=2)
        for a in range(2):
            for m in range(2):
                tok = PE("tr", psum[6][:, (2 * a + m) * P:(2 * a + m + 1) * P], kend[:, m, a * P:(a + 1) * P],
                         c_("ident"), after=(V.now(),), signal=True)
        t = V("copy", kt_, psum[6][:, :].rearrange("p (a c) -> p a c", a=2), after=(tok,))
        beside(FILL_G[3])
        stt_ = [None] + [S(256).rearrange("p (m v) -> p m v", v=P) for _ in range(3)]
        for c in range(NCH - 1):
            a, par = c // 2, c % 2
            rows = slice(64 * par, 64 * par + 64)
            b = 2 + c
            for h in range(4):
                tok = mm(psum[b][64 * (h % 2):64 * (h % 2) + 64, (h // 2) * P:(h // 2 + 1) * P],
                         kt_[rows, a, 64 * h:64 * h + 64], GV[rows, a, h * P:(h + 1) * P], True, True,
                         after=(V.now(),), signal=h == 3)
            for m in range(2):
                src = psum[b][:, m * P:(m + 1) * P]
                if c == 0:
                    V("copy", stt_[1][:, m, :], src, after=(tok,))
                else:
                    end = (c + 1) * CH - 1
                    V("stt", stt_[c + 1][:, m, :], stt_[c][:, m, :], eb[:, m, end:end + 1], src, MUL, ADD,
                      after=(tok,))
        beside(FILL_G[4])
        beside.finish()
        t = V.now()
        for par in range(2):
            rows = slice(64 * par, 64 * par + 64)
            for m in range(2):
                h = 2 * m + par
                for a in range(2):
                    at0 = m * T + a * P
                    mm(psum[6 + par][:, at0:at0 + P], GV[:, a, h * P:(h + 1) * P], sc[:, m, par, a, :],
                       True, False, after=(t,) + tuple(free[6 + par]), loose=True)
                    for c in (2 * a, 2 * a + 1):
                        if c:
                            tok = mm(psum[6 + par][:, at0 + (c % 2) * CH:at0 + (c % 2 + 1) * CH],
                                     stt_[c][rows, m, :], qf[rows, m, c * CH:(c + 1) * CH], False, True,
                                     loose=True, signal=c == 3)
        yg = Y[:, 0:4, :]
        for par in range(2):
            V("copy", yg[:, par:4:2, :], psum[6 + par][:, :].rearrange("p (k t) -> p k t", t=T), after=(tok,))
        join()
        S.at = mark
        qn, sn = t4(S(4 * T)), t4(S(4 * T))
        head_rms_gate(yg, qn, sn, gr, lambda m: p2("gla_g", m))
        cos_b = rope[:, 0:T].rearrange("p (o t) -> p o t", o=1).to_broadcast([P, 4, T])
        sin_b = rope[:, T:2 * T].rearrange("p (o t) -> p o t", o=1).to_broadcast([P, 2, T])
        for n, src in enumerate((rq, rk)):
            for m in range(4):
                b = 4 + 2 * n + m // 2
                tok = mm(psum[b][:, (m % 2) * T:(m % 2 + 1) * T], c_("swap64"), src[:, m, :], True, True,
                         signal=True)
            V("tt", src, src, cos_b, MUL, after=(tok,))
            for bb in range(2):
                V("tt", sn[:, 2 * bb:2 * bb + 2, :],
                  psum[4 + 2 * n + bb][:, :].rearrange("p (k t) -> p k t", t=T), sin_b, MUL)
            V("tt", src, src, sn, ADD)
        join()
        S.at = mark
        sc2 = S(1024).rearrange("p (m a c) -> p m a c", m=4, a=2)
        kd, qd = t4(S(4 * T)), t4(S(4 * T))
        kdt = S(1024).rearrange("p (a m c) -> p a m c", a=2, m=4)
        st2 = [None] + [S(512).rearrange("p (m v) -> p m v", v=P) for _ in range(3)]
        for m in range(4):
            tab = lambda name: c_(name)[:, m * CH:(m + 1) * CH].rearrange("p (o s) -> p o s", o=1)\
                .to_broadcast([P, NCH, CH])
            V("tt", kd[:, m, :].rearrange("p (c s) -> p c s", s=CH),
              rk[:, m, :].rearrange("p (c s) -> p c s", s=CH), tab("ret_k"), MUL)
            V("tt", qd[:, m, :].rearrange("p (c s) -> p c s", s=CH),
              rq[:, m, :].rearrange("p (c s) -> p c s", s=CH), tab("ret_q"), MUL)
        for bk in range(2):
            for j in range(4):
                m, a = 2 * bk + j // 2, j % 2
                cs = slice(a * P, (a + 1) * P)
                tok = mm(psum[bk][:, j * P:(j + 1) * P], rk[:, m, cs], rq[:, m, cs], True, True, signal=j == 3)
            for mm_ in range(2):
                m = 2 * bk + mm_
                intra = c_("ret_intra")[:, m * P:(m + 1) * P].rearrange("p (o c) -> p o c", o=1)\
                    .to_broadcast([P, 2, P])
                V("tt", sc2[:, m, :, :], ps4(bk)[:, 2 * mm_:2 * mm_ + 2, :], intra, MUL, after=(tok,))
        V("ts", sc2.rearrange("p m a c -> p (m a c)"), sc2.rearrange("p m a c -> p (m a c)"), 128 ** -0.5, None, MUL)
        for a in range(2):
            for m in range(4):
                tok = PE("tr", psum[2 + a][:, m * P:(m + 1) * P], kd[:, m, a * P:(a + 1) * P], c_("ident"),
                         after=(V.now(),), signal=m == 3)
            copy_out(kdt[:, a, :, :], ps4(2 + a), (tok,))
        t = (V.now(), A.now())
        for c in range(NCH - 1):
            a, par = c // 2, c % 2
            rows = slice(64 * par, 64 * par + 64)
            b = 4 + c
            for m in range(4):
                tok = mm(psum[b][:, m * P:(m + 1) * P], kdt[rows, a, m, :], RV[rows, a, m * P:(m + 1) * P],
                         True, True, after=t, signal=m == 3)
            for m in range(4):
                src = psum[b][:, m * P:(m + 1) * P]
                if c == 0:
                    V("copy", st2[1][:, m, :], src, after=(tok,))
                else:
                    V("stt", st2[c + 1][:, m, :], st2[c][:, m, :], c_("ret_chunk")[:, m:m + 1], src, MUL, ADD,
                      after=(tok,))
        t = V.now()
        for m in range(4):
            bank = psum[m // 2]
            for a in range(2):
                at0 = (m % 2) * T + a * P
                mm(bank[:, at0:at0 + P], RV[:, a, m * P:(m + 1) * P], sc2[:, m, a, :], True, False,
                   after=(t,), loose=True)
                for c in (2 * a, 2 * a + 1):
                    if c:
                        tok = mm(bank[:, at0 + (c % 2) * CH:at0 + (c % 2 + 1) * CH], st2[c][:, m, :],
                                 qd[:, m, c * CH:(c + 1) * CH], False, True, loose=True, signal=c == 3)
        yr = Y[:, 4:8, :]
        for b in range(2):
            V("copy", yr[:, 2 * b:2 * b + 2, :], psum[b][:, :].rearrange("p (k t) -> p k t", t=T), after=(tok,))
        t = V.now()
        for m in range(4):
            tok = mm(psum[2 + m // 2][:, (m % 2) * T:(m % 2 + 1) * T], c_("mean128"), yr[:, m, :], True, True,
                     after=(t,), signal=True)
        for b in range(2):
            V("tt", yr[:, 2 * b:2 * b + 2, :], yr[:, 2 * b:2 * b + 2, :],
              psum[2 + b][:, :].rearrange("p (k t) -> p k t", t=T), SUB, after=(tok,))
        t = A("act", qd, yr, Square, after=(V.now(),))
        sig = A("act", kd, rg, Sigmoid)
        for m in range(4):
            tok = mm(psum[4 + m // 2][:, (m % 2) * T:(m % 2 + 1) * T], c_("mean128"), qd[:, m, :], True, True,
                     after=(t,), signal=True)
        for b in range(2):
            V("ts", qd[:, 2 * b:2 * b + 2, :].rearrange("p k t -> p (k t)"), psum[4 + b][:, :], 1e-6, None, ADD,
              after=(tok,))
        t = A("act", qd, qd, Sqrt, after=(V.now(),))
        V("recip", qd, qd, after=(t, sig))
        V("tt", yr, yr, qd, MUL)
        for m in range(4):
            V("ts", yr[:, m, :], yr[:, m, :], p2("ret_g", m), p2("ret_b", m), MUL, ADD)
        V("tt", kd, kd, rg, MUL)
        V("tt", yr, yr, kd, MUL)
        join()

    def route(gates):
        rw = router[:, :].rearrange("p (k e) -> p k e", e=EXPERTS)
        sm = small
        lg, m8, idx, oh0, oh1, gt = (sm[:, 256 + 8 * n:264 + 8 * n] for n in range(6))
        idf, p0, p1_ = sm[:, 304:312], sm[:, 312:313], sm[:, 313:314]
        lane = sm[:, 320:328]
        gT = sm[0:8, 0:T]
        for e in range(EXPERTS):
            V("memset", lane[:, e:e + 1], float(e))
        for a in range(2):
            for k in range(KT):
                tok = mm_u(psum[0][:, a * 8:a * 8 + 8], k, rw[:, k, :], slice(a * P, (a + 1) * P), k == 0,
                           k == KT - 1, k == KT - 1, True)
            V("copy", lg, psum[0][:, a * 8:a * 8 + 8], after=(tok,))
            V("max8", m8, lg)
            V("maxidx", idx.bitcast(u32), m8, lg)
            V("copy", idf, idx.bitcast(u32))
            V("ts", oh0, lane, idf[:, 0:1], None, ALU.is_equal)
            V("ts", oh1, lane, idf[:, 1:2], None, ALU.is_equal)
            t = V("tt", p1_, m8[:, 1:2], m8[:, 0:1], SUB)
            t = A("act", p1_, p1_, Exp, after=(t,))
            V("ts", p0, p1_, 1.0, None, ADD, after=(t,))
            V("recip", p0, p0)
            V("tt", p1_, p1_, p0, MUL)
            V("ts", gt, oh0, p0, None, MUL)
            t = V("stt", gt, oh1, p1_, gt, MUL, ADD)
            tok = PE("tr", psum[1][0:8, a * P:(a + 1) * P], gt, c_("ident"), after=(t,))
            V("copy", gT[:, a * P:(a + 1) * P], psum[1][0:8, a * P:(a + 1) * P], after=(tok,))
        t = V.now()
        for e in range(EXPERTS):
            sel = c_("ident")[0:8, e:e + 1].to_broadcast([8, P])
            tok = mm(psum[2 + e // 2][:, (e % 2) * T:(e % 2 + 1) * T], sel, gT, True, True, after=(t,), signal=True)
        for b in range(4):
            copy_out(gates[:, 2 * b * T:(2 * b + 2) * T], psum[2 + b][:, :], (tok,))
        join()

    layer_stream = [None]

    def run(u0, n, dst, stream=None, banks=(1, 2, 3, 4, 5, 6, 7)):
        for j in range(0, n, 2):
            b = banks[(j // 2) % len(banks)]
            PE.wait(*free[b])
            k = min(2, n - j)
            for h in range(k):
                tok = project(stream or layer_stream[0], u0 + j + h, u0 + n, b, h)
            free[b] = (copy_out(dst[:, j:j + k, :].rearrange("p k t -> p (k t)"), psum[b][:, 0:k * T],
                                (tok,)),)

    def run_tokens(u0, n, dst, stream=None):
        for j in range(n):
            b = 1 + j % 7
            PE.wait(*free[b])
            tok = project_tokens(stream or layer_stream[0], u0 + j, u0 + n, b, 0)
            free[b] = (copy_out(dst[:, :, j * P:(j + 1) * P],
                                psum[b][:, 0:T].rearrange("p (a c) -> p a c", a=2), (tok,)),)

    weight_stream()

    for dst, src in ((const, a_const), (norms, a_norms[:, 0:KT]), (final2, a_norms[:, KT:2 * KT]),
                     (router, a_router)):
        nc.scalar.dma_start(dst[:, :], src).then_inc(s_in, 16)
    nc.scalar.dma_start(X, a_x.rearrange("k p t -> p k t")).then_inc(s_in, 16)
    nc.scalar.dma_start(cond[:, :], a_cond).then_inc(s_in, 16)
    for q in work:
        q.engine.wait_ge(s_in, 96)
    t = A("act", small[:, 0:8], cond[:, :], Sigmoid)
    V("tt", cond[:, :], cond[:, :], small[:, 0:8], MUL, after=(t,))
    restart()

    with nc.Fori(0, LAYERS, engines=tuple(q.engine.engine for q in work)) as layer:
        st = Stream(0, layer)
        nc.scalar.dma_start(par1[:, :], a_par1[bass.ds(layer, 1), :, :].rearrange("o p n -> p (o n)"))\
            .then_inc(s_par, 16)
        for q in work:
            q.engine.wait_ge(s_par, layer * 16 + 16)
        t4 = lambda ap: ap.rearrange("p (k t) -> p k t", t=T)
        rms(X, 1e-6, lambda k: p1("norm_mix", k))

        layer_stream[0] = st
        PA = t4(arena[:, 0:14 * T])
        run(0, 14, PA)
        join()
        beside = Modulation(st, 14)
        branch_a(PA, st, beside)
        beside.finish()
        V("copy", raw_mod[:, bass.ds(layer * MOD_UNITS, MOD_UNITS)], mod, after=(beside.fetched,))
        join()
        if probe:
            probe("ya", Y[:, 0:4, :], A)
        S = Space()
        st.split_to = MOD_UNITS + 15
        gat = t4(arena[:, split_at - 24 * T:split_at])
        gates_beside = Beside(st, MOD_UNITS + 64, (5, 7))
        gates_beside.add(MOD_UNITS + 31, GATES_B, gat[:, 0:GATES_B, :], Sigmoid)
        gates_beside.add(MOD_UNITS + 40 + GATES_B, 24 - GATES_B, gat[:, GATES_B:24, :], Sigmoid)
        PB = t4(S(12 * T))
        VB = S(1024).rearrange("p (a c) -> p a c", a=2)
        run(MOD_UNITS + 15, 8, PB[:, 0:8, :])
        run_tokens(MOD_UNITS + 23, 4, VB)
        run(MOD_UNITS + 27, 4, PB[:, 8:12, :])
        join()
        branch_b(PB, VB, S, gates_beside)
        S = Space()
        PC = t4(S(8 * T))
        VC = S(256).rearrange("p (a c) -> p a c", a=2)
        run(MOD_UNITS + GATES_B + 31, 8, PC)
        run_tokens(MOD_UNITS + GATES_B + 39, 1, VC)
        WI = small[:, 72:80]
        widx = p1("w_idx").rearrange("p (k h) -> p k h", h=4)
        for a in range(2):
            for k in range(KT):
                tok = mm_u(psum[0][:, 4 * a:4 * a + 4], k, widx[:, k, :], slice(a * P, (a + 1) * P), k == 0,
                           k == KT - 1, k == KT - 1, True)
        V("copy", WI, psum[0][:, 0:8], after=(tok,))
        join()
        branch_c(PC, VC, WI, S, gates_beside)
        for n in range(3):
            ks = slice(4 * n, 4 * n + 4)
            t = A("act", YH[:, ks, :], Y[:, ks, :], Copy)
            y_t = V("tt", YL[:, ks, :], Y[:, ks, :], YH[:, ks, :].bitcast(f32), SUB, after=(t,))
        PE.wait(y_t)
        merged = Y[:, 0:8, :]
        prod = Y[:, 8:12, :]
        for n in range(3):
            u0 = MOD_UNITS + 64 + 4 * n
            split(st, u0 + 5, MOD_UNITS + 76)
            PE.wait(parts_ready[id(st), u0 + 3])
            for dt in range(KT):
                b = (n * KT + dt) % 8
                PE.wait(*free[b])
                for m in range(4):
                    u = u0 + m
                    tok = mm3(psum[b][:, 0:T], parts(st, u, slice(dt * P, (dt + 1) * P)),
                              (YH[:, 4 * n + m, :], YL[:, 4 * n + m, :]), m == 0, m == 3, signal=m == 3)
                gk_ = gat[:, n * KT + dt, :]
                if n == 0:
                    t = V("tt", merged[:, dt, :], psum[b][:, 0:T], gk_, MUL, after=(tok,))
                else:
                    t = V("tt", prod[:, dt % 4, :], psum[b][:, 0:T], gk_, MUL, after=(tok,))
                    V("tt", merged[:, dt, :], merged[:, dt, :], prod[:, dt % 4, :], ADD)
                free[b] = (t,)
            for m in range(4):
                read_by[(u0 + m) % SPLIT] = tok
        split_u(merged, (V.now(),))
        PE.wait(V.now())
        for dt in range(KT):
            PE.wait(*free[dt])
            tok = project(st, MOD_UNITS + 76 + dt, MOD_UNITS + 84, dt, 0)
            V("tt", X[:, dt, :], X[:, dt, :], psum[dt][:, 0:T], ADD, after=(tok,))
        join()
        if probe:
            probe("hmix", X, A)
        rms(X, 1e-6, lambda k: p1("norm_ffn", k))
        feed_forward(MIX1_GROUPS + ADA_GROUPS, FF_GROUPS, layer, True, 0, 0, 0, None, lambda dt: 1.0)
        restart()

    rms(X, 1e-6, lambda k: norms[:, k:k + 1], out=X)
    join()
    if probe:
        probe("x1", X, A)
        join()
    pos = arena[:, 0:T]
    ang, turns, red = (arena[:, (1 + n) * T:(2 + n) * T] for n in range(3))
    nc.scalar.dma_start(pos.bitcast(i32), a_pos).then_inc(s_in, 16)
    for q in work:
        q.engine.wait_ge(s_in, 112)
    V("copy", ang, pos.bitcast(i32))
    V("ts", ang, ang, c_("inv_freq"), None, MUL)
    V("ts", turns, ang, float(1 / (2 * np.pi)), ROUND, MUL, ADD)
    V("ts", turns, turns, ROUND, None, SUB)
    for part in TWO_PI:
        V("stt", ang, turns, -part, ang, MUL, ADD)
    V("ts", ang, ang, -3.1415925, 3.1415925, MAX, ALU.min)
    t = V.now()
    A("act", rope[:, T:2 * T], ang, Sin, after=(t,))
    t = A("act", red, ang, Sin, scale=0.5)
    V("ts", rope[:, T:2 * T], rope[:, T:2 * T], c_("sin_sign"), None, MUL, after=(t,))
    V("tt", red, red, red, MUL)
    V("ts", rope[:, 0:T], red, -2.0, 1.0, MUL, ADD)
    join()

    at_group = LAYERS * LAYER1_GROUPS
    ff_base = 0
    for layer2 in range(LAYERS):
        nc.scalar.dma_start(par2[:, :], a_par2[layer2]).then_inc(s_par, 16)
        for q in work:
            q.engine.wait_ge(s_par, 16 * (LAYERS + layer2 + 1))
        modulation(raw_mod[:, layer2 * MOD_UNITS:(layer2 + 1) * MOD_UNITS])
        rms(X, 1e-6, lambda k: mod[:, 8 + k:9 + k], lambda k: mod[:, k:k + 1])
        st = Stream(at_group)

        def units(P2, GV, RV):
            run(0, 4, P2[:, 0:4, :], stream=st)
            run_tokens(4, 4, GV, stream=st)
            run(8, 4, P2[:, 4:8, :], stream=st)
            join()
            beside = Beside(st, 28, (7, 0))
            beside.add(12, 8, P2[:, 8:16, :])
            beside.add_tokens(20, 4, RV)
            beside.add(24, 4, P2[:, 16:20, :])
            return beside
        linear_attention(units, Space(), rope)
        if probe:
            probe(f"mix{layer2}", Y[:, 0:8, :], A)
        split_u(Y[:, 0:8, :], ())
        st.split_to = 28
        join()
        for dt in range(KT):
            tok = project(st, 28 + dt, 36, dt, 0)
            V("stt", X[:, dt, :], psum[dt][:, 0:T], mod[:, 16 + dt:17 + dt], X[:, dt, :], MUL, ADD, after=(tok,))
        join()
        at_group += MIX2_GROUPS
        rms(X, 1e-6, lambda k: mod[:, 32 + k:33 + k], lambda k: mod[:, 24 + k:25 + k])
        gates, n_groups = None, FF_GROUPS
        if layer2 == 1:
            join()
            gates, n_groups = arena[:, 0:EXPERTS * T], MOE_GROUPS
            route(gates)
        feed_forward(at_group, n_groups, None, False, FF_GROUPS * layer2, 3 * FF_GROUPS * layer2,
                     (LAYERS + layer2) * FF_GROUPS, gates, lambda dt: mod[:, 40 + dt:41 + dt])
        at_group += n_groups
        if probe:
            probe(f"x2{layer2}", X, A)
    assert at_group == ALL_GROUPS
    V("copy", norms[:, :], final2[:, :])
    rms(X, 1e-6, lambda k: norms[:, k:k + 1], out=X)
    nc.scalar.wait_ge(*V.now())
    nc.scalar.dma_start(a_out.rearrange("k p t -> p k t"), X).then_inc(s_out, 16)
    nc.scalar.wait_ge(s_out, 16)
    es.close()


TWO_PI = (6.28125, 0.0019340515136718750, float(2 * np.pi - 6.28125 - 0.0019340515136718750))
ROUND = float(1.5 * 2 ** 23)


def columns(a):
    k, n = a.shape
    return a.reshape(k // P, P, n // P, P).transpose(2, 1, 0, 3).reshape(n // P, P, k)


def per_channel(a):
    return np.asarray(a).reshape(-1, P).T


def weight_groups(inp):
    out = np.zeros((ALL_GROUPS, P, SLOT), np.float32)
    at = 0

    def put(units):
        nonlocal at
        n = len(units) // GROUP
        out[at:at + n, :, :GROUP * UNIT] = np.stack(units).reshape(n, GROUP, P, UNIT).transpose(0, 2, 1, 3)            .reshape(n, P, GROUP * UNIT)
        at += n
    A_END, B_END = 1792, 1792 + 2048
    for l in range(LAYERS):
        w = inp["w_in"][l]
        b, c = w[:, A_END:B_END], w[:, B_END:B_END + 1092]
        low = np.concatenate([np.concatenate([inp["a_w_up"][l], inp["a_a_up"][l]], 0), inp["a_g_up"][l]], 1)
        ki = c[:, 1024:1088]
        mod = inp["ada_w_2"][l].reshape(KT, P, MOD_UNITS // KT, UNIT).transpose(2, 0, 1, 3).reshape(MOD_UNITS, P, UNIT)
        gates = columns(w[:, B_END + 1092:])
        units = [*columns(w[:, :A_END]), *mod[:MOD_FIRST], low, *mod[MOD_FIRST:], *columns(b), *gates[:GATES_B],
                 *columns(c[:, 0:640]), *columns(c[:, 768:1024]), *columns(np.concatenate([ki, ki], 1)),
                 *columns(c[:, 640:768]), *gates[GATES_B:],
                 *inp["w_branch"][l].reshape(12, P, D), *columns(inp["w_o"][l])]
        put(units)
        gate, val = columns(inp["w_up"][l][:, :FF]), columns(inp["w_up"][l][:, FF:])
        down = inp["w_down"][l].reshape(FF_GROUPS, P, D)
        taps = np.concatenate([inp["conv_w"][l], inp["conv_b"][l][None]], 0).reshape(4, 2, FF_GROUPS, P)
        out[at:at + FF_GROUPS, :, GROUP * UNIT:] = taps.transpose(2, 3, 1, 0).reshape(FF_GROUPS, P, EXTRA)
        put([u for g in range(FF_GROUPS) for u in (gate[g], val[g], down[g])])
    for l in range(LAYERS):
        w = inp["w_in_2"][l]
        cut = lambda s, n: [*columns(w[:, s:s + n])]
        put([*cut(0, 512), *cut(512, 512), *cut(1024, 512), *cut(1552, 1024), *cut(2576, 512), *cut(3088, 512),
             *columns(inp["w_out_2"][l])])
        if l == 0:
            w1, w3 = columns(inp["ffn_w1_2"][0]), columns(inp["ffn_w3_2"][0])
            w2 = inp["ffn_w2_2"][0].reshape(FF_GROUPS, P, D)
        else:
            w1, w3 = (np.concatenate([columns(inp[n][0, e]) for e in range(EXPERTS)]) for n in ("moe_w1_2", "moe_w3_2"))
            w2 = inp["moe_w2_2"][0].reshape(MOE_GROUPS, P, D)
        put([u for g in range(len(w1)) for u in (w1[g], w3[g], w2[g])])
    assert at == ALL_GROUPS
    return out


def laid_out(inp):
    par1 = np.zeros((LAYERS, P, PAR1_COLS), np.float32)
    par2 = np.zeros((LAYERS, P, PAR2_COLS), np.float32)
    for l in range(LAYERS):
        put = lambda name, a: par1[l].__setitem__((slice(None), PAR1[name]), a)
        for name, key in (("norm_mix", "norm_mix_g"), ("mu", "a_mu"), ("w0", "a_w0"), ("a0", "a_a0"),
                          ("k_k", "a_k_k"), ("k_a", "a_k_a"), ("gn_g", "a_gn_g"), ("gn_b", "a_gn_b"),
                          ("b_gn_g", "b_gn_g"), ("norm_ffn", "norm_ffn_g")):
            put(name, per_channel(inp[key][l]))
        put("r_k", per_channel(inp["a_r_k"][l].reshape(-1)))
        put("lb_logits", np.concatenate([per_channel(inp["b_lb_logits"][j]) for j in range(LAYERS)], 1))
        put("lb_flag", float(l))
        put("w_idx", inp["w_in"][l][:, 4928:4932].reshape(KT, P, 4).transpose(1, 0, 2).reshape(P, 32))
        put = lambda name, a: par2[l].__setitem__((slice(None), PAR2[name]), a)
        for name, key in (("norm_mix", "norm_mix_g_2"), ("norm_ffn", "norm_ffn_g_2"), ("ada_b", "ada_b_2"),
                          ("b_alpha", "gla_b_alpha_2"), ("gla_g", "gla_norm_g_2"), ("ret_g", "ret_gn_g_2"),
                          ("ret_b", "ret_gn_b_2")):
            put(name, per_channel(inp[key][l]))
        put("w_ga", inp["w_in_2"][l][:, 1536:1552].reshape(KT, P, 16).transpose(1, 0, 2).reshape(P, 128))
        par2[l, 0:16, PAR2["w_alpha"]] = inp["gla_w_alpha_2"][l]
    return {
        "x": np.ascontiguousarray(inp["x"][0].T.reshape(KT, P, T)),
        "pos": np.ascontiguousarray(np.broadcast_to(inp["positions_2"], (P, T))),
        "cond": np.ascontiguousarray(per_channel(inp["c_2"][0])),
        "const": constants(),
        "par1": par1, "par2": par2,
        "router": np.ascontiguousarray(
            inp["router_w_2"][0].reshape(KT, P, EXPERTS).transpose(1, 0, 2).reshape(P, KT * EXPERTS)),
        "norms": np.ascontiguousarray(
            np.concatenate([per_channel(inp["norm_final_g"]), per_channel(inp["final_g_2"])], 1)),
        "weights": weight_groups(inp),
    }


def kernel(**inputs):
    import concourse.bacc as bacc
    from concourse import mybir
    from concourse.bass_utils import run_bass_kernel_spmd

    arrays = laid_out({k: np.asarray(v) for k, v in inputs.items()})
    nc = bacc.Bacc("TRN2", target_bir_lowering=False, num_devices=1)
    aps = {n: nc.dram_tensor(f"in_{n}", a.shape, mybir.dt.from_np(a.dtype), kind="ExternalInput").ap()
           for n, a in arrays.items()}
    out = nc.dram_tensor("out", (KT, P, T), mybir.dt.float32, kind="ExternalOutput").ap()
    build(nc, aps["x"], aps["pos"], aps["cond"], aps["const"], aps["par1"], aps["par2"], aps["router"],
          aps["norms"], aps["weights"], out)
    r = run_bass_kernel_spmd(nc, [{f"in_{n}": a for n, a in arrays.items()}], core_ids=[0])
    got = r.results[0]["out"]
    return np.ascontiguousarray(got.reshape(D, T).T[None])
```

```python
import numpy as np

P = 128
T = 256
D = 1024
KT = D // P
LAYERS = 2
CH = 64
NCH = T // CH
HALVES = T // P
FF, FFE, EXPERTS = 2816, 1408, 8
UNIT = KT * P
GROUP = 3
EXTRA = 8
SLOT = GROUP * UNIT + EXTRA
RING = 2
MIX1_GROUPS = 28
MIX2_GROUPS = 12
ADA_GROUPS = 16
MOD_UNITS = GROUP * ADA_GROUPS
MOD_FIRST = 9
LOW_UNIT = 14 + MOD_FIRST
GATES_LATE = 8
FF_GROUPS = FF // P
MOE_GROUPS = EXPERTS * FFE // P
LAYER1_GROUPS = MIX1_GROUPS + ADA_GROUPS + FF_GROUPS
ALL_GROUPS = LAYERS * (LAYER1_GROUPS + MIX2_GROUPS) + FF_GROUPS + MOE_GROUPS
TOPK = 64

PAR1 = {}
PAR2 = {}
CONST = {}


def _columns(table, sizes):
    at = 0
    for name, n in sizes:
        table[name] = slice(at, at + n)
        at += n
    return at


PAR1_COLS = _columns(PAR1, [
    ("norm_mix", 8), ("mu", 14), ("w0", 4), ("a0", 4), ("k_k", 4), ("k_a", 4), ("r_k", 4),
    ("gn_g", 4), ("gn_b", 4), ("b_gn_g", 4), ("norm_ffn", 8), ("lb_logits", 8), ("lb_flag", 1),
    ])
PAR2_COLS = _columns(PAR2, [
    ("norm_mix", 8), ("norm_ffn", 8), ("ada_b", 48), ("b_alpha", 2), ("gla_g", 4),
    ("ret_g", 4), ("ret_b", 4), ("w_ga", 128), ("w_alpha", 256)])
CONST_COLS = _columns(CONST, [
    ("ident", 128), ("strict_up_neg", 128), ("strict_up", 128), ("incl_up", 128),
    ("strict_low", 128), ("low16_neg", 128), ("up16_neg", 128), ("low32_neg", 128),
    ("low64_neg", 128), ("pair_blocks", 128), ("pair_mean", 128), ("mean128", 128),
    ("level0", 128), ("level1", 128), ("level2", 128), ("level3", 128),
    ("level4", 128), ("level5", 128), ("level6", 128), ("swap32", 128), ("swap64", 128),
    ("dup0", 128), ("dup1", 128), ("rope_cos", T), ("rope_sin", T), ("chunk_mask", T),
    ("noncausal", 2 * T), ("ret_intra", 4 * P), ("ret_q", 4 * CH), ("ret_k", 4 * CH),
    ("ret_chunk", 4), ("inv_freq", 1), ("sin_sign", 1)])


def constants():
    c = np.zeros((P, CONST_COLS), np.float32)
    r, q = np.arange(P)[:, None], np.arange(P)[None, :]
    same = (r // CH) == (q // CH)
    put = lambda name, a: c.__setitem__((slice(None), CONST[name]), a)
    put("ident", r == q)
    put("strict_up", same & (r < q))
    put("strict_up_neg", -1.0 * (same & (r < q)))
    put("incl_up", same & (r <= q))
    put("strict_low", same & (r > q))
    put("low16_neg", -1.0 * ((r // 16 == q // 16) & (r > q)))
    put("up16_neg", -1.0 * ((r // 16 == q // 16) & (r < q)))
    put("low32_neg", -1.0 * ((r // 32 == q // 32) & (r // 16 > q // 16)))
    put("low64_neg", -1.0 * ((r // 64 == q // 64) & (r // 32 > q // 32)))
    put("pair_blocks", same)
    put("pair_mean", same / float(CH))
    put("mean128", 1.0 / P)
    for n in range(6):
        h = 32 >> n
        put(f"level{n}", (r // (2 * h) == q // (2 * h)) & (r % (2 * h) < h) & (q % (2 * h) >= h))
    put("level6", r == q)
    put("swap32", (r // 64 == q // 64) & ((r % 64 + 32) % 64 == q % 64))
    put("swap64", (r + 64) % 128 == q)
    put("dup0", r == q % 64)
    put("dup1", r == 64 + q % 64)
    inv = np.float32(10000.0) ** (-np.arange(32, dtype=np.float32) * np.float32(2.0 / 64))
    ang = (np.arange(T, dtype=np.float32)[None, :] * inv.astype(np.float32)[:, None]).astype(np.float32)
    rows = np.arange(P) % 32
    put("rope_cos", np.cos(ang.astype(np.float64))[rows])
    put("rope_sin", np.sin(ang.astype(np.float64))[rows] * np.where(np.arange(P) % 64 < 32, -1, 1)[:, None])
    put("chunk_mask", (np.arange(T) % CH != 0)[None, :])
    s = np.arange(T)[None, :]
    put("noncausal", np.concatenate([np.where(s <= r + P * a, 0.0, -1e30) for a in range(2)], 1))
    lg = np.log(1.0 - 2.0 ** (-5.0 - np.arange(4)))
    put("ret_intra", np.concatenate([np.where(same, np.exp(g * np.abs(r - q)), 0.0) for g in lg], 1))
    t = np.arange(CH)
    put("ret_q", np.concatenate([np.exp(g * (t + 1)) for g in lg])[None, :] * 128 ** -0.5)
    put("ret_k", np.concatenate([np.exp(g * (CH - 1 - t)) for g in lg])[None, :])
    put("ret_chunk", np.exp(lg * CH)[None, :])
    inv = np.float32(10000.0) ** (-np.arange(64, dtype=np.float32) / np.float32(64))
    put("inv_freq", inv[np.arange(P) % 64][:, None])
    put("sin_sign", np.where(np.arange(P) < 64, -1.0, 1.0)[:, None])
    return c


def build(nc, a_x, a_pos, a_cond, a_const, a_par1, a_par2, a_router, a_norms, a_weights, a_out):
    import concourse.bass as bass
    from concourse import mybir
    from contextlib import ExitStack

    f32, i32, u32 = mybir.dt.float32, mybir.dt.int32, mybir.dt.uint32
    ALU, ACTF, AX = mybir.AluOpType, mybir.ActivationFunctionType, mybir.AxisListType
    MUL, ADD, SUB, MAX = ALU.mult, ALU.add, ALU.subtract, ALU.max
    Exp, Ln, Sigmoid, Tanh, Sqrt, Sin, Copy, Ident, Square, Abs = (
        ACTF.Exp, ACTF.Ln, ACTF.Sigmoid, ACTF.Tanh, ACTF.Sqrt, ACTF.Sin, ACTF.Copy,
        ACTF.Identity, ACTF.Square, ACTF.Abs)
    es = ExitStack()

    class Queue:

        def __init__(self, engine, name, chained):
            self.engine, self.sem, self.count, self.chained = engine, sem(name), 0, chained
            self.passed, self.tail = {}, None

        def wait(self, *tokens):
            for s, v in tokens:
                if isinstance(v, int):
                    if self.passed.get(id(s), 0) >= v:
                        continue
                    self.passed[id(s)] = v
                self.engine.wait_ge(s, v)

        def now(self):
            return self.tail or (self.sem, self.count)

        def __call__(self, op, *args, after=(), signal=True, raises=None, **kw):
            self.wait(*[x for x in after if x is not None])
            if self.chained and (self.count or self.tail):
                self.wait(self.now())
            ins = issue(self.engine, op)(*args, **kw)
            if raises is not None:
                self.tail = raises
                ins.then_inc(raises[0], 1)
            elif signal:
                self.tail = None
                self.count += 1
                ins.then_inc(self.sem, 1)
            return self.now()

    def issue(engine, op):
        return {
            "tt": lambda *a, **k: engine.tensor_tensor(*a, **k),
            "ts": lambda *a, **k: engine.tensor_scalar(*a, **k),
            "stt": lambda *a, **k: engine.scalar_tensor_tensor(*a, **k),
            "scan": lambda *a, **k: engine.tensor_tensor_scan(*a, **k),
            "copy": lambda *a, **k: engine.tensor_copy(*a, **k),
            "recip": lambda *a, **k: engine.reciprocal(*a, **k),
            "memset": lambda *a, **k: engine.memset(*a, **k),
            "rmax": lambda *a, **k: engine.reduce_max(*a, **k),
            "max8": lambda *a, **k: engine.max(*a, **k),
            "maxidx": lambda *a, **k: engine.max_index(*a, **k),
            "replace": lambda *a, **k: engine.match_replace(*a, **k),
            "act": lambda *a, **k: engine.activation(*a, **k),
            "mm": lambda *a, **k: engine.matmul(*a, **k),
            "tr": lambda *a, **k: engine.transpose(*a, **k),
        }[op]

    def sem(name):
        return es.enter_context(nc.semaphore(name))

    def sb(name, cols, dt=f32):
        return es.enter_context(nc.sbuf_tensor(name, [P, cols], dt))

    ring = sb("ring", RING * SLOT)
    f32r = mybir.dt.float32r
    UH = sb("u_high", KT * T, f32r)[:, :].rearrange("p (k t) -> p k t", t=T)
    UL = sb("u_low", KT * T, f32r)[:, :].rearrange("p (k t) -> p k t", t=T)
    const = sb("const", CONST_COLS)
    par1 = sb("par1", PAR1_COLS)
    par2 = sb("par2", PAR2_COLS)
    norms = sb("norms", KT)
    final2 = sb("final2", KT)
    rope = sb("rope", 2 * T)[:, :]
    extra = sb("taps", 2 * EXTRA)
    mod = sb("mod", MOD_UNITS)[:, :]
    raw_mod = sb("raw_mod", LAYERS * MOD_UNITS)[:, :]
    cond = sb("cond", KT)[:, :]
    router = sb("router", KT * EXPERTS)
    x_sb = sb("x_res", KT * T)
    rstd = sb("rstd", T)
    ones = sb("ones", P)
    small = sb("small", 512)
    y_sb = sb("y_mix", 12 * T)
    arena_base = nc.sbuf_base
    arena_cols = nc.sbuf_bytes_remaining // 4 - 64
    arena = sb("arena", arena_cols)

    def over_arena(name, col, cols):
        assert col + cols <= arena_cols
        t = nc.alloc_sbuf_tensor_at(name, [P, cols], f32r, offset=arena_base + 4 * col)
        return t[:, :]

    SPLIT = 2 * GROUP
    split_at = arena_cols - 2 * SPLIT * UNIT
    WH = over_arena("w_high", split_at, SPLIT * UNIT).rearrange("p (b n) -> p b n", n=UNIT)
    WL = over_arena("w_low", split_at + SPLIT * UNIT, SPLIT * UNIT).rearrange("p (b n) -> p b n", n=UNIT)
    y_at = 0
    YH = over_arena("y_high", y_at, 12 * T).rearrange("p (k t) -> p k t", t=T)
    YL = over_arena("y_low", y_at + 12 * T, 12 * T).rearrange("p (k t) -> p k t", t=T)
    hid_at = 24 * T
    HH = over_arena("hid_high", hid_at, 3 * T)
    HL = over_arena("hid_low", hid_at + 3 * T, 3 * T)
    psum = [es.enter_context(nc.psum_tensor(f"bank{b}", [P, 512], f32)) for b in range(8)]

    pos = small[:, 256:512]
    X = x_sb[:, :].rearrange("p (k t) -> p k t", t=T)
    Y = y_sb[:, :].rearrange("p (k t) -> p k t", t=T)

    def c_(name):
        return const[:, CONST[name]]

    def p1(name, j=None):
        s = PAR1[name]
        return par1[:, s] if j is None else par1[:, s.start + j:s.start + j + 1]

    def p2(name, j=None):
        s = PAR2[name]
        return par2[:, s] if j is None else par2[:, s.start + j:s.start + j + 1]

    class Space:

        def __init__(self, start=0):
            self.at = start

        def __call__(self, cols):
            self.at += cols
            assert self.at <= arena_cols, (self.at, arena_cols)
            return arena[:, self.at - cols:self.at]

    PE = Queue(nc.tensor, "s_pe", False)
    V = Queue(nc.vector, "s_dve", True)
    A = Queue(nc.scalar, "s_act", True)
    work = [PE, V, A]
    s_slot = [sem(f"s_slot{k}") for k in range(RING)]
    s_done = sem("s_group_done")
    s_in = sem("s_inputs")
    s_par = sem("s_params")
    s_const = sem("s_const")
    s_out = sem("s_out")
    s_up = sem("s_ff_up")
    s_down = sem("s_ff_down")
    ff_sems = {conv: tuple(sem(f"s_ff_{who}_{kind}") for who in ("act", "dve", "cut_act", "cut_dve"))
               for conv, kind in ((True, "conv"), (False, "plain"))}

    free = [()] * 8
    last_done = [None]

    def join():
        marks = [m for m in last_done if m] + [q.now() for q in work if q.count]
        for q in work:
            q.wait(*[m for m in marks])
        for b in range(8):
            free[b] = ()
        for b in range(SPLIT):
            read_by[b] = None

    def restart():
        join()
        A("act", small[:, 0:1], small[:, 0:1], Copy)
        join_engines = [q.engine.engine for q in work]
        nc.multi_engine_barrier(join_engines)
        for q in work:
            q.engine.sem_clear(q.sem)
        nc.multi_engine_barrier(join_engines)
        for q in work:
            q.count, q.passed, q.tail = 0, {}, None
        for b in range(8):
            free[b] = ()

    def weight_stream():
        def load(g, slot):
            nc.sync.dma_start(ring[:, slot * SLOT:(slot + 1) * SLOT],
                              a_weights[bass.ds(g, 1), :, :].rearrange("o p n -> p (o n)"))\
                .then_inc(s_slot[slot], 16)
        for g in range(RING):
            load(g, g)
        with nc.sync.Fori(0, (ALL_GROUPS - RING) // RING) as i:
            for j in range(RING):
                nc.sync.wait_ge(s_done, i * RING + (j + 1))
                load(i * RING + (RING + j), j)
        for g in range(ALL_GROUPS - (ALL_GROUPS - RING) % RING, ALL_GROUPS):
            nc.sync.wait_ge(s_done, g - RING + 1)
            load(g, g % RING)

    class Stream:

        def __init__(self, group0, end, layer=None):
            self.group0, self.layer, self.split_to, self.end = group0, layer, 0, end

        def scaled(self, per_layer, n):
            return n if self.layer is None else self.layer * per_layer + n

        def arrived(self, g):
            n = (self.group0 + g) // RING + 1
            slot = (self.group0 + g) % RING
            return (s_slot[slot], self.scaled(16 * (LAYER1_GROUPS // RING), 16 * n))

        def weights(self, u):
            g = u // GROUP
            at = ((self.group0 + g) % RING) * SLOT + (u % GROUP) * UNIT
            return ring[:, at:at + UNIT]

        def extra(self, g):
            at = ((self.group0 + g) % RING) * SLOT + GROUP * UNIT
            return ring[:, at:at + EXTRA]

        def done(self, g):
            return (s_done, self.scaled(LAYER1_GROUPS, self.group0 + g + 1))

    ready = {}

    def need(queue, st, u):
        g = u // GROUP
        if ready.get((id(queue), id(st))) != g:
            queue.wait(st.arrived(g))
            ready[id(queue), id(st)] = g

    read_by = [None] * SPLIT
    parts_ready = {}

    def split(st, u):
        for v in range(st.split_to, min(u + 1, st.end)):
            b = v % SPLIT
            w = st.weights(v)
            need(A, st, v)
            t = A("act", WH[:, b, :], w, Copy, after=(read_by[b],))
            need(V, st, v)
            closes = v % GROUP == GROUP - 1
            t = V("tt", WL[:, b, :], w, WH[:, b, :].bitcast(f32), SUB, after=(t, read_by[b]),
                  raises=st.done(v // GROUP) if closes else None)
            if closes:
                last_done[0] = t
            parts_ready[id(st), v] = t
            st.split_to = v + 1

    AHEAD = 4

    def mm(out, lhsT, rhs, start, stop, after=(), signal=False, loose=False):
        return PE("mm", out, lhsT, rhs, start=start, stop=stop, after=after, signal=signal,
                  skip_group_check=loose)

    def mm3(out, a, b, start, stop, signal=False, loose=False):
        (ah, al), (bh, bl) = a, b
        mm(out, ah, bh, start, False, loose=loose)
        mm(out, ah, bl, False, False, loose=loose)
        return mm(out, al, bh, False, stop, signal=signal, loose=loose)

    def last_mm(st, u, out, lhsT, rhs, start, stop, loose=False):
        if u % GROUP == GROUP - 1:
            nc.tensor.matmul(out, lhsT, rhs, start=start, stop=stop, skip_group_check=loose)\
                .then_inc(s_done, 1)
            last_done[0] = st.done(u // GROUP)
            return last_done[0]
        return mm(out, lhsT, rhs, start, stop, signal=True, loose=loose)

    def parts(st, u, cols):
        b = u % SPLIT
        return (WH[:, b, cols], WL[:, b, cols])

    def project(st, u, bank, half):
        split(st, u + AHEAD)
        PE.wait(parts_ready[id(st), u])
        out = psum[bank][:, half * T:(half + 1) * T]
        for k in range(KT):
            tok = mm3(out, parts(st, u, slice(k * P, (k + 1) * P)), (UH[:, k, :], UL[:, k, :]),
                      k == 0, k == KT - 1, signal=k == KT - 1)
        read_by[u % SPLIT] = tok
        return tok

    def project_tokens(st, u, bank):
        assert u % 2 == 0
        split(st, u + AHEAD)
        PE.wait(parts_ready[id(st), u + 1])
        b = u % SPLIT
        for a in range(HALVES):
            out = psum[bank][:, a * T:(a + 1) * T]
            ts_ = slice(a * P, (a + 1) * P)
            for k in range(KT):
                ks = slice(k * P, (k + 1) * P)
                tok = mm3(out, (UH[:, k, ts_], UL[:, k, ts_]), (WH[:, b:b + 2, ks], WL[:, b:b + 2, ks]),
                          k == 0, k == KT - 1, signal=k == KT - 1 and a == HALVES - 1)
            if a == 0:
                split(st, u + 1 + AHEAD)
        read_by[b] = read_by[b + 1] = tok
        return tok

    def mm_u(out, k, other, cols, start, stop, signal, u_first):
        for n, part in enumerate((UH, UL)):
            x = part[:, k, cols].bitcast(f32)
            lt, r_ = (x, other) if u_first else (other, x)
            tok = mm(out, lt, r_, start and n == 0, stop and n == 1, signal=signal and n == 1)
        return tok

    turn = [0]

    def copy_out(out, src, after):
        turn[0] += 1
        if turn[0] % 2:
            return A("act", out, src, Copy, after=after)
        return V("copy", out, src, after=after)

    class Beside:

        def __init__(self, st, banks):
            self.st, self.banks, self.jobs, self.made, self.held = st, banks, [], 0, []

        def add(self, u0, n, dst, act=None):
            for j in range(0, n, 2):
                self.jobs.append((u0 + j, dst[:, j:min(j + 2, n), :].rearrange("p k t -> p (k t)"), act, False))

        def add_tokens(self, u0, n, dst):
            for j in range(0, n, 2):
                self.jobs.append((u0 + j, dst[:, :, j * P:(j + 2) * P], None, True))

        def clear(self):
            for bank, dst, act, tok in self.held:
                src = psum[bank][:, 0:dst.shape[-1] if len(dst.shape) == 2 else 2 * T]
                if len(dst.shape) == 3:
                    src = src.rearrange("p (a c) -> p a c", a=2)
                free[bank] = (copy_out(dst, src, (tok,)) if act is None else A("act", dst, src, act, after=(tok,)),)
            self.held = []

        def __call__(self, n):
            self.clear()
            for _ in range(min(n, len(self.jobs))):
                u, dst, act, tokens = self.jobs.pop(0)
                bank = self.banks[self.made % len(self.banks)]
                if bank in [h[0] for h in self.held]:
                    self.clear()
                PE.wait(*free[bank])
                if tokens:
                    tok = project_tokens(self.st, u, bank)
                else:
                    for h in range(dst.shape[-1] // T):
                        tok = project(self.st, u + h, bank, h)
                self.held.append((bank, dst, act, tok))
                self.made += 1

        def finish(self):
            self(len(self.jobs))
            self.clear()

    def split_u(src, after):
        for h in range(2):
            ks = slice(4 * h, 4 * h + 4)
            t = A("act", UH[:, ks, :], src[:, ks, :], Copy, after=after)
            V("tt", UL[:, ks, :], src[:, ks, :], UH[:, ks, :].bitcast(f32), SUB, after=(t,))

    def rms(src, eps, g_of, add_of=None, out=None, meanwhile=lambda: None):
        sq = arena[:, 0:KT * T].rearrange("p (k t) -> p k t", t=T)
        un = out if out is not None else arena[:, KT * T:2 * KT * T].rearrange("p (k t) -> p k t", t=T)
        t0 = A("act", sq[:, 0:4, :], src[:, 0:4, :], Square, after=(V.now(),))
        t1 = A("act", sq[:, 4:8, :], src[:, 4:8, :], Square)
        for k in range(KT):
            tok = mm(psum[7][:, 0:T], ones[:, :], sq[:, k, :], k == 0, k == KT - 1,
                     after=(t0 if k < 4 else t1,), signal=k == KT - 1)
        meanwhile()
        t = V("ts", rstd[:, :], psum[7][:, 0:T], 1.0 / D, eps, MUL, ADD, after=(tok,))
        t = A("act", rstd[:, :], rstd[:, :], Sqrt, after=(t,))
        V("recip", rstd[:, :], rstd[:, :], after=(t,))
        for k in range(KT):
            t = V("stt", un[:, k, :], src[:, k, :], g_of(k), rstd[:, :], MUL, MUL)
            if add_of is not None:
                t = A("act", un[:, k, :], un[:, k, :], Ident, bias=add_of(k), after=(t,))
        if out is None:
            split_u(un, (t,))
        PE.wait(V.now(), A.now())

    FILL = (4, 0, 3, 2, 2, 3, 3)
    FILL_B = (1, 1, 1, 1, 1, 1, 0)
    FILL_C = (1, 1, 1)
    BRANCH_COLS = (12 + 20) * T + 3 * 1024
    FILL_G = (1, 2, 2, 2, 1)

    def branch_a(PA, st, beside):
        S = Space(14 * T)
        t4 = lambda ap: ap.rearrange("p (k t) -> p k t", t=T)
        Dif = t4(S(14 * T))
        V("tt", Dif[:, :, 1:T], PA[:, :, 0:T - 1], PA[:, :, 1:T], SUB)
        V("ts", Dif[:, :, 0:1], PA[:, :, 0:1], -1.0, None, MUL)
        for k in range(14):
            V("stt", PA[:, k, :], Dif[:, k, :], p1("mu", k), PA[:, k, :], MUL, ADD)
        beside(MOD_FIRST)
        mixed = V.now()
        S = Space(14 * T)
        R, K, VT, WA, GD = PA[:, 0:4, :], PA[:, 4:8, :], PA[:, 8:12, :], PA[:, 12, :], PA[:, 13, :]
        g_t, a_t, lw = t4(S(4 * T)), t4(S(4 * T)), t4(S(4 * T))
        kk, cw = t4(S(4 * T)), t4(S(4 * T))
        tmp = t4(Space(S.at)(4 * T))
        A("act", WA[0:64, :], WA[0:64, :], Tanh, after=(mixed,))
        low = A("act", GD[:, :], GD[:, :], Sigmoid)
        lora = st.weights(LOW_UNIT)
        need(PE, st, LOW_UNIT)
        w_up = lora[0:64, 0:512]
        a_up = lora[64:128, 0:512]
        g_up = lora[:, 512:1024]
        for m in range(4):
            b = m // 2
            o = slice((m % 2) * T, (m % 2 + 1) * T)
            cs = slice(m * P, (m + 1) * P)
            mm(psum[b][:, o], w_up[:, cs], WA[0:64, :], True, True, after=(low,))
            mm(psum[2 + b][:, o], a_up[:, cs], WA[64:128, :], True, True)
            if m < 3:
                mm(psum[4 + b][:, o], g_up[:, cs], GD, True, True)
            else:
                nc.tensor.matmul(psum[4 + b][:, o], g_up[:, cs], GD, start=True, stop=True)\
                    .then_inc(s_done, 1)
                up = last_done[0] = st.done(LOW_UNIT // GROUP)
        beside(FILL[0])
        for m in range(4):
            o = slice((m % 2) * T, (m % 2 + 1) * T)
            A("act", lw[:, m, :], psum[m // 2][:, o], Sigmoid, bias=p1("w0", m), after=(up,))
            A("act", a_t[:, m, :], psum[2 + m // 2][:, o], Sigmoid, bias=p1("a0", m))
            if m % 2:
                A("act", g_t[:, m - 1:m + 1, :].rearrange("p k t -> p (k t)"), psum[4 + m // 2][:, :], Copy)
        sig = A.now()
        V("ts", lw, lw, -float(np.exp(-0.5)), None, MUL, after=(sig,))
        for m in range(4):
            V("scan", cw[:, m, :], c_("chunk_mask"), lw[:, m, :], 0.0, MUL, ADD)
        for m in range(4):
            V("ts", kk[:, m, :], K[:, m, :], p1("k_k", m), None, MUL)
        t = V("tt", tmp, kk, kk, MUL)
        for m in range(4):
            tok = mm(psum[(6, 0)[m // 2]][:, (m % 2) * T:(m % 2 + 1) * T], c_("pair_blocks"), tmp[:, m, :],
                     True, True, after=(t,), signal=True)
        beside(FILL[1])
        for b in range(2):
            V("ts", tmp[:, 2 * b:2 * b + 2, :].rearrange("p k t -> p (k t)"), psum[(6, 0)[b]][:, :],
              1e-24, None, MAX, after=(tok,))
        t = A("act", tmp, tmp, Sqrt, after=(V.now(),))
        V("recip", tmp, tmp, after=(t,))
        V("tt", kk, kk, tmp, MUL)
        omka = small[:, 0:4]
        V("ts", omka, p1("k_a"), -1.0, 1.0, MUL, ADD)
        for m in range(4):
            V("ts", tmp[:, m, :], a_t[:, m, :], p1("k_a", m), omka[:, m:m + 1], MUL, ADD)
        V("tt", K, K, tmp, MUL)
        for m in range(4):
            V("stt", tmp[:, m, :], R[:, m, :], p1("r_k", m), K[:, m, :], MUL, MUL)
        t = V.now()
        for m in range(4):
            tok = mm(psum[m // 2][:, (m % 2) * T:(m % 2 + 1) * T], c_("pair_blocks"), tmp[:, m, :],
                     True, True, after=(t, sig), signal=True)
        beside(FILL[2])
        e = A("act", tmp, cw, Exp, scale=-1.0, after=(tok, V.now()))
        V("tt", a_t, a_t, kk, MUL)
        V("tt", a_t, a_t, tmp, MUL, after=(e,))
        V("tt", K, K, tmp, MUL)
        t = V("tt", lw, cw, lw, SUB)
        e = A("act", lw, lw, Exp, after=(t,))
        V("tt", kk, kk, lw, MUL, after=(e,))
        e = A("act", cw, cw, Exp, after=(V.now(),))
        V("tt", R, R, cw, MUL, after=(e,))
        bonus = lw
        for b in range(2):
            V("tt", bonus[:, 2 * b:2 * b + 2, :], psum[b][:, :].rearrange("p (k t) -> p k t", t=T),
              VT[:, 2 * b:2 * b + 2, :], MUL)
        at, bt, kt, rt, Dc = kk, a_t, K, R, cw
        join()
        S2 = S
        beside.out()
        tokm = []
        for n, src in enumerate((bt, kt, VT)):
            dst = S2(2 * 512).rearrange("p (a c) -> p a c", a=2)
            for a in range(2):
                b = 2 * n + a
                for m in range(4):
                    tok = PE("tr", psum[b][:, m * P:(m + 1) * P], src[:, m, a * P:(a + 1) * P],
                             c_("ident"), signal=m == 3)
                free[b] = (copy_out(dst[:, a, :], psum[b][:, :], (tok,)),)
            tokm.append(dst)
        BT, KTk, VTk = tokm
        join()
        h8 = lambda ap: ap.rearrange("p (h c) -> p h c", c=P)
        TT = [h8(S2(1024)) for _ in range(2)]
        RB = [h8(S2(1024)) for _ in range(2)]
        keep = S2.at
        RK = h8(S2(1024))
        AK = h8(Y[:, 4:8, :].rearrange("p k t -> p (k t)"))
        AKV = [Y[:, 8 + 2 * a:10 + 2 * a, :].rearrange("p k t -> p (k t)") for a in range(2)]
        names = ("N16", "NT16", "M32", "M64", "N2", "N2T", "Pm")
        spare = {n: PA[:, 8 + 2 * j:10 + 2 * j, :].rearrange("p k t -> p (k t)")
                 for j, n in enumerate(("M32", "M64", "Pm"))}
        tmps = [{n: (spare[n] if par and n in spare else S2(512)).rearrange("p (h c) -> p h c", c=P)
                 for n in names} for par in range(2)]
        for w in tmps:
            w["N4"], w["N4T"], w["N8"] = w["N16"], w["NT16"], w["N2T"]
            w["Tm"], w["Z"] = w["N16"], w["NT16"]

        def gram(bank, lt, rt_, par, a, after=()):
            rows = slice(64 * par, 64 * par + 64)
            cs = slice(a * P, (a + 1) * P)
            for m in range(4):
                tok = mm(psum[bank][:, m * P:(m + 1) * P], lt[rows, m, cs], rt_[rows, m, cs], True, True,
                         after=tuple(after) + tuple(free[bank]), signal=m == 3)
            return tok

        def b4(name):
            return c_(name).rearrange("p (o c) -> p o c", o=1).to_broadcast([P, 4, P])

        def ps4(bank):
            return psum[bank][:, :].rearrange("p (h c) -> p h c", c=P)

        beside(0)
        beside.out()
        for a in range(2):
            made = {}
            used = {}
            bank = 0

            def grams(lt, r_, outs):
                nonlocal bank
                for par in range(2):
                    tok = gram(bank, lt, r_, par, a)
                    for dst, mask in outs:
                        whole = {"AK": AK, "RB": RB[a], "RK": RK}.get(dst)
                        o = tmps[par][dst] if whole is None else whole[:, par:8:2, :]
                        t = made[par, dst] = V("tt", o, ps4(bank), b4(mask), MUL, after=(tok,))
                    free[bank] = (t,)
                    bank = (bank + 1) % 7
                    if dst == "NT16":
                        made[par, "Pm"] = V("tt", tmps[par]["Pm"], tmps[par]["NT16"], b4("ident"), ADD)
            grams(bt, at, (("NT16", "up16_neg"),))
            grams(at, bt, (("N16", "low16_neg"), ("M32", "low32_neg"), ("M64", "low64_neg")))

            def product(par, slot, lt, r_, out, add=None, over=()):
                w = tmps[par]
                bank = 4 * par + slot
                need_ = (made[par, lt], made[par, r_]) + tuple(free[bank])
                for m in range(4):
                    tok = mm(psum[bank][:, m * P:(m + 1) * P], w[lt][:, m, :], w[r_][:, m, :], True, True,
                             after=need_, signal=m == 3)
                used[par, lt] = used[par, r_] = tok
                o = w[out] if isinstance(out, str) else out
                after = (tok,) + tuple(used[par, n] for n in over if (par, n) in used)
                if add is None:
                    t = A("act", o, ps4(bank), Copy, after=after)
                else:
                    t = V("tt", o, ps4(bank), w[add], ADD, after=after)
                free[bank] = (t,)
                made[par, out if isinstance(out, str) else "TT"] = t

            def turned(par, slot, src, out, over=()):
                w = tmps[par]
                bank = 4 * par + slot
                for m in range(4):
                    tok = PE("tr", psum[bank][:, m * P:(m + 1) * P], w[src][:, m, :], c_("ident"),
                             after=(made[par, src],) + tuple(free[bank]), signal=m == 3)
                used[par, src] = tok
                after = (tok,) + tuple(used[par, n] for n in over if (par, n) in used)
                made[par, out] = A("act", w[out], ps4(bank), Copy, after=after)
                free[bank] = (made[par, out],)

            both = range(2)
            beside(2)
            for par in both:
                product(par, 0, "NT16", "N16", "N2")
                product(par, 1, "N16", "NT16", "N2T")
            grams(kt, at, (("AK", "strict_up"),))
            for par in both:
                product(par, 0, "N2T", "N2", "N4", over=("N16",))
                product(par, 1, "N2", "N2T", "N4T", over=("NT16", "N16"))
            for par in both:
                product(par, 2, "N2", "Pm", "Pm", add="Pm", over=("Pm",))
                product(par, 0, "N4T", "N4", "N8", over=("N2T", "N2"))
            grams(bt, rt, (("RB", "incl_up"),))
            for par in both:
                product(par, 2, "N4", "Pm", "Pm", add="Pm", over=("Pm",))
            grams(kt, rt, (("RK", "incl_up"),))
            beside(2)
            for par in both:
                product(par, 2, "N8", "Pm", "Pm", add="Pm", over=("Pm",))
            for m_, dst in (("M32", "Pm"), ("M64", TT[a][:, :, :])):
                beside(2)
                for par in both:
                    turned(par, 0, "Pm", "Tm", over=("N4", "Tm"))
                    product(par, 1, m_, "Pm", "Z", over=("N4T", "Z"))
                for par in both:
                    product(par, 2, "Tm", "Z", dst if isinstance(dst, str) else dst[:, par:8:2, :], add="Pm",
                            over=("Pm",))
            for h in range(8):
                tok = mm(psum[3][:, h * 64:(h + 1) * 64], AK[:, h, :], VTk[:, a, h * 64:(h + 1) * 64],
                         True, True, after=(V.now(),) + tuple(free[3]), signal=h == 7)
            free[3] = (A("act", AKV[a], psum[3][:, :], Copy, after=(tok,)),)
            for h in range(8):
                tok = mm(psum[3][64 * (h % 2):64 * (h % 2) + 64, (h // 2) * P:(h // 2 + 1) * P],
                         VTk[:, a, h * 64:(h + 1) * 64], RK[:, h, :], True, True,
                         after=(V.now(),) + tuple(free[3]), signal=h == 7)
            free[3] = (A("act", Y[:, 0:4, a * P:(a + 1) * P], ps4(3), Copy, after=(tok,)),)
            if a == 0:
                lower_bounds()
            if a:
                beside.out()
                beside(0)
            V.wait(PE.now())
            A.wait(PE.now())
        join()
        S4 = Space(keep)
        state = S4(512).rearrange("p (m c) -> p m c", c=P)
        Wv = S4(512)
        Uv = S4(512)
        sd = S4(512).rearrange("p (m c) -> p m c", c=P)
        V("memset", state, 0.0)
        V("memset", Wv, 0.0)
        ycols = Y[:, 0:4, :]
        for c in range(NCH):
            a, par = c // 2, c % 2
            rows = slice(64 * par, 64 * par + 64)
            tcs = slice(c * CH, (c + 1) * CH)
            loc = slice(64 * par, 64 * par + 64)
            for m in range(4):
                tok = mm(psum[0][:, m * P:(m + 1) * P], at[:, m, a * P:(a + 1) * P], state[:, m, :],
                         True, True, after=(V.now(), A.now()), signal=m == 3)
            t = V("tt", Wv[rows, :], psum[0][rows, :], AKV[a][rows, :], ADD, after=(tok,))
            for h in range(8):
                tok = mm(psum[1][:, h * 64:(h + 1) * 64], TT[a][:, h, :], Wv[:, h * 64:(h + 1) * 64],
                         True, True, after=(t, A.now()), signal=h == 7)
            beside(FILL[3])
            tu = A("act", Uv, psum[1][:, :], Copy, scale=-1.0, after=(tok,))
            for m in range(4):
                o = psum[2][:, m * CH:(m + 1) * CH]
                mm(o, state[:, m, :], rt[:, m, tcs], True, False, after=(tu,) if m == 0 else (), loose=True)
                for hp in range(2):
                    h = 2 * m + hp
                    oh = psum[2][64 * hp:64 * hp + 64, m * CH:(m + 1) * CH]
                    tok = mm(oh, Uv[:, h * 64:(h + 1) * 64], RB[a][:, h, loc], False, True, loose=True,
                             signal=m == 3 and hp == 1)
            beside.out()
            V("tt", ycols[:, :, tcs], psum[2][:, 0:4 * CH].rearrange("p (m t) -> p m t", t=CH),
              ycols[:, :, tcs], ADD, after=(tok,))
            if c < NCH - 1:
                for m in range(4):
                    o = psum[3][:, m * P:(m + 1) * P]
                    cs = slice(m * P, (m + 1) * P)
                    mm(o, BT[rows, a, cs], Uv[rows, cs], True, False)
                    tok = mm(o, KTk[rows, a, cs], VTk[rows, a, cs], False, True, signal=m == 3)
                beside(FILL[4])
                V("tt", sd, ps4(3), b4("pair_blocks"), MUL, after=(tok,))
                V("tt", sd, sd, state, ADD)
                end = (c + 1) * CH - 1
                V("tt", state, sd, Dc[:, :, end:end + 1].to_broadcast([P, 4, P]), MUL)
        S5 = Space(S4.at)
        q = t4(S5(4 * T))
        t = V.now()

        def head_mean(src, after):
            for m in range(4):
                tok = mm(psum[4 + m // 2][:, (m % 2) * T:(m % 2 + 1) * T], c_("pair_mean"), src[:, m, :],
                         True, True, after=after, signal=True)
            return tok
        tok = head_mean(ycols, (t,))
        beside(FILL[5])
        for b in range(2):
            V("tt", ycols[:, 2 * b:2 * b + 2, :], ycols[:, 2 * b:2 * b + 2, :],
              psum[4 + b][:, :].rearrange("p (k t) -> p k t", t=T), SUB, after=(tok,))
        t = V("tt", q, ycols, ycols, MUL)
        tok = head_mean(q, (t,))
        beside(FILL[6])
        for b in range(2):
            V("ts", q[:, 2 * b:2 * b + 2, :].rearrange("p k t -> p (k t)"), psum[4 + b][:, :], 64e-5, None,
              ADD, after=(tok,))
        t = A("act", q, q, Sqrt, after=(V.now(),))
        V("recip", q, q, after=(t,))
        V("tt", ycols, ycols, q, MUL)
        for m in range(4):
            V("ts", ycols[:, m, :], ycols[:, m, :], p1("gn_g", m), p1("gn_b", m), MUL, ADD)
        V("tt", ycols, ycols, bonus, ADD)
        V("tt", ycols, ycols, g_t, MUL)
        join()

    bounds_at = [small[:, 8 + 4 * n:12 + 4 * n] for n in range(7)]

    def lower_bounds():
        mx, e0, e1, lb, lnlb, omlb, flg = bounds_at
        lg = p1("lb_logits")
        V("tt", mx, lg[:, 0:4], lg[:, 4:8], MAX)
        V("tt", e0, lg[:, 0:4], mx, SUB)
        t = V("tt", e1, lg[:, 4:8], mx, SUB)
        A("act", e0, e0, Exp, after=(t,))
        t = A("act", e1, e1, Exp)
        V("tt", e0, e0, e1, ADD, after=(t,))
        V("recip", e0, e0)
        V("tt", lb, e1, e0, MUL)
        V("ts", lb, lb, p1("lb_flag"), None, MUL)
        V("ts", omlb, lb, -1.0, 1.0, MUL, ADD)
        V("ts", flg, lb, 2.0 ** -63, None, ALU.is_ge)
        V("ts", flg, flg, 1.0, 1e30, SUB, MUL)
        t = V("ts", lnlb, lb, 2.0 ** -63, None, MAX)
        t = A("act", lnlb, lnlb, Ln, after=(t,))
        V("tt", lnlb, lnlb, flg, ADD, after=(t,))

    def branch_b(PB, VB, S, beside):
        t4 = lambda ap: ap.rearrange("p (k t) -> p k t", t=T)
        Q, F, Gt = PB[:, 0:4, :], PB[:, 4:8, :], PB[:, 8:12, :]
        lb, lnlb, omlb = bounds_at[3:6]
        s1, s2, s3, kin, bcum = (t4(S(4 * T)) for _ in range(5))
        A("act", s1, F, Abs, after=(V.now(),))
        t = A("act", s1, s1, Exp, scale=-1.0)
        t = A("act", s1, s1, Ln, bias=1.0)
        beside(1)
        t = V("stt", kin, F, 0.0, s1, MAX, ADD, after=(t,))
        t = A("act", kin, kin, Exp, scale=-1.0, after=(t,))
        for m in range(4):
            V("ts", kin[:, m, :], kin[:, m, :], omlb[:, m:m + 1], None, MUL, after=(t,))
        beside(1)
        t = V("ts", s2, F, -43.0, None, MAX)
        t = A("act", s2, s2, Exp, scale=-1.0, after=(t,))
        for m in range(4):
            t = A("act", s2[:, m, :], s2[:, m, :], Ln, bias=1.0, scale=lb[:, m:m + 1])
        V("stt", s3, F, 0.0, s1, ALU.min, SUB)
        V("tt", s3, s3, s2, ADD, after=(t,))
        for m in range(4):
            V("ts", s3[:, m, :], s3[:, m, :], lnlb[:, m:m + 1], None, MAX)
        beside(1)
        for m in range(4):
            V("scan", bcum[:, m, :], c_("chunk_mask"), s3[:, m, :], 0.0, MUL, ADD)
        sc = S(1024).rearrange("p (g c) -> p g c", c=P)
        tmp8 = S(1024).rearrange("p (g c) -> p g c", c=P)
        Xl = s1, s2
        read_x = [None, None]

        def halves_of(n, ap):
            h = 32 >> n
            v = ap.rearrange("p k (b s) -> p (k b) s", s=2 * h)
            return v[:, :, 0:h], v[:, :, h:2 * h], v[:, :, h - 1:h].to_broadcast([P, 4 * T // (2 * h), h])

        def distances(n):
            lo, hi, _ = halves_of(n, Xl[n % 2])
            blo, bhi, ref = halves_of(n, bcum)
            V("tt", lo, ref, blo, SUB, after=(read_x[n % 2],))
            t = V("tt", hi, bhi, ref, SUB)
            return A("act", Xl[n % 2], Xl[n % 2], Exp, after=(t,))

        def keys_queries(n, t):
            lo, hi, _ = halves_of(n, Xl[n % 2])
            V("tt", lo, lo, halves_of(n, kin)[0], MUL, after=(t,))
            return V("tt", hi, hi, halves_of(n, Q)[1], MUL)
        t = keys_queries(0, distances(0))
        for n in range(7):
            x = Xl[n % 2]
            following = distances(n + 1) if n + 1 < 6 else None
            toks = []
            for bk in range(2):
                for j in range(4):
                    m, a = 2 * bk + j // 2, j % 2
                    cs = slice(a * P, (a + 1) * P)
                    lt, r_ = (x, x) if n < 6 else (kin, Q)
                    tok = mm(psum[2 * (n % 2) + bk][:, j * P:(j + 1) * P], lt[:, m, cs], r_[:, m, cs],
                             True, True, after=(t,) + tuple(free[2 * (n % 2) + bk]), signal=j == 3)
                toks.append(tok)
            read_x[n % 2] = tok
            if following is not None:
                t = keys_queries(n + 1, following)
            for bk in range(2):
                src = psum[2 * (n % 2) + bk][:, :].rearrange("p (g c) -> p g c", c=P)
                msk = c_(f"level{n}").rearrange("p (o c) -> p o c", o=1).to_broadcast([P, 4, P])
                dst = (sc if n == 0 else tmp8)[:, 4 * bk:4 * bk + 4, :]
                free[2 * (n % 2) + bk] = (V("tt", dst, src, msk, MUL, after=(toks[bk],)),)
            if n:
                V("tt", sc, sc, tmp8, ADD)
            beside(FILL_B[n])
        assert S.at <= BRANCH_COLS
        b16 = bcum.rearrange("p k (c s) -> p (k c) s", s=CH)
        s16 = s3.rearrange("p k (c s) -> p (k c) s", s=CH)
        V("tt", s16, b16[:, :, CH - 1:CH].to_broadcast([P, 16, CH]), b16, SUB)
        t = A("act", s3, s3, Exp, after=(V.now(),))
        V("tt", s3, s3, kin, MUL, after=(t,))
        eb = kin
        t = A("act", eb, bcum, Exp, after=(V.now(), PE.now()))
        t = V("tt", Q, Q, eb, MUL, after=(t,))
        khat = tmp8.rearrange("p (a m) c -> p a m c", a=2)
        for a in range(2):
            for m in range(4):
                tok = PE("tr", psum[a][:, m * P:(m + 1) * P], s3[:, m, a * P:(a + 1) * P], c_("ident"),
                         after=(t,) + tuple(free[a]), signal=m == 3)
            free[a] = (V("copy", khat[:, a, :, :], psum[a][:, :].rearrange("p (m c) -> p m c", c=P),
                         after=(tok,)),)
        st = [None, s1.rearrange("p k t -> p (k t)")[:, 0:512], s1.rearrange("p k t -> p (k t)")[:, 512:1024],
              s2.rearrange("p k t -> p (k t)")[:, 0:512]]
        t = V.now()
        for c in range(NCH - 1):
            a, par = c // 2, c % 2
            rows = slice(64 * par, 64 * par + 64)
            for m in range(4):
                tok = mm(psum[2 + c][:, m * P:(m + 1) * P], khat[rows, a, m, :], VB[rows, a, m * P:(m + 1) * P],
                         True, True, after=(t,) + tuple(free[2 + c]), signal=m == 3)
            nxt = st[c + 1].rearrange("p (m c) -> p m c", c=P)
            if c == 0:
                V("copy", nxt, psum[2][:, :].rearrange("p (m c) -> p m c", c=P), after=(tok,))
            else:
                prev = st[c].rearrange("p (m c) -> p m c", c=P)
                end = (c + 1) * CH - 1
                V("tt", nxt, prev, eb[:, :, end:end + 1].to_broadcast([P, 4, P]), MUL)
                V("tt", nxt, nxt, psum[2 + c][:, :].rearrange("p (m c) -> p m c", c=P), ADD, after=(tok,))
        beside.clear()
        t = V.now()
        yb = Y[:, 4:8, :]
        for m in range(4):
            bank = psum[6 + m // 2]
            for a in range(2):
                at0 = (m % 2) * T + a * P
                mm(bank[:, at0:at0 + P], VB[:, a, m * P:(m + 1) * P], sc[:, 2 * m + a, :], True, False,
                   after=(t,) + tuple(free[6 + m // 2]), loose=True)
                for c in (2 * a, 2 * a + 1):
                    if c:
                        tok = mm(bank[:, at0 + (c % 2) * CH:at0 + (c % 2 + 1) * CH],
                                 st[c][:, m * P:(m + 1) * P], Q[:, m, c * CH:(c + 1) * CH], False, True,
                                 loose=True, signal=c == 3)
        for b in range(2):
            V("copy", yb[:, 2 * b:2 * b + 2, :], psum[6 + b][:, :].rearrange("p (k t) -> p k t", t=T),
              after=(tok,))
        head_rms_gate(yb, s3, s1, Gt, lambda m: p1("b_gn_g", m))
        join()

    def head_rms_gate(y, q, sg, Gt, gain):
        t = A("act", q, y, Square, after=(V.now(), PE.now()))
        sig = A("act", sg, Gt, Sigmoid)
        for m in range(4):
            tok = mm(psum[m // 2][:, (m % 2) * T:(m % 2 + 1) * T], c_("mean128"), q[:, m, :],
                     True, True, after=(t,) + tuple(free[m // 2]), signal=True)
        V("tt", sg, sg, Gt, MUL, after=(sig,))
        for b in range(2):
            V("ts", q[:, 2 * b:2 * b + 2, :].rearrange("p k t -> p (k t)"), psum[b][:, :], 1e-6, None,
              ADD, after=(tok,))
            free[b] = (V.now(),)
        t = A("act", q, q, Sqrt, after=(V.now(),))
        for m in range(4):
            V("stt", sg[:, m, :], y[:, m, :], gain(m), sg[:, m, :], MUL, MUL)
        V("recip", q, q, after=(t,))
        V("tt", y, sg, q, MUL)

    def branch_c(PC, VC, WI, S, beside, ahead):
        t4 = lambda ap: ap.rearrange("p (k t) -> p k t", t=T)
        rot = t4(S(8 * T))
        cosb = c_("rope_cos").rearrange("p (o t) -> p o t", o=1).to_broadcast([P, 8, T])
        for k in range(8):
            tok = mm(psum[k // 2][:, (k % 2) * T:(k % 2 + 1) * T], c_("swap32"), PC[:, k, :], True, True,
                     signal=True)
        V("tt", rot, PC, cosb, MUL)
        for b in range(4):
            sinb = c_("rope_sin").rearrange("p (o t) -> p o t", o=1).to_broadcast([P, 2, T])
            V("tt", PC[:, 2 * b:2 * b + 2, :], psum[b][:, :].rearrange("p (k t) -> p k t", t=T), sinb, MUL,
              after=(tok,))
        t = V("tt", rot, rot, PC, ADD)
        kd = t4(S(2 * T))
        for c in range(2):
            tok = mm(psum[4][:, c * T:(c + 1) * T], c_(f"dup{c}"), rot[:, 4, :], True, True, after=(t,),
                     signal=True)
        tok2 = mm(psum[5][:, 0:T], c_("dup0"), rot[:, 7, :], True, True, signal=True)
        t = V("copy", rot[:, 7, :], psum[5][:, 0:T], after=(tok2,))
        kd_t = A("act", kd.rearrange("p k t -> p (k t)"), psum[4][:, :], Copy, after=(tok,))
        free[4] = (kd_t,)
        beside.banks = (7, 4)
        beside(FILL_C[0])
        wis = small[:, 64:72]
        V("ts", wis, WI, 0.5 * 0.125, None, MUL)
        score = S(2 * T).rearrange("p (a s) -> p a s", s=T)
        work_ = S(2 * T).rearrange("p (a s) -> p a s", s=T)
        dotw = S(T)
        top8 = small[:, 80:88]
        for a in range(2):
            n = P * (a + 1)
            for h in range(4):
                rows = slice(64 * (h % 2), 64 * (h % 2) + 64)
                b = (5, 6)[h % 2]
                tok = mm(psum[b][:, (h // 2) * T:(h // 2) * T + n], rot[rows, 5 + h // 2, a * P:(a + 1) * P],
                         rot[rows, 7, 0:n], True, True, after=(t,) + tuple(free[b]), signal=True)
            for h in range(4):
                b = (5, 6)[h % 2]
                dst = score[:, a, 0:n] if h == 0 else dotw[:, 0:n]
                V("ts", dst, psum[b][:, (h // 2) * T:(h // 2) * T + n], 0.0, wis[:, 4 * a + h:4 * a + h + 1],
                  MAX, MUL, after=(tok,))
                if h:
                    V("tt", score[:, a, 0:n], score[:, a, 0:n], dotw[:, 0:n], ADD)
            free[5] = free[6] = (V.now(),)
            if a:
                beside(FILL_C[1])
            nonc = c_("noncausal")[:, a * T:a * T + n]
            V("tt", work_[:, a, 0:n], score[:, a, 0:n], nonc, ADD)
            for n8 in range(TOPK // 8):
                if n8 in (3, 6):
                    beside(1)
                V("max8", top8, work_[:, a, 0:n])
                V("replace", work_[:, a, 0:n], top8, work_[:, a, 0:n], -3e30)
            V("ts", work_[:, a, 0:n], work_[:, a, 0:n], -2e30, -1e30, ALU.is_gt, MUL)
            V("tt", work_[:, a, 0:n], work_[:, a, 0:n], nonc, ADD)
        beside(FILL_C[2])
        Ls = [S(8 * P * (a + 1)).rearrange("p (h s) -> p h s", s=P * (a + 1)) for a in range(2)]
        probs = S(8 * T)
        for a in range(2):
            n = P * (a + 1)
            for h in range(8):
                rows = slice(64 * (h % 2), 64 * (h % 2) + 64)
                b = 2 * (h % 2) + h // 4
                tok = mm(psum[b][:, (h // 2 % 2) * T:(h // 2 % 2) * T + n], rot[rows, h // 2, a * P:(a + 1) * P],
                         kd[rows, h // 4, 0:n], True, True, after=(kd_t,) + tuple(free[b]), signal=True)
            for h in range(8):
                b = 2 * (h % 2) + h // 4
                t = V("stt", Ls[a][:, h, :], psum[b][:, (h // 2 % 2) * T:(h // 2 % 2) * T + n], 0.125,
                      work_[:, a, 0:n], MUL, ADD, after=(tok,))
            for b in range(4):
                free[b] = (t,)
        beside(12)
        ahead()
        assert S.at <= BRANCH_COLS
        for a in range(2):
            n = P * (a + 1)
            L = Ls[a]
            probT = probs[:, 0:8 * n].rearrange("p (h s) -> p h s", s=n)
            nm, sm = (small[:, 96 + 16 * a + 8 * k:104 + 16 * a + 8 * k] for k in range(2))
            t = V("rmax", nm, L, axis=AX.X, negate=True)
            for h in range(8):
                t = A("act", L[:, h, :], L[:, h, :], Exp, bias=nm[:, h:h + 1], accum_out=sm[:, h:h + 1],
                      after=(t,) if h == 0 else ())
            V("recip", sm, sm, after=(A.now(),))
            t = V("tt", L, L, sm.rearrange("p (h o) -> p h o", o=1).to_broadcast([P, 8, n]), MUL)
            beside.clear()
            for j in range(2 * (a + 1)):
                b = 4 + j
                for i in range(4):
                    idx = 4 * j + i
                    h, s = idx // (a + 1), idx % (a + 1)
                    tok = PE("tr", psum[b][:, i * P:(i + 1) * P], L[:, h, s * P:(s + 1) * P], c_("ident"),
                             after=(t,) + tuple(free[b]), signal=i == 3)
                dst = probT.rearrange("p h s -> p (h s)")[:, j * 512:(j + 1) * 512]
                free[b] = (copy_out(dst, psum[b][:, :], (tok, PE.now())),)
            pts = (V.now(), A.now())
            pt = probT.rearrange("p h (s q) -> p (h s) q", q=P)
            for h in range(8):
                rows = slice(64 * (h % 2), 64 * (h % 2) + 64)
                out = psum[0][rows, (h // 2) * P:(h // 2 + 1) * P]
                for s in range(a + 1):
                    tok = mm(out, VC[:, s, 64 * (h // 4):64 * (h // 4) + 64], pt[:, h * (a + 1) + s, :],
                             s == 0, s == a, after=pts + tuple(free[0]), signal=h == 7 and s == a)
            t = V("copy", Y[:, 8:12, a * P:(a + 1) * P], psum[0][:, :].rearrange("p (m q) -> p m q", q=P),
                  after=(tok,))
            free[0] = (t,)
        join()

    def feed_forward(group0, groups, layer, conv, before, dve0, up0, gates, scale_of, norm):
        join()
        s_a, s_v, s_ca, s_cv = ff_sems[conv]
        NA = 4 if conv else 2
        NV = 7 if conv else (4 if gates is not None else 3)
        NCA, NCV = (4 if conv else 3), 2
        zeros = small[:, 128:256]
        V("memset", zeros, 0.0)
        zt = V.now()
        for b in range(4):
            for c in range(4):
                mm(psum[b][:, c * P:(c + 1) * P], zeros, zeros, c == 0, False, after=(zt,), loose=True)
        at = [GATE_COLS]

        def buffers():
            at[0] += 2
            return [arena[:, (at[0] - 2 + n) * T:(at[0] - 1 + n) * T] for n in range(2)]
        CG, CV, SG, HD = buffers(), buffers(), buffers(), buffers()

        def at_layer(per_layer, v):
            return v if layer is None else layer * per_layer + v

        def token(kind, i, j, n):
            s, per, base = {"a": (s_a, NA, NA * before), "v": (s_v, NV, dve0), "ca": (s_ca, NCA, NCA * before),
                            "cv": (s_cv, NCV, NCV * before), "u": (s_up, 1, up0), "d": (s_down, 1, up0)}[kind]
            return (s, at_layer(FF_GROUPS * per, i * (RING * per) + (base + j * per + n)))

        def done(i, j):
            return (s_done, at_layer(LAYER1_GROUPS, i * RING + (group0 + j + 1)))

        def slot(j):
            return ((group0 + j) % RING) * SLOT

        def unit(j, n):
            return ring[:, slot(j) + n * UNIT:slot(j) + (n + 1) * UNIT]

        def halves(j, n, cols):
            b = GROUP * (j % 2) + n
            return (WH[:, b, cols], WL[:, b, cols])

        def passes(out, w, x, start, stop, loose=False):
            nc.tensor.matmul(out, w[0], x[0], start=start, stop=False, skip_group_check=loose)
            nc.tensor.matmul(out, w[0], x[1], start=False, stop=False, skip_group_check=loose)
            return nc.tensor.matmul(out, w[1], x[0], start=False, stop=stop, skip_group_check=loose)

        def cut(i, j, n, first):
            act, dve, b = nc.scalar, nc.vector, GROUP * (j % 2) + n
            arrived = (s_slot[(group0 + j) % RING],
                       at_layer(16 * (LAYER1_GROUPS // RING), i * 16 + 16 * ((group0 + j) // RING + 1)))
            if n == 0:
                act.wait_ge(*arrived)
                dve.wait_ge(*arrived)
            if not first:
                act.wait_ge(*(token("u", i, j - 2, 1) if n < 2 else token("d", i, j - 2, 1)))
            act.activation(WH[:, b, :], unit(j, n), Copy).then_inc(s_ca, 1)
            if n == 2 and conv:
                if not first:
                    act.wait_ge(*token("v", i, j - 2, NV))
                act.activation(extra[:, (j % 2) * EXTRA:(j % 2 + 1) * EXTRA],
                               ring[:, slot(j) + GROUP * UNIT:slot(j) + SLOT], Copy).then_inc(s_ca, 1)
            dve.wait_ge(*token("ca", i, j, NCA if n == 2 else n + 1))
            if not first:
                dve.wait_ge(*(token("u", i, j - 2, 1) if n < 2 else token("d", i, j - 2, 1)))
            ins = dve.tensor_tensor(WL[:, b, :], unit(j, n), WH[:, b, :].bitcast(f32), SUB)
            if n < 2:
                ins.then_inc(s_cv, 1)
            else:
                ins.then_inc(s_done, 1)

        def up(i, j, first):
            b, pe = psum[4 + j % 2], nc.tensor
            if not first:
                pe.wait_ge(*token("v", i, j - 2, 4 if conv else 2))
            for half in range(2):
                pe.wait_ge(*token("cv", i, j, half + 1))
                for k in range(KT):
                    ins = passes(b[:, half * T:(half + 1) * T], halves(j, half, slice(k * P, (k + 1) * P)),
                                 (UH[:, k, :], UL[:, k, :]), k == 0, k == KT - 1)
            ins.then_inc(s_up, 1)

        def down(i, j, last):
            pe, n = nc.tensor, j % 2
            pe.wait_ge(*done(i, j))
            pe.wait_ge(*token("a", i, j, NA))
            pe.wait_ge(*token("v", i, j, NV))
            ts_ = slice(n * T, (n + 1) * T)
            for dt in range(KT):
                ins = passes(psum[dt // 2][:, (dt % 2) * T:(dt % 2 + 1) * T],
                             halves(j, 2, slice(dt * P, (dt + 1) * P)), (HH[:, ts_], HL[:, ts_]),
                             False, last, loose=True)
            ins.then_inc(s_down, 1)

        def middle(i, j, first):
            n = j % 2
            pg, pv = (psum[4 + n][:, h * T:(h + 1) * T] for h in range(2))
            act, dve = nc.scalar, nc.vector
            chain = [0]
            ts_ = slice(n * T, (n + 1) * T)

            def v(op, *args, after=()):
                if chain[0]:
                    dve.wait_ge(*token("v", i, j, chain[0]))
                for tok in after:
                    dve.wait_ge(*tok)
                issue(dve, op)(*args).then_inc(s_v, 1)
                chain[0] += 1
            act.wait_ge(*token("u", i, j, 1))
            if not first:
                act.wait_ge(*token("v", i, j - 2, NV))
            free_hid = () if first else (token("d", i, j - 2, 1),)
            if conv:
                ex = extra[:, n * EXTRA:(n + 1) * EXTRA]
                act.wait_ge(*token("ca", i, j, NCA))
                act.activation(CG[n], pg, Ident, bias=ex[:, 3:4], scale=ex[:, 2:3]).then_inc(s_a, 1)
                act.activation(CV[n], pv, Ident, bias=ex[:, 7:8], scale=ex[:, 6:7]).then_inc(s_a, 1)
                for h, (c_buf, p_) in enumerate(((CG[n], pg), (CV[n], pv))):
                    for tap in (1, 0):
                        d = 2 - tap
                        v("stt", c_buf[:, d:T], p_[:, 0:T - d], ex[:, 4 * h + tap:4 * h + tap + 1],
                          c_buf[:, d:T], MUL, ADD, after=(token("a", i, j, 2),) if h == 0 and tap else ())
                act.wait_ge(*token("v", i, j, 4))
                act.activation(SG[n], CG[n], Sigmoid).then_inc(s_a, 1)
                v("tt", SG[n], SG[n], CG[n], MUL, after=(token("a", i, j, 3),))
                v("tt", HD[n], SG[n], CV[n], MUL)
            else:
                act.activation(SG[n], pg, Sigmoid).then_inc(s_a, 1)
                v("tt", SG[n], SG[n], pg, MUL, after=(token("a", i, j, 1),))
                v("tt", HD[n], SG[n], pv, MUL)
                if gates is not None:
                    e = (i * RING + j) // (FFE // P)
                    g = gates[:, e * T:(e + 1) * T] if isinstance(e, int) else gates[:, bass.ds(e * T, T)]
                    v("tt", HD[n], HD[n], g, MUL)
            act.wait_ge(*token("v", i, j, chain[0]))
            for tok in free_hid:
                act.wait_ge(*tok)
            act.activation(HH[:, ts_], HD[n], Copy).then_inc(s_a, 1)
            v("tt", HL[:, ts_], HD[n], HH[:, ts_].bitcast(f32), SUB, after=(token("a", i, j, NA),) + free_hid)

        def steps(i, j, first, more=True):
            up(i, j, first)
            if not (first and j == 0):
                down(i, j - 1, False)
            if more:
                for n in range(2):
                    cut(i, j + 1, n, first and j == 0)
            middle(i, j, first)
            if more:
                cut(i, j + 1, 2, first and j == 0)

        def first_cuts():
            for n in range(GROUP):
                cut(0, 0, n, True)
        norm(first_cuts)
        steps(0, 0, True)
        steps(0, 1, True)
        rounds = (groups - 3) // RING
        with nc.Fori(0, rounds, engines=(nc.tensor.engine, nc.vector.engine, nc.scalar.engine)) as i:
            for j in range(2, 2 + RING):
                steps(i, j, False)
        for g in range(2 + rounds * RING, groups):
            steps(rounds, g - rounds * RING, False, more=g < groups - 1)
        last = groups - 1 - rounds * RING
        down(rounds, last, True)
        last_done[0] = done(rounds, last)
        fin = token("d", rounds, last, 1)
        for dt in range(KT):
            src = psum[dt // 2][:, (dt % 2) * T:(dt % 2 + 1) * T]
            V("stt", X[:, dt, :], src, scale_of(dt), X[:, dt, :], MUL, ADD, after=(fin,) if dt == 0 else ())
        A.wait(fin)
        join()

    GATE_COLS = 8

    class Modulation:
        ROUND_UNITS = 2 * KT

        def __init__(self, st, u0):
            self.st, self.u0, self.taken, self.stage, self.turned = st, u0, 0, 0, 0

        def unit(self, j):
            return self.u0 + j + (1 if j >= MOD_FIRST else 0)

        def __call__(self, n):
            r = self.stage // 3
            if self.stage % 3 == 1:
                for i in range(4):
                    self.last = PE("tr", psum[7][:, i * P:(i + 1) * P], rope[:, i * P:(i + 1) * P], c_("ident"),
                                   after=(self.fetched,), signal=i == 3)
                self.stage += 1
            if self.stage % 3:
                return
            end = min(self.taken + n, (r + 1) * self.ROUND_UNITS, MOD_UNITS)
            for j in range(self.taken, end):
                u, k = self.unit(j), j % KT
                if j == r * self.ROUND_UNITS and r:
                    PE.wait(self.fetched)
                need(PE, self.st, u)
                w = self.st.weights(u)
                for h in range(2):
                    q = (2 * (j // KT) + h) % 4
                    args = (psum[7][32 * q:32 * q + 32, :], cond[:, k:k + 1].to_broadcast([P, 32]),
                            w[:, h * 512:(h + 1) * 512], k == 0, k == KT - 1)
                    if h == 0:
                        mm(*args)
                    else:
                        self.last = last_mm(self.st, u, *args)
                self.taken = j + 1

        def out(self):
            r = self.stage // 3
            if self.stage % 3 == 0 and self.taken == (r + 1) * self.ROUND_UNITS:
                self.fetched = A("act", rope, psum[7][:, :], Copy, after=(self.last,))
                self.stage += 1
            elif self.stage % 3 == 2:
                src = psum[7][:, :].rearrange("p (i q s) -> p q i s", i=4, q=4)[:, :, :, 0:1]
                dst = mod[:, 16 * r:16 * r + 16].rearrange("p (q i o) -> p q i o", q=4, o=1)
                self.fetched = A("act", dst, src, Copy, after=(self.last,))
                self.stage += 1

        def finish(self):
            while self.stage < 3 * MOD_UNITS // self.ROUND_UNITS:
                self(MOD_UNITS)
                self.out()

    def modulation(raw):
        V("tt", mod, raw, p2("ada_b"), ADD)
        for n, norm in ((1, "norm_mix"), (4, "norm_ffn")):
            V("stt", mod[:, 8 * n:8 * n + 8], mod[:, 8 * n:8 * n + 8], 1.0, p2(norm), ADD, MUL)

    def linear_attention(units, S, rope):
        t4 = lambda ap: ap.rearrange("p (k t) -> p k t", t=T)
        P2 = t4(S(20 * T))
        GV = S(2 * 512).rearrange("p (a c) -> p a c", a=2)
        RV = S(2 * 512).rearrange("p (a c) -> p a c", a=2)
        beside = units(P2, GV, RV)
        gq, gk, gr, rq, rk, rg = (P2[:, s:e, :] for s, e in ((0, 2), (2, 4), (4, 8), (8, 12), (12, 16), (16, 20)))
        mark = S.at
        la, eb, enb, s4 = t4(S(2 * T)), t4(S(2 * T)), t4(S(2 * T)), t4(S(2 * T))
        ga = S(T)
        wga = p2("w_ga").rearrange("p (k r) -> p k r", r=16)
        for k in range(KT):
            tok = mm_u(psum[0][0:16, 0:T], k, wga[:, k, :], slice(0, T), k == 0, k == KT - 1, k == KT - 1, False)
        t = V("copy", ga[0:16, :], psum[0][0:16, 0:T], after=(tok,))
        for m in range(2):
            tok = mm(psum[1][:, m * T:(m + 1) * T], p2("w_alpha")[0:16, m * P:(m + 1) * P], ga[0:16, :],
                     True, True, after=(t,), signal=True)
        beside(FILL_G[0])
        for m in range(2):
            V("ts", la[:, m, :], psum[1][:, m * T:(m + 1) * T], p2("b_alpha", m), None, ADD, after=(tok,))
        A("act", s4, la, Abs, after=(V.now(),))
        t = A("act", s4, s4, Exp, scale=-1.0)
        t = A("act", s4, s4, Ln, bias=1.0)
        V("stt", la, la, 0.0, s4, ALU.min, SUB, after=(t,))
        V("ts", la, la, 1.0 / 16.0, None, MUL)
        bc_ = s4
        for m in range(2):
            V("scan", bc_[:, m, :], c_("chunk_mask"), la[:, m, :], 0.0, MUL, ADD)
        t = A("act", eb, bc_, Exp, after=(V.now(),))
        t = A("act", enb, bc_, Exp, scale=-1.0)
        beside(FILL_G[1])
        kend = la
        split = lambda ap: ap.rearrange("p k (c s) -> p (k c) s", s=CH)
        V("tt", split(kend), split(bc_)[:, :, CH - 1:CH].to_broadcast([P, 8, CH]), split(bc_), SUB)
        e = A("act", kend, kend, Exp, after=(V.now(),))
        V("tt", kend, kend, gk, MUL, after=(e,))
        V("ts", gq, gq, 0.125, None, MUL)
        kb, qf, kf, qb = t4(S(2 * T)), t4(S(2 * T)), t4(S(2 * T)), s4
        V("tt", qb, gq, enb, MUL)
        V("tt", qf, gq, eb, MUL)
        V("tt", kf, gk, enb, MUL)
        t = V("tt", kb, gk, eb, MUL)
        ps4 = lambda b: psum[b][:, :].rearrange("p (h c) -> p h c", c=P)
        sc = S(1024).rearrange("p (m r a c) -> p m r a c", m=2, r=2, a=2)
        tmp = S(512).rearrange("p (g c) -> p g c", c=P)
        for par in range(2):
            rows = slice(64 * par, 64 * par + 64)
            for d, (lt, r_, mask) in enumerate(((kf, qf, "incl_up"), (kb, qb, "strict_low"))):
                b = 2 + 2 * d + par
                for m in range(2):
                    for a in range(2):
                        cs = slice(a * P, (a + 1) * P)
                        tok = mm(psum[b][:, (2 * m + a) * P:(2 * m + a + 1) * P], lt[rows, m, cs],
                                 r_[rows, m, cs], True, True, after=(t,), signal=m == 1 and a == 1)
                msk = c_(mask).rearrange("p (o c) -> p o c", o=1).to_broadcast([P, 4, P])
                V("tt", tmp, ps4(b), msk, MUL, after=(tok,))
                for m in range(2):
                    dst = sc[:, m, par, :, :]
                    src = tmp[:, 2 * m:2 * m + 2, :]
                    V("copy", dst, src) if d == 0 else V("tt", dst, dst, src, ADD)
        beside(FILL_G[2])
        kt_ = S(512).rearrange("p (a c) -> p a c", a=2)
        for a in range(2):
            for m in range(2):
                tok = PE("tr", psum[6][:, (2 * a + m) * P:(2 * a + m + 1) * P], kend[:, m, a * P:(a + 1) * P],
                         c_("ident"), after=(V.now(),), signal=True)
        t = V("copy", kt_, psum[6][:, :].rearrange("p (a c) -> p a c", a=2), after=(tok,))
        beside(FILL_G[3])
        stt_ = [None] + [S(256).rearrange("p (m v) -> p m v", v=P) for _ in range(3)]
        for c in range(NCH - 1):
            a, par = c // 2, c % 2
            rows = slice(64 * par, 64 * par + 64)
            b = 2 + c
            for h in range(4):
                tok = mm(psum[b][64 * (h % 2):64 * (h % 2) + 64, (h // 2) * P:(h // 2 + 1) * P],
                         kt_[rows, a, 64 * h:64 * h + 64], GV[rows, a, h * P:(h + 1) * P], True, True,
                         after=(V.now(),), signal=h == 3)
            for m in range(2):
                src = psum[b][:, m * P:(m + 1) * P]
                if c == 0:
                    V("copy", stt_[1][:, m, :], src, after=(tok,))
                else:
                    end = (c + 1) * CH - 1
                    V("stt", stt_[c + 1][:, m, :], stt_[c][:, m, :], eb[:, m, end:end + 1], src, MUL, ADD,
                      after=(tok,))
        beside(FILL_G[4])
        beside.finish()
        t = V.now()
        for par in range(2):
            rows = slice(64 * par, 64 * par + 64)
            for m in range(2):
                h = 2 * m + par
                for a in range(2):
                    at0 = m * T + a * P
                    mm(psum[6 + par][:, at0:at0 + P], GV[:, a, h * P:(h + 1) * P], sc[:, m, par, a, :],
                       True, False, after=(t,) + tuple(free[6 + par]), loose=True)
                    for c in (2 * a, 2 * a + 1):
                        if c:
                            tok = mm(psum[6 + par][:, at0 + (c % 2) * CH:at0 + (c % 2 + 1) * CH],
                                     stt_[c][rows, m, :], qf[rows, m, c * CH:(c + 1) * CH], False, True,
                                     loose=True, signal=c == 3)
        yg = Y[:, 0:4, :]
        for par in range(2):
            V("copy", yg[:, par:4:2, :], psum[6 + par][:, :].rearrange("p (k t) -> p k t", t=T), after=(tok,))
        join()
        S.at = mark
        qn, sn = t4(S(4 * T)), t4(S(4 * T))
        head_rms_gate(yg, qn, sn, gr, lambda m: p2("gla_g", m))
        cos_b = rope[:, 0:T].rearrange("p (o t) -> p o t", o=1).to_broadcast([P, 4, T])
        sin_b = rope[:, T:2 * T].rearrange("p (o t) -> p o t", o=1).to_broadcast([P, 2, T])
        for n, src in enumerate((rq, rk)):
            for m in range(4):
                b = 4 + 2 * n + m // 2
                tok = mm(psum[b][:, (m % 2) * T:(m % 2 + 1) * T], c_("swap64"), src[:, m, :], True, True,
                         signal=True)
            V("tt", src, src, cos_b, MUL, after=(tok,))
            for bb in range(2):
                V("tt", sn[:, 2 * bb:2 * bb + 2, :],
                  psum[4 + 2 * n + bb][:, :].rearrange("p (k t) -> p k t", t=T), sin_b, MUL)
            V("tt", src, src, sn, ADD)
        join()
        S.at = mark
        sc2 = S(1024).rearrange("p (m a c) -> p m a c", m=4, a=2)
        kd, qd = t4(S(4 * T)), t4(S(4 * T))
        kdt = S(1024).rearrange("p (a m c) -> p a m c", a=2, m=4)
        st2 = [None] + [S(512).rearrange("p (m v) -> p m v", v=P) for _ in range(3)]
        for m in range(4):
            tab = lambda name: c_(name)[:, m * CH:(m + 1) * CH].rearrange("p (o s) -> p o s", o=1)\
                .to_broadcast([P, NCH, CH])
            V("tt", kd[:, m, :].rearrange("p (c s) -> p c s", s=CH),
              rk[:, m, :].rearrange("p (c s) -> p c s", s=CH), tab("ret_k"), MUL)
            V("tt", qd[:, m, :].rearrange("p (c s) -> p c s", s=CH),
              rq[:, m, :].rearrange("p (c s) -> p c s", s=CH), tab("ret_q"), MUL)
        for bk in range(2):
            for j in range(4):
                m, a = 2 * bk + j // 2, j % 2
                cs = slice(a * P, (a + 1) * P)
                tok = mm(psum[bk][:, j * P:(j + 1) * P], rk[:, m, cs], rq[:, m, cs], True, True, signal=j == 3)
            for mm_ in range(2):
                m = 2 * bk + mm_
                intra = c_("ret_intra")[:, m * P:(m + 1) * P].rearrange("p (o c) -> p o c", o=1)\
                    .to_broadcast([P, 2, P])
                V("tt", sc2[:, m, :, :], ps4(bk)[:, 2 * mm_:2 * mm_ + 2, :], intra, MUL, after=(tok,))
        V("ts", sc2.rearrange("p m a c -> p (m a c)"), sc2.rearrange("p m a c -> p (m a c)"), 128 ** -0.5, None, MUL)
        for a in range(2):
            for m in range(4):
                tok = PE("tr", psum[2 + a][:, m * P:(m + 1) * P], kd[:, m, a * P:(a + 1) * P], c_("ident"),
                         after=(V.now(),), signal=m == 3)
            copy_out(kdt[:, a, :, :], ps4(2 + a), (tok,))
        t = (V.now(), A.now())
        for c in range(NCH - 1):
            a, par = c // 2, c % 2
            rows = slice(64 * par, 64 * par + 64)
            b = 4 + c
            for m in range(4):
                tok = mm(psum[b][:, m * P:(m + 1) * P], kdt[rows, a, m, :], RV[rows, a, m * P:(m + 1) * P],
                         True, True, after=t, signal=m == 3)
            for m in range(4):
                src = psum[b][:, m * P:(m + 1) * P]
                if c == 0:
                    V("copy", st2[1][:, m, :], src, after=(tok,))
                else:
                    V("stt", st2[c + 1][:, m, :], st2[c][:, m, :], c_("ret_chunk")[:, m:m + 1], src, MUL, ADD,
                      after=(tok,))
        t = V.now()
        for m in range(4):
            bank = psum[m // 2]
            for a in range(2):
                at0 = (m % 2) * T + a * P
                mm(bank[:, at0:at0 + P], RV[:, a, m * P:(m + 1) * P], sc2[:, m, a, :], True, False,
                   after=(t,), loose=True)
                for c in (2 * a, 2 * a + 1):
                    if c:
                        tok = mm(bank[:, at0 + (c % 2) * CH:at0 + (c % 2 + 1) * CH], st2[c][:, m, :],
                                 qd[:, m, c * CH:(c + 1) * CH], False, True, loose=True, signal=c == 3)
        yr = Y[:, 4:8, :]
        for b in range(2):
            V("copy", yr[:, 2 * b:2 * b + 2, :], psum[b][:, :].rearrange("p (k t) -> p k t", t=T), after=(tok,))
        t = V.now()
        for m in range(4):
            tok = mm(psum[2 + m // 2][:, (m % 2) * T:(m % 2 + 1) * T], c_("mean128"), yr[:, m, :], True, True,
                     after=(t,), signal=True)
        for b in range(2):
            V("tt", yr[:, 2 * b:2 * b + 2, :], yr[:, 2 * b:2 * b + 2, :],
              psum[2 + b][:, :].rearrange("p (k t) -> p k t", t=T), SUB, after=(tok,))
        t = A("act", qd, yr, Square, after=(V.now(),))
        sig = A("act", kd, rg, Sigmoid)
        for m in range(4):
            tok = mm(psum[4 + m // 2][:, (m % 2) * T:(m % 2 + 1) * T], c_("mean128"), qd[:, m, :], True, True,
                     after=(t,), signal=True)
        for b in range(2):
            V("ts", qd[:, 2 * b:2 * b + 2, :].rearrange("p k t -> p (k t)"), psum[4 + b][:, :], 1e-6, None, ADD,
              after=(tok,))
        t = A("act", qd, qd, Sqrt, after=(V.now(),))
        V("tt", kd, kd, rg, MUL, after=(sig,))
        V("recip", qd, qd, after=(t,))
        V("tt", yr, yr, qd, MUL)
        for m in range(4):
            V("ts", yr[:, m, :], yr[:, m, :], p2("ret_g", m), p2("ret_b", m), MUL, ADD)
        V("tt", yr, yr, kd, MUL)
        join()

    def route(gates):
        rw = router[:, :].rearrange("p (k e) -> p k e", e=EXPERTS)
        sm = small
        lg, m8, idx, oh0, oh1, gt = (sm[:, 256 + 8 * n:264 + 8 * n] for n in range(6))
        idf, p0, p1_ = sm[:, 304:312], sm[:, 312:313], sm[:, 313:314]
        lane = sm[:, 320:328]
        gT = sm[0:8, 0:T]
        for e in range(EXPERTS):
            V("memset", lane[:, e:e + 1], float(e))
        for a in range(2):
            for k in range(KT):
                tok = mm_u(psum[0][:, a * 8:a * 8 + 8], k, rw[:, k, :], slice(a * P, (a + 1) * P), k == 0,
                           k == KT - 1, k == KT - 1, True)
            V("copy", lg, psum[0][:, a * 8:a * 8 + 8], after=(tok,))
            V("max8", m8, lg)
            V("maxidx", idx.bitcast(u32), m8, lg)
            V("copy", idf, idx.bitcast(u32))
            V("ts", oh0, lane, idf[:, 0:1], None, ALU.is_equal)
            V("ts", oh1, lane, idf[:, 1:2], None, ALU.is_equal)
            t = V("tt", p1_, m8[:, 1:2], m8[:, 0:1], SUB)
            t = A("act", p1_, p1_, Exp, after=(t,))
            V("ts", p0, p1_, 1.0, None, ADD, after=(t,))
            V("recip", p0, p0)
            V("tt", p1_, p1_, p0, MUL)
            V("ts", gt, oh0, p0, None, MUL)
            t = V("stt", gt, oh1, p1_, gt, MUL, ADD)
            tok = PE("tr", psum[1][0:8, a * P:(a + 1) * P], gt, c_("ident"), after=(t,))
            V("copy", gT[:, a * P:(a + 1) * P], psum[1][0:8, a * P:(a + 1) * P], after=(tok,))
        t = V.now()
        for e in range(EXPERTS):
            sel = c_("ident")[0:8, e:e + 1].to_broadcast([8, P])
            tok = mm(psum[2 + e // 2][:, (e % 2) * T:(e % 2 + 1) * T], sel, gT, True, True, after=(t,), signal=True)
        for b in range(4):
            copy_out(gates[:, 2 * b * T:(2 * b + 2) * T], psum[2 + b][:, :], (tok,))
        join()

    layer_stream = [None]

    def run(u0, n, dst, stream=None, banks=(1, 2, 3, 4, 5, 6, 7)):
        for j in range(0, n, 2):
            b = banks[(j // 2) % len(banks)]
            PE.wait(*free[b])
            k = min(2, n - j)
            for h in range(k):
                tok = project(stream or layer_stream[0], u0 + j + h, b, h)
            free[b] = (copy_out(dst[:, j:j + k, :].rearrange("p k t -> p (k t)"), psum[b][:, 0:k * T],
                                (tok,)),)

    def run_tokens(u0, n, dst, stream=None):
        for j in range(0, n, 2):
            b = 1 + j // 2
            PE.wait(*free[b])
            tok = project_tokens(stream or layer_stream[0], u0 + j, b)
            free[b] = (copy_out(dst[:, :, j * P:(j + 2) * P],
                                psum[b][:, :].rearrange("p (a c) -> p a c", a=2), (tok,)),)

    weight_stream()

    nc.scalar.dma_start(cond[:, :], a_cond).then_inc(s_in, 16)
    nc.scalar.dma_start(X, a_x.rearrange("k p t -> p k t")).then_inc(s_in, 16)
    for dst, src in ((const[:, :], a_const), (pos.bitcast(i32), a_pos), (par2[:, :], a_par2[0]),
                     (norms[:, :], a_norms[:, 0:KT]), (final2[:, :], a_norms[:, KT:2 * KT]),
                     (router[:, :], a_router)):
        nc.scalar.dma_start(dst, src).then_inc(s_const, 16)
    V("memset", ones[:, :], 1.0)
    for q in work:
        q.engine.wait_ge(s_in, 32)
    t = A("act", small[:, 0:8], cond[:, :], Sigmoid)
    V("tt", cond[:, :], cond[:, :], small[:, 0:8], MUL, after=(t,))
    restart()

    with nc.Fori(0, LAYERS, engines=tuple(q.engine.engine for q in work)) as layer:
        st = Stream(0, 14, layer)
        nc.scalar.dma_start(par1[:, :], a_par1[bass.ds(layer, 1), :, :].rearrange("o p n -> p (o n)"))\
            .then_inc(s_par, 16)
        for q in work:
            q.engine.wait_ge(s_par, layer * 16 + 16)
        t4 = lambda ap: ap.rearrange("p (k t) -> p k t", t=T)
        layer_stream[0] = st
        rms(X, 1e-6, lambda k: p1("norm_mix", k), meanwhile=lambda: split(st, AHEAD - 1))
        PA = t4(arena[:, 0:14 * T])
        run(0, 14, PA)
        for q in work:
            q.engine.wait_ge(s_const, 6 * 16)
        join()
        beside = Modulation(st, 14)
        branch_a(PA, st, beside)
        beside.finish()
        V("copy", raw_mod[:, bass.ds(layer * MOD_UNITS, MOD_UNITS)], mod, after=(beside.fetched,))
        join()
        S = Space()
        st.split_to, st.end = MOD_UNITS + 15, MOD_UNITS + 84
        gat = t4(arena[:, split_at - 24 * T:split_at])
        gates_beside = Beside(st, (5, 7))
        PC = t4(arena[:, BRANCH_COLS:BRANCH_COLS + 9 * T])
        assert BRANCH_COLS + 9 * T <= split_at - (24 - GATES_LATE) * T
        gates_beside.add(MOD_UNITS + 31, 9, PC)
        gates_beside.add(MOD_UNITS + 40, 24 - GATES_LATE, gat[:, GATES_LATE:24, :])
        gates_beside.add(MOD_UNITS + 64 - GATES_LATE, GATES_LATE, gat[:, 0:GATES_LATE, :])
        PB = t4(S(12 * T))
        VB = S(1024).rearrange("p (a c) -> p a c", a=2)
        run(MOD_UNITS + 15, 9, PB[:, 0:9, :])
        run_tokens(MOD_UNITS + 24, 4, VB)
        run(MOD_UNITS + 28, 3, PB[:, 9:12, :])
        join()
        branch_b(PB, VB, S, gates_beside)
        S = Space()
        VC = S(256).rearrange("p (a c) -> p a c", a=2)
        WI = small[:, 72:80]
        for n, tile in ((0, 7), (1, 8)):
            for a in range(2):
                tok = PE("tr", psum[6][:, (2 * n + a) * P:(2 * n + a + 1) * P], PC[:, tile, a * P:(a + 1) * P],
                         c_("ident"), after=tuple(free[4]) + tuple(free[5]) + tuple(free[6]))
        V("copy", WI.rearrange("p (a h) -> p a h", a=2),
          psum[6][:, 0:T].rearrange("p (a c) -> p a c", a=2)[:, :, 64:68], after=(tok,))
        V("copy", VC, psum[6][:, T:2 * T].rearrange("p (a c) -> p a c", a=2))
        join()
        branch_c(PC[:, 0:8, :], VC, WI, S, gates_beside,
                 lambda: split(st, MOD_UNITS + 64 + SPLIT - 1))
        y_t, opened = [], []
        for n in range(3):
            ks = slice(4 * n, 4 * n + 4)
            t = A("act", YH[:, ks, :], Y[:, ks, :], Copy)
            y_t.append(V("tt", YL[:, ks, :], Y[:, ks, :], YH[:, ks, :].bitcast(f32), SUB, after=(t,)))
        for n in range(3):
            opened.append(A("act", gat[:, 8 * n:8 * n + 8, :], gat[:, 8 * n:8 * n + 8, :], Sigmoid))
        merged = Y[:, 0:8, :]
        prod = Y[:, 8:12, :]
        for n in range(3):
            PE.wait(y_t[n])
            for m in range(4):
                u = MOD_UNITS + 64 + 4 * n + m
                split(st, u + AHEAD)
                PE.wait(parts_ready[id(st), u])
                for dt in range(KT):
                    if m == 0:
                        PE.wait(*free[dt])
                    tok = mm3(psum[dt][:, 0:T], parts(st, u, slice(dt * P, (dt + 1) * P)),
                              (YH[:, 4 * n + m, :], YL[:, 4 * n + m, :]), m == 0, m == 3,
                              signal=m == 3 or dt == KT - 1)
                    if m < 3:
                        continue
                    gk_ = gat[:, n * KT + dt, :]
                    if n == 0:
                        t = V("tt", merged[:, dt, :], psum[dt][:, 0:T], gk_, MUL, after=(tok, opened[n], y_t[2]))
                    else:
                        t = V("tt", prod[:, dt % 4, :], psum[dt][:, 0:T], gk_, MUL, after=(tok, opened[n]))
                        V("tt", merged[:, dt, :], merged[:, dt, :], prod[:, dt % 4, :], ADD)
                    free[dt] = (t,)
                read_by[u % SPLIT] = tok
        split_u(merged, (V.now(),))
        PE.wait(V.now())
        for dt in range(KT):
            PE.wait(*free[dt])
            tok = project(st, MOD_UNITS + 76 + dt, dt, 0)
            V("tt", X[:, dt, :], X[:, dt, :], psum[dt][:, 0:T], ADD, after=(tok,))
        join()
        feed_forward(MIX1_GROUPS + ADA_GROUPS, FF_GROUPS, layer, True, 0, 0, 0, None, lambda dt: 1.0,
                     lambda cuts: rms(X, 1e-6, lambda k: p1("norm_ffn", k), meanwhile=cuts))
        restart()

    def rotary_tables():
        ang, turns, red = (arena[:, (20 + n) * T:(21 + n) * T] for n in range(3))
        V("copy", ang, pos.bitcast(i32))
        V("ts", ang, ang, c_("inv_freq"), None, MUL)
        V("ts", turns, ang, float(1 / (2 * np.pi)), ROUND, MUL, ADD)
        V("ts", turns, turns, ROUND, None, SUB)
        for part in TWO_PI:
            V("stt", ang, turns, -part, ang, MUL, ADD)
        t = V("ts", ang, ang, -3.1415925, 3.1415925, MAX, ALU.min)
        A("act", rope[:, T:2 * T], ang, Sin, after=(t,))
        t = A("act", red, ang, Sin, scale=0.5)
        V("ts", rope[:, T:2 * T], rope[:, T:2 * T], c_("sin_sign"), None, MUL, after=(t,))
        V("tt", red, red, red, MUL)
        V("ts", rope[:, 0:T], red, -2.0, 1.0, MUL, ADD)
    rms(X, 1e-6, lambda k: norms[:, k:k + 1], out=X, meanwhile=rotary_tables)

    at_group = LAYERS * LAYER1_GROUPS
    ff_base = 0
    for layer2 in range(LAYERS):
        if layer2:
            for q in work:
                q.engine.wait_ge(s_par, 16 * (LAYERS + layer2))
        modulation(raw_mod[:, layer2 * MOD_UNITS:(layer2 + 1) * MOD_UNITS])
        st = Stream(at_group, 36)
        rms(X, 1e-6, lambda k: mod[:, 8 + k:9 + k], lambda k: mod[:, k:k + 1],
            meanwhile=lambda: split(st, AHEAD - 1))

        def units(P2, GV, RV):
            run(0, 4, P2[:, 0:4, :], stream=st)
            run_tokens(4, 4, GV, stream=st)
            run(8, 4, P2[:, 4:8, :], stream=st)
            join()
            beside = Beside(st, (7, 0))
            beside.add(12, 8, P2[:, 8:16, :])
            beside.add_tokens(20, 4, RV)
            beside.add(24, 4, P2[:, 16:20, :])
            return beside
        linear_attention(units, Space(), rope)
        split_u(Y[:, 0:8, :], ())
        join()
        for dt in range(KT):
            tok = project(st, 28 + dt, dt, 0)
            V("stt", X[:, dt, :], psum[dt][:, 0:T], mod[:, 16 + dt:17 + dt], X[:, dt, :], MUL, ADD, after=(tok,))
        join()
        at_group += MIX2_GROUPS
        norm2 = lambda cuts: rms(X, 1e-6, lambda k: mod[:, 32 + k:33 + k], lambda k: mod[:, 24 + k:25 + k],
                                 meanwhile=cuts)
        gates, n_groups = None, FF_GROUPS
        if layer2 + 1 < LAYERS:
            nc.scalar.dma_start(par2[:, :], a_par2[layer2 + 1]).then_inc(s_par, 16)
        if layer2 == 1:
            norm2(lambda: None)
            norm2 = lambda cuts: cuts()
            join()
            gates, n_groups = arena[:, 0:EXPERTS * T], MOE_GROUPS
            route(gates)
        feed_forward(at_group, n_groups, None, False, FF_GROUPS * layer2, 3 * FF_GROUPS * layer2,
                     (LAYERS + layer2) * FF_GROUPS, gates, lambda dt: mod[:, 40 + dt:41 + dt], norm2)
        at_group += n_groups
    assert at_group == ALL_GROUPS
    V("copy", norms[:, :], final2[:, :])
    rms(X, 1e-6, lambda k: norms[:, k:k + 1], out=X)
    nc.scalar.wait_ge(*V.now())
    nc.scalar.dma_start(a_out.rearrange("k p t -> p k t"), X).then_inc(s_out, 16)
    nc.scalar.wait_ge(s_out, 16)
    es.close()


TWO_PI = (6.28125, 0.0019340515136718750, float(2 * np.pi - 6.28125 - 0.0019340515136718750))
ROUND = float(1.5 * 2 ** 23)


def columns(a):
    k, n = a.shape
    return a.reshape(k // P, P, n // P, P).transpose(2, 1, 0, 3).reshape(n // P, P, k)


def per_channel(a):
    return np.asarray(a).reshape(-1, P).T


def weight_groups(inp):
    out = np.zeros((ALL_GROUPS, P, SLOT), np.float32)
    at = 0

    def put(units):
        nonlocal at
        n = len(units) // GROUP
        out[at:at + n, :, :GROUP * UNIT] = np.stack(units).reshape(n, GROUP, P, UNIT).transpose(0, 2, 1, 3)\
            .reshape(n, P, GROUP * UNIT)
        at += n
    A_END, B_END = 1792, 1792 + 2048
    for l in range(LAYERS):
        w = inp["w_in"][l]
        b, c = w[:, A_END:B_END], w[:, B_END:B_END + 1092]
        low = np.concatenate([np.concatenate([inp["a_w_up"][l], inp["a_a_up"][l]], 0), inp["a_g_up"][l]], 1)
        index = np.concatenate([c[:, 1024:1092], np.zeros((D, 60), np.float32)], 1)
        mod = inp["ada_w_2"][l].reshape(KT, P, MOD_UNITS // KT, UNIT).transpose(2, 0, 1, 3).reshape(MOD_UNITS, P, UNIT)
        gates = columns(w[:, B_END + 1092:])
        qfg = np.concatenate([columns(b[:, 0:1024]), columns(b[:, 1536:2048])])
        units = [*columns(w[:, :A_END]), *mod[:MOD_FIRST], low, *mod[MOD_FIRST:], *qfg[:9], *columns(b[:, 1024:1536]), *qfg[9:],
                 *columns(c[:, 0:640]), *columns(c[:, 768:1024]), *columns(index),
                 *columns(c[:, 640:768]), *gates[GATES_LATE:], *gates[:GATES_LATE],
                 *inp["w_branch"][l].reshape(12, P, D), *columns(inp["w_o"][l])]
        put(units)
        gate, val = columns(inp["w_up"][l][:, :FF]), columns(inp["w_up"][l][:, FF:])
        down = inp["w_down"][l].reshape(FF_GROUPS, P, D)
        taps = np.concatenate([inp["conv_w"][l], inp["conv_b"][l][None]], 0).reshape(4, 2, FF_GROUPS, P)
        out[at:at + FF_GROUPS, :, GROUP * UNIT:] = taps.transpose(2, 3, 1, 0).reshape(FF_GROUPS, P, EXTRA)
        put([u for g in range(FF_GROUPS) for u in (gate[g], val[g], down[g])])
    for l in range(LAYERS):
        w = inp["w_in_2"][l]
        cut = lambda s, n: [*columns(w[:, s:s + n])]
        put([*cut(0, 512), *cut(512, 512), *cut(1024, 512), *cut(1552, 1024), *cut(2576, 512), *cut(3088, 512),
             *columns(inp["w_out_2"][l])])
        if l == 0:
            w1, w3 = columns(inp["ffn_w1_2"][0]), columns(inp["ffn_w3_2"][0])
            w2 = inp["ffn_w2_2"][0].reshape(FF_GROUPS, P, D)
        else:
            w1, w3 = (np.concatenate([columns(inp[n][0, e]) for e in range(EXPERTS)]) for n in ("moe_w1_2", "moe_w3_2"))
            w2 = inp["moe_w2_2"][0].reshape(MOE_GROUPS, P, D)
        put([u for g in range(len(w1)) for u in (w1[g], w3[g], w2[g])])
    assert at == ALL_GROUPS
    return out


def laid_out(inp):
    par1 = np.zeros((LAYERS, P, PAR1_COLS), np.float32)
    par2 = np.zeros((LAYERS, P, PAR2_COLS), np.float32)
    for l in range(LAYERS):
        put = lambda name, a: par1[l].__setitem__((slice(None), PAR1[name]), a)
        for name, key in (("norm_mix", "norm_mix_g"), ("mu", "a_mu"), ("w0", "a_w0"), ("a0", "a_a0"),
                          ("k_k", "a_k_k"), ("k_a", "a_k_a"), ("gn_g", "a_gn_g"), ("gn_b", "a_gn_b"),
                          ("b_gn_g", "b_gn_g"), ("norm_ffn", "norm_ffn_g")):
            put(name, per_channel(inp[key][l]))
        put("r_k", per_channel(inp["a_r_k"][l].reshape(-1)))
        put("lb_logits", np.concatenate([per_channel(inp["b_lb_logits"][j]) for j in range(LAYERS)], 1))
        put("lb_flag", float(l))
        put = lambda name, a: par2[l].__setitem__((slice(None), PAR2[name]), a)
        for name, key in (("norm_mix", "norm_mix_g_2"), ("norm_ffn", "norm_ffn_g_2"), ("ada_b", "ada_b_2"),
                          ("b_alpha", "gla_b_alpha_2"), ("gla_g", "gla_norm_g_2"), ("ret_g", "ret_gn_g_2"),
                          ("ret_b", "ret_gn_b_2")):
            put(name, per_channel(inp[key][l]))
        put("w_ga", inp["w_in_2"][l][:, 1536:1552].reshape(KT, P, 16).transpose(1, 0, 2).reshape(P, 128))
        par2[l, 0:16, PAR2["w_alpha"]] = inp["gla_w_alpha_2"][l]
    return {
        "x": np.ascontiguousarray(inp["x"][0].T.reshape(KT, P, T)),
        "pos": np.ascontiguousarray(np.broadcast_to(inp["positions_2"], (P, T))),
        "cond": np.ascontiguousarray(per_channel(inp["c_2"][0])),
        "const": constants(),
        "par1": par1, "par2": par2,
        "router": np.ascontiguousarray(
            inp["router_w_2"][0].reshape(KT, P, EXPERTS).transpose(1, 0, 2).reshape(P, KT * EXPERTS)),
        "norms": np.ascontiguousarray(
            np.concatenate([per_channel(inp["norm_final_g"]), per_channel(inp["final_g_2"])], 1)),
        "weights": weight_groups(inp),
    }


def kernel(**inputs):
    import concourse.bacc as bacc
    from concourse import mybir
    from concourse.bass_utils import run_bass_kernel_spmd

    arrays = laid_out({k: np.asarray(v) for k, v in inputs.items()})
    nc = bacc.Bacc("TRN2", target_bir_lowering=False, num_devices=1)
    aps = {n: nc.dram_tensor(f"in_{n}", a.shape, mybir.dt.from_np(a.dtype), kind="ExternalInput").ap()
           for n, a in arrays.items()}
    out = nc.dram_tensor("out", (KT, P, T), mybir.dt.float32, kind="ExternalOutput").ap()
    build(nc, aps["x"], aps["pos"], aps["cond"], aps["const"], aps["par1"], aps["par2"], aps["router"],
          aps["norms"], aps["weights"], out)
    r = run_bass_kernel_spmd(nc, [{f"in_{n}": a for n, a in arrays.items()}], core_ids=[0])
    got = r.results[0]["out"]
    return np.ascontiguousarray(got.reshape(D, T).T[None])
```
